# Optimizing a Trainium2 kernel written in Bass

```python
import math
import jax, jax.numpy as jnp
from jax import lax
import numpy as np

D_MODEL = 1024
BATCH = 1
SEQ = 1024
DEPTH = 1

CHUNK = 64
N_MEM = 256
RMS_EPS = 1e-6
NEG_INF = -1e30
D_FF = 2816
ML_HEADS = 4
ML_DV = D_MODEL // 8
ML_DQK = ML_DV // 2
ML_V_W = ML_HEADS * ML_DV
ML_QK_W = ML_HEADS * ML_DQK
CONV_W = 4
SW_QHEADS = 8
SW_KVHEADS = 2
SW_DH = 64
SW_Q_W = SW_QHEADS * SW_DH
SW_KV_W = SW_KVHEADS * SW_DH
WINDOW = 128
WIN_CHUNKS = WINDOW // CHUNK
ROPE_THETA = 500000.0
ROT_DIM = SW_DH // 4
MX_HEADS = 4
MX_DH = 128
MX_W = MX_HEADS * MX_DH
N_BRANCH = 3

IN_SIZES = (ML_QK_W, ML_QK_W, ML_V_W, ML_HEADS, ML_HEADS, ML_V_W,
            SW_Q_W, SW_KV_W, SW_KV_W, MX_W, N_BRANCH * D_MODEL)
IN_TOTAL = int(sum(IN_SIZES))
IN_SPLITS = [int(s) for s in np.cumsum(IN_SIZES)[:-1]]

kernel_name = "hybrid_mlstm_swa_memattn_macaron"

def rms_norm(x, g):
    xf = x.astype(jnp.float32)
    y = xf * lax.rsqrt(jnp.mean(xf * xf, axis=-1, keepdims=True) + RMS_EPS)
    return (y * g.astype(jnp.float32)).astype(x.dtype)

def swiglu(h, w_in, w_out):
    a, b = jnp.split(h @ w_in, 2, axis=-1)
    return (jax.nn.silu(a) * b) @ w_out

def causal_conv(x, w):
    k = w.shape[0]
    return lax.conv_general_dilated(
        x, w[:, None, :].astype(x.dtype), window_strides=(1,), padding=[(k - 1, 0)],
        dimension_numbers=("NWC", "WIO", "NWC"), feature_group_count=x.shape[-1])

def partial_rope(x, pos):
    half = ROT_DIM // 2
    inv = ROPE_THETA ** (-jnp.arange(half, dtype=jnp.float32) * (2.0 / ROT_DIM))
    ang = pos.astype(jnp.float32)[..., None] * inv
    cos = jnp.cos(ang)[:, :, None, :]
    sin = jnp.sin(ang)[:, :, None, :]
    xr = x[..., :ROT_DIM].astype(jnp.float32)
    x1, x2 = xr[..., :half], xr[..., half:]
    rot = jnp.concatenate([x1 * cos - x2 * sin, x2 * cos + x1 * sin], axis=-1)
    return jnp.concatenate([rot.astype(x.dtype), x[..., ROT_DIM:]], axis=-1)

def mlstm(q, k, v, i_pre, f_pre):
    b_sz, s_len, n_h = q.shape[0], q.shape[1], q.shape[2]
    nc = s_len // CHUNK
    f32 = jnp.float32

    def to_chunks(t):
        t = t.astype(f32).reshape((b_sz, nc, CHUNK) + t.shape[2:])
        return jnp.moveaxis(t, [1, 3], [0, 2])

    qc = to_chunks(q)
    kc = to_chunks(k) * (ML_DQK ** -0.5)
    vc = to_chunks(v)
    ic = to_chunks(i_pre)
    lfc = to_chunks(jax.nn.log_sigmoid(f_pre.astype(f32)))
    causal = jnp.tril(jnp.ones((CHUNK, CHUNK), dtype=bool))

    def body(carry, xs):
        c_st, n_st, m_st = carry
        qq, kk, vv, ig, lf = xs
        bcum = jnp.cumsum(lf, axis=-1)
        dmat = bcum[..., :, None] - bcum[..., None, :] + ig[..., None, :]
        dmat = jnp.where(causal, dmat, NEG_INF)
        g = bcum + m_st[..., None]
        m_t = jnp.maximum(dmat.max(axis=-1), g)
        sc = jnp.einsum("bhtd,bhsd->bhts", qq, kk) * jnp.exp(dmat - m_t[..., None])
        inter = jnp.exp(g - m_t)
        num = (jnp.einsum("bhts,bhse->bhte", sc, vv)
               + inter[..., None] * jnp.einsum("bhtd,bhde->bhte", qq, c_st))
        den = sc.sum(axis=-1) + inter * jnp.einsum("bhtd,bhd->bht", qq, n_st)
        h = num / jnp.maximum(jnp.abs(den), jnp.exp(-m_t))[..., None]
        b_last = bcum[..., -1]
        a = b_last[..., None] - bcum + ig
        m_new = jnp.maximum(b_last + m_st, a.max(axis=-1))
        w = jnp.exp(a - m_new[..., None])
        decay = jnp.exp(b_last + m_st - m_new)
        c_new = decay[..., None, None] * c_st + jnp.einsum("bhs,bhsd,bhse->bhde", w, kk, vv)
        n_new = decay[..., None] * n_st + jnp.einsum("bhs,bhsd->bhd", w, kk)
        return (c_new, n_new, m_new), h

    init = (jnp.zeros((b_sz, n_h, ML_DQK, ML_DV), f32),
            jnp.zeros((b_sz, n_h, ML_DQK), f32),
            jnp.zeros((b_sz, n_h), f32))
    _, hs = lax.scan(body, init, (qc, kc, vc, ic, lfc))
    hs = jnp.moveaxis(hs, [0, 2], [1, 3])
    return hs.reshape(b_sz, s_len, n_h, ML_DV).astype(v.dtype)

def swa_sinks(q, k, v, sinks):
    b_sz, s_len = q.shape[0], q.shape[1]
    nc = s_len // CHUNK
    grp = SW_QHEADS // SW_KVHEADS
    pad = WIN_CHUNKS - 1
    qc = q.reshape(b_sz, nc, CHUNK, SW_KVHEADS, grp, SW_DH)
    kc = k.reshape(b_sz, nc, CHUNK, SW_KVHEADS, SW_DH)
    vc = v.reshape(b_sz, nc, CHUNK, SW_KVHEADS, SW_DH)
    padw = ((0, 0), (pad, 0), (0, 0), (0, 0), (0, 0))
    kp, vp = jnp.pad(kc, padw), jnp.pad(vc, padw)
    kw = jnp.concatenate([kp[:, j:j + nc] for j in range(WIN_CHUNKS)], axis=2)
    vw = jnp.concatenate([vp[:, j:j + nc] for j in range(WIN_CHUNKS)], axis=2)
    valid = (jnp.arange(nc)[:, None] - pad + jnp.arange(WIN_CHUNKS)[None, :]) >= 0
    valid = jnp.repeat(valid, CHUNK, axis=1)
    s = jnp.einsum("bcqkgd,bcskd->bckgqs", qc, kw).astype(jnp.float32)
    s = jnp.where(valid[None, :, None, None, None, :], s, NEG_INF)
    sink = sinks.astype(jnp.float32).reshape(SW_KVHEADS, grp)[None, None, :, :, None, None]
    m = jnp.maximum(s.max(axis=-1, keepdims=True), sink)
    p = jnp.exp(s - m)
    p = p / (p.sum(axis=-1, keepdims=True) + jnp.exp(sink - m))
    o = jnp.einsum("bckgqs,bcskd->bcqkgd", p.astype(v.dtype), vw)
    return o.reshape(b_sz, s_len, SW_Q_W)

def mem_attention(q, k, v):
    s = jnp.einsum("bshd,bmhd->bhsm", q, k).astype(jnp.float32)
    p = jax.nn.softmax(s, axis=-1).astype(v.dtype)
    o = jnp.einsum("bhsm,bmhd->bshd", p, v)
    return o.reshape(q.shape[0], q.shape[1], MX_W)

def setup_inputs(seed: int = 0) -> dict:
    key = jax.random.key(seed)
    ks = iter(jax.random.split(key, 40))
    f32 = jnp.float32

    def dense(shape, fan_in):
        return jax.random.normal(next(ks), (DEPTH,) + shape, f32) * (fan_in ** -0.5)

    def gain(n):
        return 1.0 + 0.02 * jax.random.normal(next(ks), (DEPTH, n), f32)

    def small(n, scale):
        return scale * jax.random.normal(next(ks), (DEPTH, n), f32)

    x = jax.random.normal(next(ks), (BATCH, SEQ, D_MODEL), f32)
    mem = jax.random.normal(next(ks), (BATCH, N_MEM, D_MODEL), f32)
    offset = jax.random.randint(next(ks), (BATCH, 1), 0, 64, dtype=jnp.int32) * CHUNK
    positions = (offset + jnp.arange(SEQ, dtype=jnp.int32)[None, :]).astype(jnp.int32)
    ml_b_f = (jnp.linspace(3.0, 6.0, ML_HEADS, dtype=f32)[None, :]
              + 0.1 * jax.random.normal(next(ks), (DEPTH, ML_HEADS), f32))
    return {
        "x": x,
        "mem": mem,
        "positions": positions,
        "ffn1_norm": gain(D_MODEL),
        "ffn1_w_in": dense((D_MODEL, 2 * D_FF), D_MODEL),
        "ffn1_w_out": dense((D_FF, D_MODEL), D_FF),
        "mix_norm": gain(D_MODEL),
        "mem_norm": gain(D_MODEL),
        "w_in": dense((D_MODEL, IN_TOTAL), D_MODEL),
        "b_gate": small(N_BRANCH * D_MODEL, 0.02),
        "ml_conv_q": dense((CONV_W, ML_QK_W), CONV_W),
        "ml_conv_k": dense((CONV_W, ML_QK_W), CONV_W),
        "ml_b_i": small(ML_HEADS, 0.1),
        "ml_b_f": ml_b_f,
        "ml_out_norm": gain(ML_V_W),
        "sw_q_norm": gain(SW_DH),
        "sw_k_norm": gain(SW_DH),
        "sw_sinks": small(SW_QHEADS, 0.5),
        "mx_w_kv": dense((D_MODEL, 2 * MX_W), D_MODEL),
        "mx_q_norm": gain(MX_DH),
        "mx_k_norm": gain(MX_DH),
        "w_br_ml": dense((ML_V_W, D_MODEL), ML_V_W),
        "w_br_sw": dense((SW_Q_W, D_MODEL), SW_Q_W),
        "w_br_mx": dense((MX_W, D_MODEL), MX_W),
        "w_out": dense((D_MODEL, D_MODEL), D_MODEL),
        "ffn2_norm": gain(D_MODEL),
        "ffn2_w_in": dense((D_MODEL, 2 * D_FF), D_MODEL),
        "ffn2_w_out": dense((D_FF, D_MODEL), D_FF),
    }

def reference(x, mem, positions, ffn1_norm, ffn1_w_in, ffn1_w_out, mix_norm, mem_norm,
              w_in, b_gate, ml_conv_q, ml_conv_k, ml_b_i, ml_b_f, ml_out_norm,
              sw_q_norm, sw_k_norm, sw_sinks, mx_w_kv, mx_q_norm, mx_k_norm,
              w_br_ml, w_br_sw, w_br_mx, w_out, ffn2_norm, ffn2_w_in, ffn2_w_out):
    b_sz, s_len = x.shape[0], x.shape[1]
    n_mem = mem.shape[1]
    for l in range(DEPTH):
        x = x + 0.5 * swiglu(rms_norm(x, ffn1_norm[l]), ffn1_w_in[l], ffn1_w_out[l])

        h = rms_norm(x, mix_norm[l])
        (m_q, m_k, m_v, m_i, m_f, m_o, s_q, s_k, s_v, c_q, gate_pre) = jnp.split(
            h @ w_in[l], IN_SPLITS, axis=-1)

        m_q = jax.nn.silu(causal_conv(m_q, ml_conv_q[l])).reshape(b_sz, s_len, ML_HEADS, ML_DQK)
        m_k = jax.nn.silu(causal_conv(m_k, ml_conv_k[l])).reshape(b_sz, s_len, ML_HEADS, ML_DQK)
        m_v = m_v.reshape(b_sz, s_len, ML_HEADS, ML_DV)
        h_t = mlstm(m_q, m_k, m_v, m_i + ml_b_i[l], m_f + ml_b_f[l])
        h_t = rms_norm(h_t, ml_out_norm[l].reshape(ML_HEADS, ML_DV)).reshape(b_sz, s_len, ML_V_W)
        y_a = jax.nn.sigmoid(m_o) * h_t

        s_q = rms_norm(s_q.reshape(b_sz, s_len, SW_QHEADS, SW_DH), sw_q_norm[l])
        s_k = rms_norm(s_k.reshape(b_sz, s_len, SW_KVHEADS, SW_DH), sw_k_norm[l])
        s_q = partial_rope(s_q, positions) * (SW_DH ** -0.5)
        s_k = partial_rope(s_k, positions)
        s_v = s_v.reshape(b_sz, s_len, SW_KVHEADS, SW_DH)
        y_b = swa_sinks(s_q, s_k, s_v, sw_sinks[l])

        c_k, c_v = jnp.split(rms_norm(mem, mem_norm[l]) @ mx_w_kv[l], 2, axis=-1)
        c_q = rms_norm(c_q.reshape(b_sz, s_len, MX_HEADS, MX_DH), mx_q_norm[l]) * (MX_DH ** -0.5)
        c_k = rms_norm(c_k.reshape(b_sz, n_mem, MX_HEADS, MX_DH), mx_k_norm[l])
        c_v = c_v.reshape(b_sz, n_mem, MX_HEADS, MX_DH)
        y_c = mem_attention(c_q, c_k, c_v)

        g_a, g_b, g_c = jnp.split(jax.nn.sigmoid(gate_pre + b_gate[l]), N_BRANCH, axis=-1)
        merged = (g_a * (y_a @ w_br_ml[l]) + g_b * (y_b @ w_br_sw[l])
                  + g_c * (y_c @ w_br_mx[l]))
        x = x + merged @ w_out[l]

        x = x + 0.5 * swiglu(rms_norm(x, ffn2_norm[l]), ffn2_w_in[l], ffn2_w_out[l])
    return x


_drawn_inputs = setup_inputs


def setup_inputs(seed=0):
    import zlib

    import numpy as np

    out = dict(_drawn_inputs(seed))
    spreads = {}
    factors = {'ffn1_norm': 6.175,
     'mix_norm': 5.167,
     'mem_norm': 8.0,
     'b_gate': 8.0,
     'ml_b_i': 8.0,
     'ml_out_norm': 8.0,
     'sw_q_norm': 8.0,
     'sw_k_norm': 8.0,
     'sw_sinks': 8.0,
     'mx_q_norm': 8.0,
     'mx_k_norm': 8.0,
     'ffn2_norm': 7.356}
    for name, (base, spread) in spreads.items():
        noise = np.random.default_rng([zlib.crc32(name.encode()), seed]).standard_normal(out[name].shape)
        drawn = base * np.exp(spread * noise) if base else spread * noise
        out[name] = __import__('jax').numpy.asarray(drawn.astype(out[name].dtype))
    for name, factor in factors.items():
        out[name] = (out[name] * factor).astype(out[name].dtype)
    return out
```

```python
import math
from contextlib import ExitStack

import numpy as np

import concourse.bass as bass
from concourse import mybir

F32 = mybir.dt.float32
F32R = mybir.dt.float32r
I32 = mybir.dt.int32
ALU = mybir.AluOpType
ACT = mybir.ActivationFunctionType
AX = mybir.AxisListType

P = 128
D = 1024
KD = D // P
T = 1024
HT = T // 2
FF = 2816
NF = FF // P
NPAIR = NF // 2
NMEM = 256
NG = 24
NT = T // P
MLH = 4
SWH = 8
MXH = 4
EPS = 1e-6
NEG = -1e30
WIN = 192

B_FFN1 = 0
B_MIX1 = B_FFN1 + 6 * NPAIR
N_MIX1 = 18
B_GATE1 = B_MIX1 + N_MIX1
B_MIX2 = B_GATE1 + 16
N_MIX2 = 13
B_GATE2 = B_MIX2 + N_MIX2
B_MERGE = B_GATE2 + 8
B_FFN2 = B_MERGE + 20
NB = B_FFN2 + 6 * NPAIR

COLS = {}
for _n, _w in (("ffn1", KD), ("mix", KD), ("ffn2", KD), ("mem", KD), ("bgate", NG), ("convq", 8),
               ("convk", 8), ("mlnorm", 4), ("swq", 1), ("swk", 1), ("mxq", 1), ("mxk", 1),
               ("sink", SWH), ("bi", 1), ("bf", 1), ("inv", 1), ("eps", 1)):
    COLS[_n] = (sum(w for _, w in COLS.values()), _w)
NCOL = sum(w for _, w in COLS.values())

C_ID, C_ONE, C_BLK, C_PERM, C_MASK = (P * i for i in range(5))
C_BLK2 = 5 * P
NCONST = C_BLK2 + 2

PI2_A = 6.28125
PI2_B = float(np.float32(np.round((2 * np.pi - PI2_A) * 2.0**21) / 2.0**21))
PI2_C = float(np.float32(2 * np.pi - PI2_A - PI2_B))
ROUND = 12582912.0
PI_IN = 3.1415925


def build(nc, xT, memT, pos, wts, cols_d, const_d, sel_d, out):
    with ExitStack() as top:
        sem_names = []

        def sem(name):
            sem_names.append(name)
            return top.enter_context(nc.semaphore(name))

        def era(side):
            st = ExitStack()

            def sb(name, shape, dt=F32):
                return st.enter_context(nc.sbuf_tensor(name, shape, dt, side=side))
            return st, sb

        gate_scr = nc.dram_tensor("gate_scr", (NG, P, T), F32, kind="Internal").ap()
        x_scr = nc.dram_tensor("x_scr", (P, KD, T), F32, kind="Internal").ap()

        base, sb = era("left")
        raw = [sb(f"raw{i}", [P, 1024]) for i in range(2)]
        whi = [sb(f"whi{i}", [P, 1024], F32R) for i in range(2)]
        wlo = [sb(f"wlo{i}", [P, 1024], F32R) for i in range(2)]
        cst = sb("cst", [P, NCONST])
        cols = sb("cols", [P, NCOL])

        def col(name, i=0, p0=0, p1=P):
            c = COLS[name][0] + i
            return cols[p0:p1, c:c + 1]

        ident = cst[:, C_ID:C_ID + P]
        ones = cst[:, C_ONE:C_ONE + P]
        blk64 = cst[:, C_BLK:C_BLK + P]
        perm = cst[:, C_PERM:C_PERM + P]
        mask = cst[:, C_MASK:C_MASK + P]
        blk2 = cst[:, C_BLK2:C_BLK2 + 2]

        eh, sb = era("left")
        h_hi = sb("h_hi", [P, KD, T], F32R)
        h_lo = sb("h_lo", [P, KD, T], F32R)
        em_, sb = era("left")
        mh_hi = sb("mh_hi", [P, KD, NMEM], F32R)
        mh_lo = sb("mh_lo", [P, KD, NMEM], F32R)

        def ffn_buffers(tag, sb):
            return dict(
                u_hi=sb("u_hi" + tag, [P, 2, T], F32R), u_lo=sb("u_lo" + tag, [P, 2, T], F32R),
                sa=sb("sa" + tag, [P, 2, HT]), uf=sb("uf" + tag, [P, 2, 2, HT]),
                sq=sb("sq" + tag, [P, 4, HT]), hf=sb("hf" + tag, [P, 2, HT]), rs=sb("rs" + tag, [P, 2, HT]))

        e1, sb = era("right")
        x1 = sb("x1", [P, KD, T])
        f1 = ffn_buffers("1", sb)
        memx = sb("memx", [P, KD, NMEM])
        e1.close()

        ey, sb = era("right")
        y_c = sb("y_c", [P, 4, T])
        y_b = sb("y_b", [P, 4, T])
        m1, sb = era("right")
        kv_all = sb("kv_all", [P, 2, 64 + T])
        rope_c = sb("rope_c", [P, T])
        rope_s = sb("rope_s", [P, T])
        ck = sb("ck", [P, MXH, NMEM])
        cv = sb("cv", [P, 2, 4 * P])
        rq = sb("rq", [P, NT, 12])
        p_mx = sb("p_mx", [P, MXH, NMEM])
        pt_mx = sb("pt_mx", [P, 2 * MXH, P])
        p_sw = sb("p_sw", [P, SWH, P])
        pt_sw = sb("pt_sw", [P, SWH, P])
        q_mx = sb("q_mx", [P, 4, P])
        q_sw = sb("q_sw", [P, 4, P])
        q_rot = sb("q_rot", [P, 4, P])
        q_tmp = sb("q_tmp", [P, 4, P])
        kv_st = sb("kv_st", [P, 2, WIN])
        v_win = sb("v_win", [P, 2, P])
        gst1 = [sb(f"gst1_{i}", [P, HT]) for i in range(2)]
        gains = sb("gains", [P, 2])
        rq_st = sb("rq_st", [P, 12])
        m_mx, nb_mx, sum_mx, ri_mx = (sb(n, [P, MXH]) for n in ("m_mx", "nb_mx", "sum_mx", "ri_mx"))
        m_sw, nb_sw, sum_sw, ri_sw, es_in, es = (sb(n, [P, SWH]) for n in ("m_sw", "nb_sw", "sum_sw", "ri_sw", "es_in", "es"))
        negrow = sb("negrow", [1, 2 * P])
        pos_i = pt_mx[:, :, :].rearrange("p a b -> p (a b)").bitcast(I32)
        m1.close()
        em_.close()

        m2, sb = era("right")
        y_a = sb("y_a", [P, 4, T])
        m2b, sb = era("right")
        ml_q = sb("ml_q", [P, 2, T])
        ml_k = sb("ml_k", [P, 2, T])
        ml_v = sb("ml_v", [P, 4, T])
        rows = sb("rows", [68, T])
        cw = sb("cw", [36, T])
        m2d, sb = era("right")
        cpad = [sb(f"cpad{i}", [P, 3 + T]) for i in range(2)]
        cacc = sb("cacc", [P, T])
        reset = sb("reset", [4, T])
        mst = sb("mst", [4, NT])
        m2d.close()
        m2e, sb = era("right")
        sel = sb("sel", [4, 6 * P])
        ks = sb("ks", [P, MLH, P])
        ktok = sb("ktok", [P, MLH, 64])
        vs = sb("vs", [P, 4, P])
        qd = sb("qd", [P, 2, P])
        rws = sb("rws", [4, 5, P])
        cwt = sb("cwt", [P, 8])
        dec = sb("dec", [P, 2])
        ml_e = sb("ml_e", [P, 4, P])
        em_sb = sb("em_sb", [P, 4 * P])
        wvx = sb("wvx", [P, 4, 2 * P])
        num_sb = sb("num_sb", [P, 4 * P])
        c_st = sb("c_st", [P, MLH, 2 * P])
        gst2 = [sb("gst2", [P, HT])] * 2
        m2e.close()
        m2b.close()
        eh.close()

        ex, sb = era("left")
        x2 = sb("x2", [P, KD, T])
        eyh, sb = era("left")
        yh = {b: sb(f"yh_{b}", [P, 4, T], F32R) for b in "cba"}
        yl = {b: sb(f"yl_{b}", [P, 4, T], F32R) for b in "cba"}
        m2.close()
        ey.close()
        eg, sb = era("right")
        gt = {g: sb(f"gt_{g}", [P, T]) for g in ("c0", "b0", "a0", "a1", "c1", "b1")}
        mg_hi = sb("mg_hi", [P, 2, T], F32R)
        mg_lo = sb("mg_lo", [P, 2, T], F32R)
        mg = sb("mg", [P, 2, T])
        mtmp = sb("mtmp", [P, HT])
        eg.close()
        eyh.close()
        e2, sb = era("left")
        h2_hi = sb("h2_hi", [P, KD, T], F32R)
        h2_lo = sb("h2_lo", [P, KD, T], F32R)
        f2 = ffn_buffers("2", sb)
        e2.close()
        ex.close()

        bank = [top.enter_context(nc.psum_tensor(f"bank{i}", [P, HT], F32)) for i in range(4)]
        wide = [top.enter_context(nc.psum_tensor(f"wide{i}", [P, 2 * HT], F32)) for i in range(2)]
        bank += [wide[i // 2][:, (i % 2) * HT:(i % 2 + 1) * HT] for i in range(4)]
        bank = [b if i >= 4 else b[:, :] for i, b in enumerate(bank)]

        raw_loaded = [sem(f"raw_loaded{i}") for i in range(2)]
        w_hi_ready = sem("w_hi_ready")
        split_ready = sem("split_ready")
        block_done = sem("block_done")
        const_in, cols_in, mem_in, pos_in, sel_in = (sem(n) for n in ("const_in", "cols_in", "mem_in", "pos_in", "sel_in"))
        x_in = [sem(f"x_in{i}") for i in range(2)]
        x_saved, x_back, out_done = sem("x_saved"), sem("x_back"), sem("out_done")
        gate_stored = [sem(f"gate_stored{i}") for i in range(2)]
        gt_in = {g: sem(f"gt_in_{g}") for g in gt}
        mem_sq, mem_sum, mem_rms, mem_rstd, mem_h, mem_hi, mem_ready = (
            sem(n) for n in ("mem_sq", "mem_sum", "mem_rms", "mem_rstd", "mem_h", "mem_hi", "mem_ready"))
        sq_ready, sq_used, rms_ready, rstd_ready, hf_ready, h_hi_ready, h_ready = (
            sem(n) for n in ("sq_ready", "sq_used", "rms_ready", "rstd_ready", "hf_ready", "h_hi_ready", "h_ready"))
        a_full, a_free, b_full, b_free = sem("a_full"), sem("a_free"), sem("b_full"), sem("b_free")
        u_hi_ready, u_ready, o_full, x_added = sem("u_hi_ready"), sem("u_ready"), sem("o_full"), sem("x_added")

        block = top.enter_context(nc.Block())

        def half(t):
            return slice(t * HT, (t + 1) * HT)

        PAIRS = {"ffn1": 0, "merge": NPAIR, "ffn2": NPAIR + 4}

        def done(j):
            return j + 2

        def prev(j):
            return j + 1

        def lsem(name):
            return sem(name)

        p_full, p_free, psq_ready, stats_done = (sem(n) for n in ("p_full", "p_free", "psq_ready", "stats_done"))
        consts_ready, own = sem("consts_ready"), sem("dve_chain")
        sin_arg, rope_ready = sem("sin_arg"), sem("rope_ready")
        rq_rms, rq_ready = sem("rq_rms"), sem("rq_ready")
        k_sum, k_rms, k_rstd, k_norm, k_swap, k_ready = (sem(n) for n in ("k_sum", "k_rms", "k_rstd", "k_norm", "k_swap", "k_ready"))
        c_sum, c_rms, c_rstd, ck_ready, cv_turned, cv_ready = (sem(n) for n in ("c_sum", "c_rms", "c_rstd", "ck_ready", "cv_turned", "cv_ready"))
        gate_full, gate_done = sem("gate_full"), sem("gate_done")
        (q_mx_ready, q_sw_ready, kv_ready, rq_tile, s1_done, mx_max, mx_bias, rope_t, rope_x, q_rot_ready, mx_exp,
         mx_rinv, mx_p_ready, s2_done, sw_max, sw_bias, sw_exp, sw_rinv, sw_p_ready, neg_done, v_win_ready, mx_turned,
         mx_pt, sw_turned, sw_pt, mx_out, y_c_done, sw_out, y_b_done) = L1 = [lsem(n) for n in (
            "q_mx_ready", "q_sw_ready", "kv_ready", "rq_tile", "s1_done", "mx_max", "mx_bias", "rope_t", "rope_x",
            "q_rot_ready", "mx_exp", "mx_rinv", "mx_p_ready", "s2_done", "sw_max", "sw_bias", "sw_exp", "sw_rinv",
            "sw_p_ready", "neg_done", "v_win_ready", "mx_turned", "mx_pt", "sw_turned", "sw_pt", "mx_out", "y_c_done",
            "sw_out", "y_b_done")]
        sw_small = sem("sw_small")
        ml_small, row_init = sem("ml_small"), sem("row_init")
        y_split, yh_ready, m_full, m_prod, gated = (sem(n) for n in ("y_split", "yh_ready", "m_full", "m_prod", "gated"))
        waited = sem("waited")

        def apart(eng):
            eng.sem_inc(waited, 1)

        def gate_group(pe, feature_group, n, slot, g, t):
            if t == 0:
                pe.wait_ge(split_ready, n + 1)
            pe.wait_ge(gate_done, g * 2 + (t + 1))
            mm = feature_group(bank[t], slot, h_hi, h_lo, half(t))
            mm.then_inc(block_done if t else gate_full, 1)

        def gate_tanh(act, n, g, t, gst):
            if t == 0:
                act.wait_ge(gate_full, g + 1)
            else:
                act.wait_ge(block_done, n + 1)
            act.wait_ge(gate_stored[t], g * 16 + 16)
            if gst[0] is gst[1]:
                act.wait_ge(gate_stored[1 - t], g * 16 + 16 * (1 + t))
            apart(act)
            act.activation(gst[t][:, :], bank[t], ACT.Tanh, bias=cols[:, bass.ds(g + COLS["bgate"][0], 1)],
                           scale=0.5).then_inc(gate_done, 1)
            act.wait_ge(gate_done, g * 2 + (t + 3))
            act.dma_start(gate_scr[bass.ds(g, 1), :, half(t)].rearrange("a p n -> p (a n)"), gst[t][:, :]
                          ).then_inc(gate_stored[t], 16)

        sqs = [p_sw[:, :, :].rearrange("p a b -> p (a b)"), pt_sw[:, :, :].rearrange("p a b -> p (a b)")]
        p_mxf = p_mx[:, :, :].rearrange("p a b -> p (a b)")
        pt_mxf = pt_mx[:, :, :].rearrange("p a b -> p (a b)")
        ckf = ck[:, :, :].rearrange("p a b -> p (a b)")
        w0, w1 = wide[0][:, :], wide[1][:, :]
        k_raw = kv_all[:, 0, 64:64 + T]

        def tile_of(ap, j):
            return ap[:, :, bass.ds(j * P, P)]

        def mix1_pe(pe, feature_group):
            def stats(f):
                pe.wait_ge(psq_ready, f + 1)
                rhs, c, w = (ones[:, 0:1], f, 1) if f < 4 else (blk2, 4 + 2 * (f - 4), 2)
                for t in range(NT):
                    mm = pe.matmul(bank[4][:, 12 * t + c:12 * t + c + w], sqs[f % 2][:, t * P:(t + 1) * P], rhs,
                                   start=True, stop=True)
                mm.then_inc(stats_done, 1)

            for f in range(18):
                n = B_MIX1 + f
                pe.wait_ge(split_ready, n + 1)
                if f < 10:
                    for t in range(2):
                        q = 2 * f + t
                        if q >= 4:
                            pe.wait_ge(p_free, q - 3)
                        mm = feature_group(bank[q % 4], n % 2, h_hi, h_lo, half(t), 16 + 8 * t if f == 0 else None)
                        mm.then_inc(block_done if t else p_full, 1)
                else:
                    q = 10 + f
                    pe.wait_ge(p_free, q - 3)
                    if f == 10:
                        pe.wait_ge(mem_ready, 1)
                    mm = feature_group(bank[q % 4][:, 0:NMEM], n % 2, mh_hi, mh_lo, slice(0, NMEM))
                    mm.then_inc(block_done, 1)
                if 1 <= f <= 8:
                    stats(f - 1)
                if f == 9:
                    pe.wait_ge(psq_ready, 9)
                    for t in range(2):
                        mm = pe.matmul(wide[1][:, half(t)], blk64, sqs[0][:, half(t)], start=True, stop=True)
                    mm.then_inc(k_sum, 1)
                if f == 15:
                    pe.wait_ge(k_norm, 1)
                    for t in range(2):
                        mm = pe.matmul(wide[1][:, half(t)], perm, kv_all[:, 0, 64 + t * HT:64 + (t + 1) * HT], start=True, stop=True)
                    mm.then_inc(k_swap, 1)
                if f == 17:
                    pe.wait_ge(psq_ready, 10)
                    pe.wait_ge(k_ready, 1)
                    for t in range(2):
                        mm = pe.matmul(wide[1][:, half(t)], ones, sqs[1][:, half(t)], start=True, stop=True)
                    mm.then_inc(c_sum, 1)
            pe.wait_ge(p_free, 28)
            pe.wait_ge(rq_rms, 2)
            for h in range(MXH):
                for kk in range(2):
                    mm = pe.transpose(wide[0][:, kk * 4 * P + h * P:kk * 4 * P + (h + 1) * P], p_mx[:, h, kk * P:(kk + 1) * P], ident)
            mm.then_inc(cv_turned, 1)
            pe.wait_ge(ck_ready, 1)
            pe.wait_ge(cv_ready, 1)

            for s in (s1_done, s2_done, mx_turned, sw_turned, mx_out, sw_out):
                pe.sem_inc(s, 1)
            with pe.Fori(0, NT) as j:
                n = j * 2 + B_GATE1
                pe.wait_ge(q_mx_ready, done(j))
                pe.wait_ge(mx_pt, prev(j))
                for h in range(MXH):
                    pe.matmul(w0[:, h * NMEM:(h + 1) * NMEM], q_mx[:, h, :], ck[:, h, :], start=True, stop=True)
                pe.wait_ge(q_sw_ready, done(j))
                pe.wait_ge(y_b_done, prev(j))
                pe.matmul(bank[3], perm, q_sw[:, :, :].rearrange("p a b -> p (a b)"), start=True, stop=True)
                pe.wait_ge(kv_ready, done(j))
                pe.wait_ge(y_c_done, prev(j))
                for w in range(2):
                    mm = pe.transpose(bank[2][:, w * P:(w + 1) * P], kv_st[:, 1, 64 * w:64 * w + P], ident)
                mm.then_inc(s1_done, 1)
                gate_group(pe, feature_group, n, 0, j * 2, 0)
                pe.wait_ge(q_rot_ready, done(j))
                pe.wait_ge(sw_pt, prev(j))
                pe.wait_ge(neg_done, prev(j))
                for g in range(2):
                    pe.matmul(w1[:, g * HT:(g + 1) * HT], negrow[0:1, 0:P],
                              negrow[0:1, P:2 * P].unsqueeze(1).broadcast_to([1, 4, P]), start=True, stop=False,
                              skip_group_check=True)
                    for i in range(4):
                        for w in range(2):
                            mm = pe.matmul(w1[64 * w:64 * w + 64, g * HT + i * P:g * HT + (i + 1) * P],
                                           q_rot[64 * g:64 * g + 64, i, 64 * w:64 * w + 64],
                                           kv_st[64 * g:64 * g + 64, 0, 64 * w:64 * w + P], start=False, stop=(i == 3 and w == 1),
                                           skip_group_check=True)
                mm.then_inc(s2_done, 1)
                gate_group(pe, feature_group, n, 0, j * 2, 1)
                pe.wait_ge(mx_p_ready, done(j))
                for h in range(MXH):
                    for kk in range(2):
                        mm = pe.transpose(w0[:, (2 * h + kk) * P:(2 * h + kk + 1) * P], p_mx[:, h, kk * P:(kk + 1) * P], ident)
                mm.then_inc(mx_turned, 1)
                gate_group(pe, feature_group, n + 1, 1, j * 2 + 1, 0)
                pe.wait_ge(sw_p_ready, done(j))
                for h in range(SWH):
                    mm = pe.transpose(w1[:, h * P:(h + 1) * P], p_sw[:, h, :], ident)
                mm.then_inc(sw_turned, 1)
                pe.wait_ge(mx_pt, done(j))
                pe.wait_ge(v_win_ready, done(j))
                for h in range(MXH):
                    for kk in range(2):
                        mm = pe.matmul(bank[2][:, h * P:(h + 1) * P], cv[:, kk, h * P:(h + 1) * P], pt_mx[:, 2 * h + kk, :],
                                       start=kk == 0, stop=kk == 1)
                mm.then_inc(mx_out, 1)
                gate_group(pe, feature_group, n + 1, 1, j * 2 + 1, 1)
                pe.wait_ge(sw_pt, done(j))
                b3 = bank[3].rearrange("p (i c) -> p i c", i=4)
                for g in range(2):
                    for w in range(2):
                        mm = pe.matmul(b3[64 * g:64 * g + 64, :, 64 * w:64 * w + 64], v_win[:, w, 64 * g:64 * g + 64],
                                       pt_sw[:, 4 * g:4 * g + 4, 64 * w:64 * w + 64], start=True, stop=True)
                mm.then_inc(sw_out, 1)

        def mix1_act(act):
            act.wait_ge(h_hi_ready, 32)
            act.wait_ge(x_added, 16 * NPAIR + 16)
            act.dma_start(x_scr, x1[:, :, :]).then_inc(x_saved, 16)
            act.wait_ge(x_saved, 16)
            act.wait_ge(h_ready, 32)
            act.dma_start(pos_i, pos).then_inc(pos_in, 16)
            for f in range(8):
                act.wait_ge(p_free, 2 * f + 2)
                if f >= 2:
                    act.wait_ge(stats_done, f - 1)
                act.activation(sqs[f % 2], (y_c if f < 4 else y_b)[:, f % 4, :], ACT.Square).then_inc(psq_ready, 1)
                if f == 3:
                    for i, table in enumerate((rope_s, rope_c)):
                        act.wait_ge(sin_arg, i + 1)
                        act.activation(table[:, :], table[:, :], ACT.Sin).then_inc(rope_ready, 1)
            act.wait_ge(p_free, 18)
            act.wait_ge(stats_done, 7)
            act.activation(sqs[0], k_raw, ACT.Square).then_inc(psq_ready, 1)
            act.wait_ge(stats_done, 8)
            st = bank[4][:, 0:12 * NT].rearrange("p (t c) -> p t c", c=12)
            act.activation(rq[:, :, 0:4], st[:, :, 0:4], ACT.Sqrt, bias=col("eps"), scale=1.0 / P).then_inc(rq_rms, 1)
            act.activation(rq[:, :, 4:12], st[:, :, 4:12], ACT.Sqrt, bias=col("eps"), scale=1.0 / 64).then_inc(rq_rms, 1)
            act.wait_ge(k_sum, 1)
            act.wait_ge(sin_arg, 2)
            act.activation(pt_mxf, w1, ACT.Sqrt, bias=col("eps"), scale=1.0 / 64).then_inc(k_rms, 1)
            act.wait_ge(p_free, 24)
            act.activation(sqs[1], ckf, ACT.Square).then_inc(psq_ready, 1)
            act.wait_ge(c_sum, 1)
            act.activation(sqs[0], w1, ACT.Sqrt, bias=col("eps"), scale=1.0 / P).then_inc(c_rms, 1)
            act.wait_ge(cv_turned, 1)
            act.activation(cv[:, :, :].rearrange("p a b -> p (a b)"), w0, ACT.Copy).then_inc(cv_ready, 1)
            act.wait_ge(c_rstd, 1)
            act.wait_ge(ck_ready, 1)
            for s in (mx_exp, sw_exp, v_win_ready, mx_pt, sw_pt, y_c_done, y_b_done):
                act.sem_inc(s, 1)
            act.sem_inc(gate_done, 2)
            for t in range(2):
                act.sem_inc(gate_stored[t], 16)
            with act.Fori(0, NT) as j:
                n = j * 2 + B_GATE1
                act.wait_ge(mx_bias, done(j))
                act.wait_ge(mx_turned, prev(j))
                for h in range(MXH):
                    ins = act.activation(p_mx[:, h, :], w0[:, h * NMEM:(h + 1) * NMEM], ACT.Exp, bias=nb_mx[:, h:h + 1],
                                         scale=rq_st[:, h:h + 1], accum_out=sum_mx[:, h:h + 1])
                ins.then_inc(mx_exp, 1)
                act.wait_ge(sw_out, prev(j))
                act.activation(v_win[:, :, :].rearrange("p a b -> p (a b)"), bank[2][:, 0:2 * P], ACT.Copy).then_inc(v_win_ready, 1)
                gate_tanh(act, n, j * 2, 0, gst1)
                act.wait_ge(sw_bias, done(j))
                act.wait_ge(sw_turned, prev(j))
                act.activation(es[:, :], es_in[:, :], ACT.Exp)
                for h in range(SWH):
                    c = 4 + 2 * (h % 4) + h // 4
                    ins = act.activation(p_sw[:, h, :], w1[:, h * P:(h + 1) * P], ACT.Exp, bias=nb_sw[:, h:h + 1],
                                         scale=rq_st[:, c:c + 1], accum_out=sum_sw[:, h:h + 1])
                ins.then_inc(sw_exp, 1)
                gate_tanh(act, n, j * 2, 1, gst1)
                act.wait_ge(mx_turned, done(j))
                act.wait_ge(mx_out, prev(j))
                act.activation(pt_mxf, w0, ACT.Copy).then_inc(mx_pt, 1)
                gate_tanh(act, n + 1, j * 2 + 1, 0, gst1)
                act.wait_ge(sw_turned, done(j))
                act.wait_ge(sw_out, prev(j))
                act.activation(sqs[1], w1, ACT.Copy).then_inc(sw_pt, 1)
                act.wait_ge(mx_out, done(j))
                apart(act)
                act.activation(tile_of(y_c, j), bank[2].rearrange("p (a b) -> p a b", a=4), ACT.Copy).then_inc(y_c_done, 1)
                gate_tanh(act, n + 1, j * 2 + 1, 1, gst1)
                act.wait_ge(sw_out, done(j))
                apart(act)
                act.activation(tile_of(y_b, j), bank[3].rearrange("p (a b) -> p a b", a=4), ACT.Copy).then_inc(y_b_done, 1)

        def mix1_dve(dve):
            step = [0]

            def chain(ins):
                ins.then_inc(own, 1)
                step[0] += 1
                dve.wait_ge(own, step[0])

            def evac(f, dst, t):
                if f < 10:
                    q, width = 2 * f + t, HT
                    if t == 0:
                        dve.wait_ge(p_full, f + 1)
                    else:
                        dve.wait_ge(block_done, B_MIX1 + f + 1)
                else:
                    q, width = 10 + f, NMEM
                    dve.wait_ge(block_done, B_MIX1 + f + 1)
                dve.tensor_copy(dst, bank[q % 4][:, 0:width]).then_inc(p_free, 1)

            def angles():
                dve.wait_ge(pos_in, 16)
                chain(dve.tensor_copy(rope_c[:, :], pos_i))
                chain(dve.tensor_scalar(p_mxf, rope_c[:, :], col("inv"), None, ALU.mult))
                for table, turn in ((rope_s, 0.0), (rope_c, 0.25)):
                    chain(dve.tensor_scalar(pt_mxf, p_mxf, 1.0 / (2 * math.pi), turn, ALU.mult, ALU.add))
                    chain(dve.tensor_scalar(pt_mxf, pt_mxf, ROUND, ROUND, ALU.add, ALU.subtract))
                    src = p_mxf
                    for part in (PI2_A, PI2_B, PI2_C):
                        chain(dve.scalar_tensor_tensor(table[:, :], pt_mxf, -part, src, ALU.mult, ALU.add))
                        src = table[:, :]
                    chain(dve.tensor_scalar(table[:, :], table[:, :], 2 * math.pi * turn, PI_IN, ALU.add, ALU.min))
                    dve.tensor_scalar(table[:, :], table[:, :], -PI_IN, None, ALU.max).then_inc(sin_arg, 1)
                    dve.wait_ge(sin_arg, 1 if turn == 0.0 else 2)

            dve.wait_ge(x_saved, 16)
            chain(dve.memset(kv_all[:, :, 0:64], 0.0))
            chain(dve.memset(negrow[:, :], 0.0))
            chain(dve.memset(negrow[0:1, 0:64], 1.0))
            chain(dve.memset(negrow[0:1, P:P + 64], NEG))
            chain(dve.tensor_scalar(gains[:, 0:1], col("swq"), 64 ** -0.5, None, ALU.mult))
            chain(dve.scalar_tensor_tensor(gains[:, 1:2], col("mxq"), float(P) ** -0.5, col("mxk"), ALU.mult, ALU.mult))
            for f in range(10):
                for t in range(2):
                    dst = (y_c[:, f % 4, half(t)] if f < 4 else y_b[:, f % 4, half(t)] if f < 8
                           else kv_all[:, f - 8, 64 + t * HT:64 + (t + 1) * HT])
                    evac(f, dst, t)
                if f == 0:
                    angles()
            for f in range(10, 14):
                evac(f, ck[:, f - 10, :], 0)
            dve.wait_ge(k_rms, 1)
            dve.reciprocal(pt_mxf, pt_mxf).then_inc(k_rstd, 1)
            dve.wait_ge(k_rstd, 1)
            dve.scalar_tensor_tensor(k_raw, k_raw, col("swk"), pt_mxf, ALU.mult, ALU.mult).then_inc(k_norm, 1)
            dve.wait_ge(rq_rms, 2)
            dve.reciprocal(rq[:, :, :], rq[:, :, :]).then_inc(rq_ready, 1)
            for f in range(14, 16):
                evac(f, p_mx[:, f - 14, :], 0)
            dve.wait_ge(k_swap, 1)
            dve.wait_ge(rope_ready, 2)
            dve.wait_ge(k_norm, 1)
            chain(dve.tensor_tensor(pt_mxf, w1, rope_s[:, :], ALU.mult))
            chain(dve.tensor_tensor(k_raw, k_raw, rope_c[:, :], ALU.mult))
            dve.tensor_tensor(k_raw, k_raw, pt_mxf, ALU.add).then_inc(k_ready, 1)
            dve.wait_ge(k_ready, 1)
            for f in range(16, 18):
                evac(f, p_mx[:, f - 14, :], 0)
            dve.wait_ge(c_rms, 1)
            dve.reciprocal(sqs[0], sqs[0]).then_inc(c_rstd, 1)
            dve.wait_ge(c_rstd, 1)
            dve.scalar_tensor_tensor(ckf, ckf, gains[:, 1:2], sqs[0], ALU.mult, ALU.mult).then_inc(ck_ready, 1)
            dve.wait_ge(rq_ready, 1)

            for s in (q_mx_ready, q_sw_ready, kv_ready, rq_tile, mx_max, mx_bias, rope_t, rope_x, q_rot_ready, mx_rinv,
                      mx_p_ready, sw_max, sw_bias, sw_rinv, sw_p_ready, neg_done):
                dve.sem_inc(s, 1)
            rqt = rq_st[:, 4:12].rearrange("p (i g) -> p g i", g=2)
            with dve.Fori(0, NT) as j:
                dve.wait_ge(s1_done, prev(j))
                dve.tensor_copy(q_mx[:, :, :], tile_of(y_c, j)).then_inc(q_mx_ready, 1)
                dve.wait_ge(q_rot_ready, prev(j))
                dve.tensor_scalar(q_sw[:, :, :], tile_of(y_b, j), gains[:, 0:1], None, ALU.mult).then_inc(q_sw_ready, 1)
                dve.wait_ge(s2_done, prev(j))
                dve.tensor_copy(kv_st[:, :, :], kv_all[:, :, bass.ds(j * P, WIN)]).then_inc(kv_ready, 1)
                dve.wait_ge(sw_exp, prev(j))
                dve.tensor_copy(rq_st[:, :], rq[:, bass.ds(j, 1), :].rearrange("p a b -> p (a b)")).then_inc(rq_tile, 1)
                dve.wait_ge(s1_done, done(j))
                dve.tensor_reduce(m_mx[:, :], w0.rearrange("p (h k) -> p h k", h=MXH), AX.X, ALU.max).then_inc(mx_max, 1)
                dve.wait_ge(mx_max, done(j))
                dve.wait_ge(rq_tile, done(j))
                dve.scalar_tensor_tensor(nb_mx[:, :], m_mx[:, :], -1.0, rq_st[:, 0:4], ALU.mult, ALU.mult).then_inc(mx_bias, 1)
                dve.tensor_tensor(q_tmp[:, :, :], bank[3].rearrange("p (a b) -> p a b", a=4),
                                  rope_s[:, bass.ds(j * P, P)].unsqueeze(1).broadcast_to([P, 4, P]), ALU.mult).then_inc(rope_t, 1)
                dve.wait_ge(q_sw_ready, done(j))
                dve.tensor_tensor(q_rot[:, :, :], q_sw[:, :, :],
                                  rope_c[:, bass.ds(j * P, P)].unsqueeze(1).broadcast_to([P, 4, P]), ALU.mult).then_inc(rope_x, 1)
                dve.wait_ge(rope_t, done(j))
                dve.wait_ge(rope_x, done(j))
                dve.tensor_tensor(q_rot[:, :, :], q_rot[:, :, :], q_tmp[:, :, :], ALU.add).then_inc(q_rot_ready, 1)
                dve.wait_ge(mx_exp, done(j))
                dve.reciprocal(ri_mx[:, :], sum_mx[:, :]).then_inc(mx_rinv, 1)
                dve.wait_ge(mx_rinv, done(j))
                dve.tensor_tensor(p_mx[:, :, :], p_mx[:, :, :], ri_mx[:, :].unsqueeze(2).broadcast_to([P, MXH, NMEM]),
                                  ALU.mult).then_inc(mx_p_ready, 1)
                dve.wait_ge(s2_done, done(j))
                dve.memset(negrow[0:1, P:P + 64], 0.0).then_inc(neg_done, 1)
                dve.tensor_reduce(m_sw[:, :], w1.rearrange("p (h k) -> p h k", h=SWH), AX.X, ALU.max).then_inc(sw_max, 1)
                dve.wait_ge(sw_max, done(j))
                dve.tensor_tensor(m_sw[:, :].rearrange("p (g i) -> p g i", g=2), m_sw[:, :].rearrange("p (g i) -> p g i", g=2),
                                  rqt, ALU.mult).then_inc(sw_small, 1)
                dve.wait_ge(sw_small, j * 4 + 1)
                sink = cols[:, COLS["sink"][0]:COLS["sink"][0] + SWH]
                dve.tensor_tensor(m_sw[:, :], m_sw[:, :], sink, ALU.max).then_inc(sw_small, 1)
                dve.wait_ge(sw_small, j * 4 + 2)
                dve.tensor_scalar(nb_sw[:, :], m_sw[:, :], -1.0, None, ALU.mult).then_inc(sw_small, 1)
                dve.tensor_tensor(es_in[:, :], sink, m_sw[:, :], ALU.subtract).then_inc(sw_bias, 1)
                dve.wait_ge(sw_exp, done(j))
                dve.tensor_tensor(sum_sw[:, :], sum_sw[:, :], es[:, :], ALU.add).then_inc(sw_small, 1)
                dve.wait_ge(sw_small, j * 4 + 4)
                dve.reciprocal(ri_sw[:, :], sum_sw[:, :]).then_inc(sw_rinv, 1)
                dve.wait_ge(sw_rinv, done(j))
                dve.tensor_tensor(p_sw[:, :, :], p_sw[:, :, :], ri_sw[:, :].unsqueeze(2).broadcast_to([P, SWH, P]),
                                  ALU.mult).then_inc(sw_p_ready, 1)

        o_free, conv_step, ml_silu, q_scaled, zi_ready, zabs, row_ln, row_step, row_arg, row_exp, y_a_gain = (sem(n) for n in (
            "o_free", "conv_step", "ml_silu", "q_scaled", "zi_ready", "zabs", "row_ln", "row_step", "row_arg", "row_exp",
            "y_a_gain"))
        (ml_staged, v_staged, b_rows, b_kqv, qd_ready, e_arg, e_exp, e_masked, sc_ready, em_copied, kv_tok, wv_done,
         numden, c_upd, num_copied, den_abs, num_sq, c_new, dn_ready, d2_ready, ms_done, t_ready, t_ok, t_root,
         t_inv, y_norm, y_a_done) = [lsem(n) for n in (
            "ml_staged", "v_staged", "b_rows", "b_kqv", "qd_ready", "e_arg", "e_exp", "e_masked", "sc_ready", "em_copied",
            "kv_tok", "wv_done", "numden", "c_upd", "num_copied", "den_abs", "num_sq", "c_new", "dn_ready", "d2_ready",
            "ms_done", "t_ready", "t_ok", "t_root", "t_inv", "y_norm", "y_a_done")]

        dabs = wvx[:, 0:2, :].rearrange("p a b -> p (a b)")
        sqn = wvx[:, 2:4, :].rearrange("p a b -> p (a b)")
        zrow, irow, lrow, mrow = cpad[0][0:4, 0:T], cpad[1][0:4, 0:T], cacc[0:4, :], reset[:, :]

        def by_chunk(ap):
            return ap.rearrange("p (c t) -> p c t", t=P)

        def mix2_pe(pe, feature_group):
            pe.wait_ge(gate_done, 2 + 32)
            pe.wait_ge(y_b_done, done(NT - 1))
            for f in range(N_MIX2):
                n = B_MIX2 + f
                pe.wait_ge(split_ready, n + 1)
                for t in range(2):
                    q = 2 * f + t
                    if f >= 11:
                        pe.wait_ge(o_free, 2 * (f - 11) + t + 1)
                    else:
                        pe.wait_ge(p_free, 28 + q - 3 if q >= 4 else 28)
                    mm = feature_group(bank[q % 4], n % 2, h_hi, h_lo, half(t))
                    mm.then_inc(block_done if t else p_full, 1)
            pe.wait_ge(o_free, 8)
            pe.wait_ge(sel_in, 16)
            for s in (b_rows, b_kqv, numden, c_upd, ms_done):
                pe.sem_inc(s, 1)
            with pe.Fori(0, NT // 2) as i:
                for u in range(2):
                    j = i * 2 + u
                    n = j + B_GATE2
                    slot = (B_GATE2 + u) % 2
                    pe.wait_ge(ml_staged, done(j))
                    pe.wait_ge(num_copied, prev(j))
                    for h in range(MLH):
                        pe.matmul(bank[2][:, h * P:(h + 1) * P], sel[:, h * P:(h + 1) * P], rws[:, 0, :], start=True, stop=True)
                    pe.wait_ge(em_copied, prev(j))
                    for h in range(MLH):
                        pe.matmul(bank[3][:, h * P:(h + 1) * P], sel[:, h * P:(h + 1) * P], rws[:, 2, :], start=True, stop=True)
                    pe.wait_ge(qd_ready, prev(j))
                    for pr in range(2):
                        pe.matmul(bank[4][:, pr * P:(pr + 1) * P], sel[:, (4 + pr) * P:(5 + pr) * P], rws[:, 1, :], start=True, stop=True)
                    for k in range(2):
                        mm = pe.transpose(bank[4][:, 2 * P + 4 * k:2 * P + 4 * k + 4], rws[:, 3 + k, :], ident[0:4, 0:4])
                    mm.then_inc(b_rows, 1)
                    pe.wait_ge(c_new, prev(j))
                    for h in range(MLH):
                        pe.matmul(bank[5][:, h * P:(h + 1) * P], ks[:, h, :], ml_q[:, h // 2, bass.ds(j * P, P)], start=True, stop=True)
                    pe.wait_ge(t_ready, prev(j))
                    for h in range(MLH):
                        pe.transpose(bank[6][:, h * P:(h + 1) * P], ks[:, h, :], ident)
                    pe.wait_ge(v_staged, done(j))
                    pe.wait_ge(den_abs, prev(j))
                    for h in range(MLH):
                        mm = pe.transpose(bank[7][:, h * P:(h + 1) * P], vs[:, h, :], ident)
                    mm.then_inc(b_kqv, 1)
                    gate_group(pe, feature_group, n, slot, j + 16, 0)
                    pe.wait_ge(sc_ready, done(j))
                    pe.wait_ge(kv_tok, done(j))
                    pe.wait_ge(qd_ready, done(j))
                    pe.matmul(bank[7], ones, ml_e[:, :, :].rearrange("p a b -> p (a b)"), start=True, stop=False, skip_group_check=True)
                    for h in range(MLH):
                        pe.matmul(bank[7][:, h * P:(h + 1) * P], c_st[:, h, P:2 * P], qd[:, h // 2, :],
                                  start=False, stop=h == 3, skip_group_check=True)
                    for h in range(MLH):
                        pe.matmul(bank[2][:, h * P:(h + 1) * P], vs[:, h, :], ml_e[:, h, :], start=True, stop=False)
                        mm = pe.matmul(bank[2][:, h * P:(h + 1) * P], c_st[:, h, 0:P], qd[:, h // 2, :],
                                       start=False, stop=True)
                    mm.then_inc(numden, 1)
                    pe.wait_ge(wv_done, done(j))
                    for h in range(MLH):
                        r = 64 * (h % 2)
                        mm = pe.matmul(bank[5][r:r + 64, (h // 2) * 2 * P:(h // 2 + 1) * 2 * P], ktok[:, h, :],
                                       wvx[:, h, :], start=True, stop=True)
                    mm.then_inc(c_upd, 1)
                    pe.wait_ge(num_sq, done(j))
                    pe.matmul(bank[6], ones, sqn, start=True, stop=True).then_inc(ms_done, 1)
                    gate_group(pe, feature_group, n, slot, j + 16, 1)

        def mix2_act(act):
            for t in range(2):
                act.wait_ge(gate_stored[t], 16 * 17)
            act.wait_ge(y_b_done, done(NT - 1))
            for f in range(4):
                act.wait_ge(conv_step, 4 * (f + 1))
                act.activation((ml_q if f < 2 else ml_k)[:, f % 2, :], cacc[:, :], ACT.Silu).then_inc(ml_silu, 1)
            act.wait_ge(zi_ready, 4)
            act.wait_ge(ml_silu, 4)
            act.activation(lrow, zrow, ACT.Abs).then_inc(zabs, 1)
            act.wait_ge(zabs, 1)
            act.activation(lrow, lrow, ACT.Exp, scale=-1.0).then_inc(zabs, 1)
            act.wait_ge(zabs, 2)
            act.activation(lrow, lrow, ACT.Ln, bias=ones[0:4, 0:1]).then_inc(row_ln, 1)
            act.wait_ge(row_step, 3)
            act.activation(rows[64:68, :], mrow, ACT.Exp, scale=-1.0).then_inc(row_exp, 1)
            act.wait_ge(row_arg, 2)
            act.activation(rows[32:36, :], zrow, ACT.Exp).then_inc(row_exp, 1)
            act.activation(cw[32:36, :], irow, ACT.Exp).then_inc(row_exp, 1)
            act.wait_ge(row_exp, 3)
            act.dma_start(sel[:, :], sel_d).then_inc(sel_in, 16)
            for f in range(9, 13):
                for t in range(2):
                    if t == 0:
                        act.wait_ge(p_full, 10 + f + 1)
                    else:
                        act.wait_ge(block_done, B_MIX2 + f + 1)
                    act.activation(y_a[:, f - 9, half(t)], bank[(2 * f + t) % 4], ACT.Sigmoid).then_inc(o_free, 1)
            for s in (v_staged, e_exp, em_copied, kv_tok, num_copied, den_abs, num_sq, d2_ready, t_root):
                act.sem_inc(s, 1)
            with act.Fori(0, NT // 2) as i:
                for u in range(2):
                    j = i * 2 + u
                    n = j + B_GATE2
                    act.wait_ge(numden, prev(j))
                    act.wait_ge(wv_done, prev(j))
                    apart(act)
                    act.activation(vs[:, :, :], tile_of(ml_v, j), ACT.Copy).then_inc(v_staged, 1)
                    act.wait_ge(b_rows, done(j))
                    act.wait_ge(y_norm, prev(j))
                    act.activation(em_sb[:, :], bank[3], ACT.Copy).then_inc(em_copied, 1)
                    act.wait_ge(e_arg, done(j))
                    ef = ml_e[:, :, :].rearrange("p a b -> p (a b)")
                    act.activation(ef, ef, ACT.Exp).then_inc(e_exp, 1)
                    act.wait_ge(b_kqv, done(j))
                    for o in range(2):
                        act.activation(ktok[:, o:MLH:2, :], bank[6].rearrange("p (a b) -> p a b", a=4)[:, o:MLH:2, 64 * o:64 * o + 64],
                                       ACT.Copy)
                    act.activation(vs[:, :, :].rearrange("p a b -> p (a b)"), bank[7], ACT.Copy).then_inc(kv_tok, 1)
                    gate_tanh(act, n, j + 16, 0, gst2)
                    act.wait_ge(numden, done(j))
                    act.activation(num_sb[:, :], bank[2], ACT.Copy).then_inc(num_copied, 1)
                    act.wait_ge(c_upd, done(j))
                    act.wait_ge(num_copied, done(j))
                    act.activation(sqn, num_sb[:, :], ACT.Square).then_inc(num_sq, 1)
                    act.activation(dabs, bank[7], ACT.Abs).then_inc(den_abs, 1)
                    act.wait_ge(dn_ready, done(j))
                    act.activation(em_sb[:, :], em_sb[:, :], ACT.Square, scale=EPS ** 0.5).then_inc(d2_ready, 1)
                    act.wait_ge(t_ok, done(j))
                    act.activation(em_sb[:, :], em_sb[:, :], ACT.Sqrt).then_inc(t_root, 1)
                    gate_tanh(act, n, j + 16, 1, gst2)

        def mix2_dve(dve):
            for t in range(2):
                dve.wait_ge(gate_stored[t], 16 * 17)
            dve.wait_ge(y_b_done, done(NT - 1))
            inits = [(cpad[0][:, 0:3], 0.0), (cpad[1][:, 0:3], 0.0), (rows[:, :], 0.0), (cw[:, :], 0.0),
                     (reset[:, :], 1.0), (mst[:, :], 0.0)]
            for k, (where, value) in enumerate(inits):
                dve.memset(where, value).then_inc(row_init, 1)
            dve.wait_ge(row_init, len(inits))
            dve.memset(by_chunk(reset[:, :])[:, :, 0:1], 0.0).then_inc(row_init, 1)

            def wait_full(f, t):
                if t == 0:
                    dve.wait_ge(p_full, 10 + f + 1)
                else:
                    dve.wait_ge(block_done, B_MIX2 + f + 1)

            for f in range(4):
                pad = cpad[f % 2]
                for t in range(2):
                    wait_full(f, t)
                    dve.tensor_copy(pad[:, 3 + t * HT:3 + (t + 1) * HT], bank[(2 * f + t) % 4]).then_inc(p_free, 1)
                dve.wait_ge(p_free, 28 + 2 * f + 2)
                if f:
                    dve.wait_ge(ml_silu, f)
                for s, tap in enumerate((3, 2, 1, 0)):
                    w = col("convq" if f < 2 else "convk", 4 * (f % 2) + tap)
                    if s == 0:
                        dve.tensor_scalar(cacc[:, :], pad[:, tap:tap + T], w, None, ALU.mult).then_inc(conv_step, 1)
                    else:
                        dve.wait_ge(conv_step, 4 * f + s)
                        dve.scalar_tensor_tensor(cacc[:, :], pad[:, tap:tap + T], w, cacc[:, :], ALU.mult, ALU.add
                                                 ).then_inc(conv_step, 1)
            dve.wait_ge(ml_silu, 2)
            dve.tensor_scalar(ml_q[:, :, :], ml_q[:, :, :], 64 ** -0.5, None, ALU.mult).then_inc(q_scaled, 1)
            for t in range(2):
                wait_full(4, t)
                b = bank[(8 + t) % 4]
                dve.wait_ge(conv_step, 16)
                dve.tensor_scalar(zrow[:, half(t)], b[32:36, :], col("bf", 0, 32, 36), None, ALU.add).then_inc(zi_ready, 1)
                dve.tensor_scalar(irow[:, half(t)], b[0:4, :], col("bi", 0, 0, 4), None, ALU.add).then_inc(zi_ready, 1)
                dve.wait_ge(zi_ready, 2 * t + 2)
                dve.sem_inc(p_free, 1)
            dve.wait_ge(row_ln, 1)
            dve.scalar_tensor_tensor(zrow, zrow, 0.0, lrow, ALU.min, ALU.subtract).then_inc(row_step, 1)
            dve.wait_ge(row_step, 1)
            dve.wait_ge(row_init, len(inits) + 1)
            dve.tensor_tensor_scan(lrow, reset[:, :], zrow, 0.0, ALU.mult, ALU.add).then_inc(row_step, 1)
            dve.wait_ge(row_step, 2)
            dve.tensor_tensor_scan(mrow, zrow, irow, 0.0, ALU.add, ALU.max).then_inc(row_step, 1)
            dve.wait_ge(row_step, 3)
            dve.tensor_tensor(rows[0:4, :], lrow, mrow, ALU.subtract).then_inc(row_step, 1)
            dve.tensor_tensor(cw[0:4, :], irow, lrow, ALU.subtract).then_inc(row_step, 1)
            dve.tensor_copy(mst[:, 1:NT].unsqueeze(2), by_chunk(mrow)[:, 0:NT - 1, P - 1:P]).then_inc(row_step, 1)
            dve.wait_ge(row_step, 6)
            r_c, c_c = by_chunk(rows[0:4, :]), by_chunk(cw[0:4, :])
            dve.tensor_tensor(by_chunk(zrow), r_c, mst[:, :].unsqueeze(2).broadcast_to([4, NT, P]), ALU.add).then_inc(row_arg, 1)
            dve.tensor_tensor(by_chunk(irow), c_c, r_c[:, :, P - 1:P].broadcast_to([4, NT, P]), ALU.add).then_inc(row_arg, 1)
            for f in range(5, 9):
                for t in range(2):
                    wait_full(f, t)
                    dve.tensor_copy(ml_v[:, f - 5, half(t)], bank[(2 * f + t) % 4]).then_inc(p_free, 1)
            for i in range(4):
                dve.wait_ge(o_free, 2 * i + 2)
                dve.tensor_scalar(y_a[:, i, :], y_a[:, i, :], col("mlnorm", i), None, ALU.mult).then_inc(y_a_gain, 1)
            dve.wait_ge(y_a_gain, 4)
            dve.wait_ge(row_exp, 3)
            dve.wait_ge(q_scaled, 1)
            dve.memset(c_st[:, :, :], 0.0).then_inc(row_init, 1)
            dve.memset(ks[:, :, :], 0.0).then_inc(row_init, 1)
            dve.wait_ge(row_init, len(inits) + 3)
            for s in (ml_staged, qd_ready, e_arg, e_masked, sc_ready, wv_done, c_new, dn_ready, t_ready, t_ok, t_inv,
                      y_norm, y_a_done):
                dve.sem_inc(s, 1)
            with dve.Fori(0, NT // 2) as i:
                for u in range(2):
                    j = i * 2 + u
                    tok = bass.ds(j * P, P)
                    dve.wait_ge(c_upd, prev(j))
                    for k, row in enumerate((rows[0:4, tok], rows[32:36, tok], rows[64:68, tok], cw[0:4, tok], cw[32:36, tok])):
                        dve.tensor_copy(rws[:, k, :], row)
                    for o in range(2):
                        r = 64 * o
                        ins = dve.tensor_copy(ks[r:r + 64, o:MLH:2, :], ml_k[r:r + 64, :, tok])
                    ins.then_inc(ml_staged, 1)
                    dve.wait_ge(b_rows, done(j))
                    dve.tensor_copy(cwt[:, :], bank[4][:, 2 * P:2 * P + 8]).then_inc(ml_small, 1)
                    dve.tensor_copy(dec[:, :].unsqueeze(2), by_chunk(bank[4][:, 0:2 * P])[:, :, P - 1:P]).then_inc(ml_small, 1)
                    dve.tensor_tensor(qd[:, :, :], tile_of(ml_q, j), by_chunk(bank[4][:, 0:2 * P]), ALU.mult).then_inc(qd_ready, 1)
                    dve.wait_ge(ml_small, j * 2 + 2)
                    for h in range(MLH):
                        ins = dve.tensor_scalar(ml_e[:, h, :], bank[2][:, h * P:(h + 1) * P], cwt[:, h:h + 1], 0.0, ALU.add, ALU.min)
                    ins.then_inc(e_arg, 1)
                    dve.wait_ge(e_exp, done(j))
                    dve.tensor_tensor(ml_e[:, :, :], ml_e[:, :, :], mask.unsqueeze(1).broadcast_to([P, MLH, P]), ALU.mult
                                      ).then_inc(e_masked, 1)
                    dve.wait_ge(e_masked, done(j))
                    dve.wait_ge(b_kqv, done(j))
                    dve.tensor_tensor(ml_e[:, :, :], ml_e[:, :, :], by_chunk(bank[5]), ALU.mult).then_inc(sc_ready, 1)
                    dve.wait_ge(kv_tok, done(j))
                    dve.tensor_tensor(wvx[:, :, 0:P], vs[:, :, :], cwt[:, 4:8].unsqueeze(2).broadcast_to([P, MLH, P]), ALU.mult)
                    dve.tensor_copy(wvx[:, :, P:2 * P], cwt[:, 4:8].unsqueeze(2).broadcast_to([P, MLH, P])).then_inc(wv_done, 1)
                    dve.wait_ge(c_upd, done(j))
                    for h in range(MLH):
                        r, pr = 64 * (h % 2), h // 2
                        ins = dve.scalar_tensor_tensor(c_st[r:r + 64, h, :], c_st[r:r + 64, h, :], dec[r:r + 64, pr:pr + 1],
                                                       bank[5][r:r + 64, pr * 2 * P:(pr + 1) * 2 * P], ALU.mult, ALU.add)
                    ins.then_inc(c_new, 1)
                    dve.wait_ge(den_abs, done(j))
                    dve.tensor_tensor(em_sb[:, :], em_sb[:, :], dabs, ALU.max).then_inc(dn_ready, 1)
                    dve.wait_ge(ms_done, done(j))
                    dve.wait_ge(d2_ready, done(j))
                    dve.scalar_tensor_tensor(em_sb[:, :], bank[6], 1.0 / P, em_sb[:, :], ALU.mult, ALU.add).then_inc(t_ready, 1)
                    dve.wait_ge(t_ready, done(j))
                    dve.tensor_scalar(em_sb[:, :], em_sb[:, :], 2.0 ** -116, 2.0 ** 117, ALU.max, ALU.min).then_inc(t_ok, 1)
                    dve.wait_ge(t_root, done(j))
                    dve.reciprocal(em_sb[:, :], em_sb[:, :]).then_inc(t_inv, 1)
                    dve.wait_ge(t_inv, done(j))
                    dve.tensor_tensor(num_sb[:, :], num_sb[:, :], em_sb[:, :], ALU.mult).then_inc(y_norm, 1)
                    dve.wait_ge(y_norm, done(j))
                    dve.tensor_tensor(tile_of(y_a, j), tile_of(y_a, j), by_chunk(num_sb[:, :]), ALU.mult).then_inc(y_a_done, 1)

        ys = {"c": y_c, "b": y_b, "a": y_a}
        MERGE = ((("c", 0), ("b", 0)), (("a", 0), ("a", 1)), (("c", 1), ("b", 1)))

        def merge_block(p, b):
            return B_MERGE + b if p == 0 else B_MERGE + 3 + 5 * (p - 1) + (b if b < 2 else 4)

        def merge_out(p):
            return B_MERGE + (5 * (p + 1) if p < 3 else 18)

        def merge_pe(pe, passes, project_out):
            def products(p, b):
                n = merge_block(p, b)
                pe.wait_ge(split_ready, n + 1)
                for i, (branch, _) in enumerate(MERGE[b]):
                    for t in range(2):
                        g = 2 * i + t
                        q = 3 * p + b
                        if q:
                            pe.wait_ge(gated, 4 * q + g - 3)
                        for k in range(4):
                            if p == 0 and t == 0:
                                pe.wait_ge(y_split, 4 * "cba".index(branch) + k + 1)
                            mm = passes(bank[g], n % 2, (4 * i + k) * P, yh[branch][:, k, half(t)], yl[branch][:, k, half(t)],
                                        k == 0, k == 3)
                        mm.then_inc(block_done if g == 3 else m_full, 1)

            pe.wait_ge(gate_done, 2 * NG + 2)
            pe.wait_ge(t_ready, done(NT - 1))
            for p in range(4):
                products(p, 0)
                products(p, 1)
                if p:
                    project_out(PAIRS["merge"] + p - 1, merge_out(p - 1), merge_out(p - 1) % 2, mg_hi, mg_lo)
                products(p, 2)
            project_out(PAIRS["merge"] + 3, merge_out(3), merge_out(3) % 2, mg_hi, mg_lo)

        def merge_act(act):
            act.wait_ge(block_done, B_MERGE)
            for t in range(2):
                act.wait_ge(gate_stored[t], 16 * (NG + 1))
            for b in "cba":
                if b == "a":
                    act.wait_ge(y_a_done, done(NT - 1))
                for k in range(4):
                    act.activation(yh[b][:, k, :], ys[b][:, k, :], ACT.Copy).then_inc(yh_ready, 1)
            act.wait_ge(y_split, 12)
            for p in range(4):
                for m in range(2):
                    for t in range(2):
                        act.wait_ge(gated, 12 * p + (5 + t if m == 0 else 11 + t))
                        if p and m == 0 and t == 0:
                            act.wait_ge(block_done, merge_out(p - 1) + 2)
                        act.activation(mg_hi[:, m, half(t)], mg[:, m, half(t)], ACT.Copy).then_inc(u_hi_ready, 1)

        def merge_dve(dve, add_out, split_u):
            dve.wait_ge(block_done, B_MERGE)
            for t in range(2):
                dve.wait_ge(gate_stored[t], 16 * (NG + 1))
            dve.wait_ge(y_a_done, done(NT - 1))
            for b in "cba":
                for k in range(4):
                    dve.wait_ge(yh_ready, 4 * "cba".index(b) + k + 1)
                    dve.tensor_tensor(yl[b][:, k, :], ys[b][:, k, :], yh[b][:, k, :], ALU.subtract).then_inc(y_split, 1)
            dve.wait_ge(y_split, 12)

            def gate(p, b):
                n = merge_block(p, b)
                for i, (branch, m) in enumerate(MERGE[b]):
                    g = gt[branch + str(m)]
                    for t in range(2):
                        if 2 * i + t == 3:
                            dve.wait_ge(block_done, n + 1)
                        else:
                            dve.wait_ge(m_full, 9 * p + 3 * b + 2 * i + t + 1)
                        if t == 0:
                            dve.wait_ge(gt_in[branch + str(m)], 16 * (p + 1))
                        first = (branch, m) in (("c", 0), ("a", 1))
                        dst = mg[:, m, half(t)] if first else mtmp[:, :]
                        count = 12 * p + 4 * b + 2 * i + t + 1
                        if count > 1:
                            dve.wait_ge(gated, count - 1)
                        ins = dve.scalar_tensor_tensor(dst, g[:, half(t)], 1.0, bank[2 * i + t], ALU.add, ALU.mult)
                        if first:
                            ins.then_inc(gated, 1)
                        else:
                            ins.then_inc(m_prod, 1)
                            m_count[0] += 1
                            dve.wait_ge(m_prod, m_count[0])
                            dve.tensor_tensor(mg[:, m, half(t)], mg[:, m, half(t)], mtmp[:, :], ALU.add).then_inc(gated, 1)

            m_count = [0]
            for p in range(4):
                gate(p, 0)
                gate(p, 1)
                if p:
                    add_out(PAIRS["merge"] + p - 1, merge_out(p - 1), x2)
                else:
                    dve.wait_ge(x_back, 16)
                split_u(PAIRS["merge"] + p, 0, mg, mg_hi, mg_lo)
                gate(p, 2)
                split_u(PAIRS["merge"] + p, 1, mg, mg_hi, mg_lo)
            add_out(PAIRS["merge"] + 3, merge_out(3), x2)

        @block.sync
        def _(sp):
            def load(n, slot):
                sp.wait_ge(split_ready, n - 1)
                sp.dma_start(raw[slot][:, :], wts[bass.ds(n, 1)].rearrange("a p n -> p (a n)")
                             ).then_inc(raw_loaded[slot], 16)

            def load_gate(g, m, uses):
                if uses:
                    sp.wait_ge(gated, uses)
                elif g == "c0":
                    sp.wait_ge(y_split, 12)
                    for i in range(2):
                        sp.wait_ge(gate_stored[i], 16 * (NG + 1))
                sp.dma_start(gt[g][:, :], gate_scr[{"a": 0, "b": 8, "c": 16}[g[0]] + m]).then_inc(gt_in[g], 16)

            sp.dma_start(cst[:, :], const_d).then_inc(const_in, 16)
            for t in range(2):
                sp.dma_start(x1[:, :, half(t)], xT[:, :, half(t)]).then_inc(x_in[t], 16)
                sp.dma_start(raw[t][:, :], wts[t]).then_inc(raw_loaded[t], 16)
            first = B_MERGE // 2
            with sp.Fori(1, first) as i:
                load(i * 2, 0)
                load(i * 2 + 1, 1)
            for n in range(2 * first, B_MERGE):
                load(n, n % 2)
            for k in range(20):
                for p in range(1, 4):
                    if k == 5 * p - 2:
                        load_gate("c0", 2 * p, 12 * (p - 1) + 2)
                        load_gate("b0", 2 * p, 12 * (p - 1) + 4)
                    if k == 5 * p - 1:
                        load_gate("a0", 2 * p, 12 * (p - 1) + 6)
                        load_gate("a1", 2 * p + 1, 12 * (p - 1) + 8)
                    if k == 5 * p + 1:
                        load_gate("c1", 2 * p + 1, 12 * (p - 1) + 10)
                        load_gate("b1", 2 * p + 1, 12 * (p - 1) + 12)
                load(B_MERGE + k, (B_MERGE + k) % 2)
                if k == 1:
                    sp.wait_ge(block_done, B_MERGE)
                    sp.wait_ge(x_saved, 16)
                    sp.dma_start(x2[:, :, :], x_scr).then_inc(x_back, 16)
                    for g in ("c0", "b0", "a0", "a1", "c1", "b1"):
                        load_gate(g, int(g[1]), 0)
            for n in range(B_FFN2, B_FFN2 + B_FFN2 % 2):
                load(n, n % 2)
            with sp.Fori((B_FFN2 + 1) // 2, NB // 2) as i:
                load(i * 2, 0)
                load(i * 2 + 1, 1)
            for n in range(NB - NB % 2, NB):
                load(n, n % 2)
            for k in range(KD):
                sp.wait_ge(x_added, 16 * (PAIRS["ffn2"] + NPAIR) + 2 * k + 2)
                sp.dma_start(out[k], x2[:, k, :]).then_inc(out_done, 16)
            sp.wait_ge(out_done, 16 * KD)

        @block.gpsimd
        def _(pool):
            def split(n, turn, slot):
                if not (isinstance(n, int) and n < 2):
                    pool.wait_ge(block_done, n - 1)
                pool.wait_ge(raw_loaded[slot], turn * 16 + 16)
                apart(pool)
                pool.tensor_scalar(whi[slot][:, :], raw[slot][:, :], 1.0, None, ALU.mult).then_inc(w_hi_ready, 1)
                pool.wait_ge(w_hi_ready, n + 1)
                pool.tensor_tensor(wlo[slot][:, :], raw[slot][:, :], whi[slot][:, :],
                                   ALU.subtract).then_inc(split_ready, 1)

            pool.dma_start(cols[:, :], cols_d).then_inc(cols_in, 16)
            pool.dma_start(memx[:, :, :], memT).then_inc(mem_in, 16)
            pool.wait_ge(cols_in, 16)
            split(0, 0, 0)
            split(1, 0, 1)
            with pool.Fori(1, NB // 2) as i:
                split(i * 2, i, 0)
                split(i * 2 + 1, i, 1)
            for n in range(NB - NB % 2, NB):
                split(n, n // 2, n % 2)

        @block.tensor
        def _(pe):
            def passes(dst, slot, wcol, r_hi, r_lo, first, last):
                w_h, w_l = whi[slot][:, wcol:wcol + P], wlo[slot][:, wcol:wcol + P]
                pe.matmul(dst, w_h, r_hi, start=first, stop=False)
                pe.matmul(dst, w_h, r_lo, start=False, stop=False)
                return pe.matmul(dst, w_l, r_hi, start=False, stop=last)

            def feature_group(dst, slot, hi, lo, cols_of, k_wait=None):
                for k in range(KD):
                    if k_wait is not None:
                        pe.wait_ge(h_ready, k_wait + k + 1)
                    mm = passes(dst, slot, k * P, hi[:, k, cols_of], lo[:, k, cols_of], k == 0, k == KD - 1)
                return mm

            def norm(i):
                for t in range(2):
                    for k in range(KD):
                        n = 16 * i + 8 * t + k
                        pe.wait_ge(sq_ready, n + 1)
                        pe.matmul(bank[t], ones, (f1, f1, f2)[i]["sq"][:, n % 4, :], start=k == 0,
                                  stop=k == KD - 1).then_inc(sq_used, 1)

            def ffn_tile(r, tile, n, slot_a, hi, lo, k_wait=None):
                for which, full, free in ((0, a_full, a_free), (1, b_full, b_free)):
                    slot = (slot_a + which) % 2
                    pe.wait_ge(split_ready, n + which + 1)
                    for t in range(2):
                        if not (isinstance(tile, int) and tile == 0):
                            pe.wait_ge(free, 44 * r + tile * 2 + t - 1)
                        mm = feature_group(bank[2 * which + t], slot, hi, lo, half(t),
                                           k_wait + 8 * t if k_wait is not None and which == 0 else None)
                        mm.then_inc(block_done if t else full, 1)

            def project_out(pair, n, slot0, hi, lo):
                pe.wait_ge(u_ready, pair * 4 + 4)
                for b in range(2):
                    slot = (slot0 + b) % 2
                    pe.wait_ge(split_ready, n + b + 1)
                    for m in range(4):
                        for t in range(2):
                            o = 8 * b + 2 * m + t
                            pe.wait_ge(x_added, pair * 16 + (o + 13))
                            for k in range(2):
                                mm = passes(bank[4 + o % 4], slot, (2 * m + k) * P, hi[:, k, half(t)],
                                            lo[:, k, half(t)], k == 0, k == 1)
                            mm.then_inc(block_done if o % 8 == 7 else o_full, 1)

            def ffn(r, f, hi, lo, b0, pairs, norm_at):
                s0 = b0 % 2
                ffn_tile(r, 0, b0, s0, hi, lo, 16 * norm_at)
                ffn_tile(r, 1, b0 + 2, s0, hi, lo)
                with pe.Fori(1, NPAIR) as c:
                    n = c * 6 + (b0 - 2)
                    ffn_tile(r, c * 2, n, s0, hi, lo)
                    project_out(c + (pairs - 1), n + 2, s0, f["u_hi"], f["u_lo"])
                    ffn_tile(r, c * 2 + 1, n + 4, s0, hi, lo)
                project_out(pairs + NPAIR - 1, b0 + 6 * NPAIR - 2, s0, f["u_hi"], f["u_lo"])

            pe.wait_ge(const_in, 16)
            pe.wait_ge(mem_sq, 1)
            sqv = f1["sq"][:, :, :].rearrange("p a b -> p (a b)")
            for k in range(KD):
                mm = pe.matmul(bank[2][:, 0:NMEM], ones, sqv[:, k * NMEM:(k + 1) * NMEM], start=k == 0, stop=k == KD - 1)
            mm.then_inc(mem_sum, 1)
            norm(0)
            ffn(0, f1, h_hi, h_lo, B_FFN1, PAIRS["ffn1"], 0)
            norm(1)
            mix1_pe(pe, feature_group)
            mix2_pe(pe, feature_group)
            merge_pe(pe, passes, project_out)
            norm(2)
            ffn(1, f2, h2_hi, h2_lo, B_FFN2, PAIRS["ffn2"], 2)

        @block.scalar
        def _(act):
            def norm(i, x, f, hi):
                eps = col("eps")

                def square(t, k):
                    n = 16 * i + 8 * t + k
                    if i == 0 and k == 0:
                        act.wait_ge(x_in[t], 16)
                    if n % 16 >= 4:
                        act.wait_ge(sq_used, n - 3)
                    if i:
                        act.wait_ge(x_added, 16 * (PAIRS["ffn1"] + NPAIR if i == 1 else PAIRS["ffn2"]) + 1 + 2 * k + t)
                    act.activation(f["sq"][:, n % 4, :], x[:, k, half(t)], ACT.Square).then_inc(sq_ready, 1)

                def root(t):
                    act.wait_ge(sq_used, 16 * i + 8 * t + 8)
                    act.activation(f["rs"][:, t, :], bank[t], ACT.Sqrt, bias=eps, scale=1.0 / D).then_inc(rms_ready, 1)

                def round_h(t, k):
                    act.wait_ge(hf_ready, 16 * i + 8 * t + k + 1)
                    act.activation(hi[:, k, half(t)], f["hf"][:, k % 2, :], ACT.Copy).then_inc(h_hi_ready, 1)

                for k in range(KD):
                    square(0, k)
                root(0)
                for k in range(KD):
                    square(1, k)
                root(1)
                for t in range(2):
                    for k in range(KD):
                        round_h(t, k)

            def ffn(r, f, b0, pairs):
                def silu(tile, n, t):
                    if t == 0:
                        act.wait_ge(a_full, tile + (22 * r + 1))
                    else:
                        act.wait_ge(block_done, n + 1)
                    if not (isinstance(tile, int) and tile == 0):
                        act.wait_ge(b_free, tile * 2 + (44 * r + t - 1))
                    act.activation(f["sa"][:, t, :], bank[t], ACT.Silu).then_inc(a_free, 1)

                def round_u(tile, which, t):
                    act.wait_ge(b_free, tile * 2 + (44 * r + t + 1))
                    act.activation(f["u_hi"][:, which, half(t)], f["uf"][:, which, t, :], ACT.Copy).then_inc(u_hi_ready, 1)

                for tile in range(2):
                    for t in range(2):
                        silu(tile, b0 + 2 * tile, t)
                    for t in range(2):
                        round_u(tile, tile, t)
                with act.Fori(1, NPAIR) as c:
                    n = c * 6 + (b0 - 2)
                    for t in range(2):
                        silu(c * 2, n, t)
                    act.wait_ge(block_done, n + 4)
                    for t in range(2):
                        round_u(c * 2, 0, t)
                    for t in range(2):
                        silu(c * 2 + 1, n + 4, t)
                    for t in range(2):
                        round_u(c * 2 + 1, 1, t)

            act.wait_ge(mem_in, 16)
            act.wait_ge(cols_in, 16)
            sqv = f1["sq"][:, :, :].rearrange("p a b -> p (a b)")
            mxv = memx[:, :, :].rearrange("p a b -> p (a b)")
            act.activation(sqv, mxv, ACT.Square).then_inc(mem_sq, 1)
            act.wait_ge(mem_sum, 1)
            act.activation(f1["rs"][:, 0, 0:NMEM], bank[2][:, 0:NMEM], ACT.Sqrt, bias=col("eps"), scale=1.0 / D).then_inc(mem_rms, 1)
            act.wait_ge(mem_h, KD)
            act.activation(mh_hi[:, :, :].rearrange("p a b -> p (a b)"), mxv, ACT.Copy).then_inc(mem_hi, 1)
            norm(0, x1, f1, h_hi)
            ffn(0, f1, B_FFN1, PAIRS["ffn1"])
            norm(1, x1, f1, h_hi)
            mix1_act(act)
            mix2_act(act)
            merge_act(act)
            norm(2, x2, f2, h2_hi)
            ffn(1, f2, B_FFN2, PAIRS["ffn2"])

        @block.vector
        def _(dve):
            def norm(i, x, f, hi, lo, gain):
                for t in range(2):
                    dve.wait_ge(rms_ready, 2 * i + t + 1)
                    dve.reciprocal(f["rs"][:, t, :], f["rs"][:, t, :]).then_inc(rstd_ready, 1)
                    dve.wait_ge(rstd_ready, 2 * i + t + 1)
                    for k in range(KD + 1):
                        n = 16 * i + 8 * t + k
                        if k < KD:
                            if n % 16 >= 2:
                                dve.wait_ge(h_ready, n - 1)
                            dve.scalar_tensor_tensor(f["hf"][:, k % 2, :], x[:, k, half(t)], col(gain, k), f["rs"][:, t, :],
                                                     ALU.mult, ALU.mult).then_inc(hf_ready, 1)
                        if k:
                            dve.wait_ge(h_hi_ready, n)
                            dve.tensor_tensor(lo[:, k - 1, half(t)], f["hf"][:, (k - 1) % 2, :], hi[:, k - 1, half(t)],
                                              ALU.subtract).then_inc(h_ready, 1)

            def add_out(pair, n, x):
                for o in range(16):
                    if o % 8 == 7:
                        dve.wait_ge(block_done, n + o // 8 + 1)
                    else:
                        dve.wait_ge(o_full, pair * 14 + (7 * (o // 8) + o % 8 + 1))
                    dve.wait_ge(x_added, pair * 16 + (o + 1))
                    xs = x[:, o // 2, half(o % 2)]
                    dve.scalar_tensor_tensor(xs, bank[4 + o % 4], 0.5, xs, ALU.mult, ALU.add).then_inc(x_added, 1)

            def split_u(pair, which, src, f_hi, f_lo):
                for t in range(2):
                    dve.wait_ge(u_hi_ready, pair * 4 + (2 * which + t + 1))
                    dve.tensor_tensor(f_lo[:, which, half(t)], src[:, which, t, :] if len(src.shape) == 4 else src[:, which, half(t)],
                                      f_hi[:, which, half(t)], ALU.subtract).then_inc(u_ready, 1)

            def ffn(r, x, f, b0, pairs):
                def product(tile, which, n):
                    for t in range(2):
                        if t == 0:
                            dve.wait_ge(b_full, tile + (22 * r + 1))
                        else:
                            dve.wait_ge(block_done, n + 2)
                        dve.wait_ge(a_free, tile * 2 + (44 * r + t + 1))
                        dve.tensor_tensor(f["uf"][:, which, t, :], f["sa"][:, t, :], bank[2 + t], ALU.mult).then_inc(b_free, 1)

                for tile in range(2):
                    product(tile, tile, b0 + 2 * tile)
                    split_u(pairs, tile, f["uf"], f["u_hi"], f["u_lo"])
                with dve.Fori(1, NPAIR) as c:
                    n = c * 6 + (b0 - 2)
                    product(c * 2, 0, n)
                    add_out(c + (pairs - 1), n + 2, x)
                    split_u(c + pairs, 0, f["uf"], f["u_hi"], f["u_lo"])
                    product(c * 2 + 1, 1, n + 4)
                    split_u(c + pairs, 1, f["uf"], f["u_hi"], f["u_lo"])
                add_out(pairs + NPAIR - 1, b0 + 6 * NPAIR - 2, x)

            dve.wait_ge(cols_in, 16)
            bgate = cols[:, COLS["bgate"][0]:COLS["bgate"][0] + NG]
            dve.tensor_scalar(bgate, bgate, 0.5, None, ALU.mult).then_inc(consts_ready, 1)
            dve.wait_ge(mem_rms, 1)
            dve.reciprocal(f1["rs"][:, 0, 0:NMEM], f1["rs"][:, 0, 0:NMEM]).then_inc(mem_rstd, 1)
            dve.wait_ge(mem_rstd, 1)
            dve.wait_ge(mem_in, 16)
            for k in range(KD):
                dve.scalar_tensor_tensor(memx[:, k, :], memx[:, k, :], col("mem", k), f1["rs"][:, 0, 0:NMEM],
                                         ALU.mult, ALU.mult).then_inc(mem_h, 1)
            dve.wait_ge(mem_hi, 1)
            dve.tensor_tensor(mh_lo[:, :, :], memx[:, :, :], mh_hi[:, :, :], ALU.subtract).then_inc(mem_ready, 1)
            dve.wait_ge(x_in[0], 16)
            dve.wait_ge(x_in[1], 16)
            dve.sem_inc(x_added, 16)
            norm(0, x1, f1, h_hi, h_lo, "ffn1")
            ffn(0, x1, f1, B_FFN1, PAIRS["ffn1"])
            norm(1, x1, f1, h_hi, h_lo, "mix")
            mix1_dve(dve)
            mix2_dve(dve)
            merge_dve(dve, add_out, split_u)
            norm(2, x2, f2, h2_hi, h2_lo, "ffn2")
            ffn(1, x2, f2, B_FFN2, PAIRS["ffn2"])


def constants():
    c = np.zeros((P, NCONST), np.float32)
    i = np.arange(P)
    c[:, C_ID:C_ID + P] = np.eye(P)
    c[:, C_ONE:C_ONE + P] = 1.0
    c[:, C_BLK:C_BLK + P] = (i[:, None] // 64 == i[None, :] // 64)
    for o in (0, 64):
        for d in range(8):
            c[o + d + 8, C_PERM + o + d] = -1.0
            c[o + d, C_PERM + o + d + 8] = 1.0
    c[:, C_MASK:C_MASK + P] = (i[:, None] <= i[None, :])
    c[:, C_BLK2:C_BLK2 + 2] = (i[:, None] // 64 == np.arange(2)[None, :])
    s = np.zeros((MLH, 6 * P), np.float32)
    for h in range(MLH):
        s[h, h * P:(h + 1) * P] = 1.0
        s[h, (8 + h) * 64:(9 + h) * 64] = 1.0
    return c, s


def weight_stream(w):
    def feature(m, j=None):
        m = m if j is None else m[:, j * P:(j + 1) * P]
        return m.reshape(KD, P, P).transpose(1, 0, 2).reshape(P, 1024)

    def outs(m, pair):
        v = m[2 * pair * P:(2 * pair + 2) * P].reshape(2, P, 2, 4, P)
        return [v[:, :, b].transpose(1, 2, 0, 3).reshape(P, 1024) for b in range(2)]

    def ffn(w_in, w_out):
        blocks = []
        for c in range(NPAIR):
            ab = [feature(w_in, o + 2 * c + i) for i in range(2) for o in (0, NF)]
            blocks += ab[:2] + (outs(w_out, c - 1) if c else []) + ab[2:]
        return blocks + outs(w_out, NPAIR - 1)

    at = np.cumsum((0, 256, 256, 512, 4, 4, 512, 512, 128, 128, 512, 3072))
    mq, mk, mv, mi, mf, mo, sq, sk, sv, cq, gates = (w["w_in"][:, a:b] for a, b in zip(at[:-1], at[1:]))
    order = [h for i in range(4) for h in (i, i + 4)]
    sq = sq.reshape(D, SWH, 64)[:, order].reshape(D, 512)
    br_sw = w["w_br_sw"].reshape(SWH, 64, D)[order].reshape(512, D)
    pre = np.zeros((D, P), np.float32)
    pre[:, 0:4], pre[:, 32:36] = mi, mf
    gate = [feature(gates, g) for g in range(NG)]
    blocks = ffn(w["ffn1_w_in"], w["ffn1_w_out"])
    blocks += [feature(cq, i) for i in range(4)] + [feature(sq, i) for i in range(4)] + [feature(sk), feature(sv)]
    blocks += [feature(w["mx_w_kv"], i) for i in range(8)]
    blocks += gate[:16]
    blocks += [feature(mq, i) for i in range(2)] + [feature(mk, i) for i in range(2)] + [feature(pre)]
    blocks += [feature(mv, i) for i in range(4)] + [feature(mo, i) for i in range(4)]
    blocks += gate[16:]
    branch = {"a": w["w_br_ml"], "b": br_sw, "c": w["w_br_mx"]}

    def half_block(b, m):
        return branch[b][:, m * P:(m + 1) * P].reshape(4, P, P).transpose(1, 0, 2).reshape(P, 512)

    for p in range(4):
        m0, m1 = 2 * p, 2 * p + 1
        b = [np.concatenate([half_block(*x), half_block(*y)], axis=1) for x, y in (
            (("c", m0), ("b", m0)), (("a", m0), ("a", m1)), (("c", m1), ("b", m1)))]
        blocks += b[:2] + (outs(w["w_out"], p - 1) if p else []) + b[2:]
    blocks += outs(w["w_out"], 3)
    blocks += ffn(w["ffn2_w_in"], w["ffn2_w_out"])
    assert len(blocks) == NB
    return np.stack(blocks)


def columns(v):
    c = np.zeros((P, NCOL), np.float32)

    def put(name, x):
        c[:, COLS[name][0]:COLS[name][0] + COLS[name][1]] = x

    for name, key in (("ffn1", "ffn1_norm"), ("mix", "mix_norm"), ("ffn2", "ffn2_norm"), ("mem", "mem_norm"),
                      ("bgate", "b_gate"), ("mlnorm", "ml_out_norm"), ("mxq", "mx_q_norm"), ("mxk", "mx_k_norm")):
        put(name, v[key].reshape(-1, P).T)
    for name, key in (("convq", "ml_conv_q"), ("convk", "ml_conv_k")):
        put(name, v[key].reshape(4, 2, P).transpose(2, 1, 0).reshape(P, 8))
    for name, key in (("swq", "sw_q_norm"), ("swk", "sw_k_norm")):
        put(name, np.concatenate([v[key], v[key]])[:, None])
    put("sink", np.broadcast_to(v["sw_sinks"][None, :], (P, SWH)))
    c[0:4, COLS["bi"][0]] = v["ml_b_i"]
    c[32:36, COLS["bf"][0]] = v["ml_b_f"]
    half = 8
    inv = np.float32(500000.0) ** (-np.arange(half, dtype=np.float32) * np.float32(2.0 / 16))
    for o in (0, 8, 64, 72):
        c[o:o + 8, COLS["inv"][0]] = inv
    c[:, COLS["eps"][0]] = EPS
    return c


def kernel(**inputs):
    import concourse.bacc as bacc
    from concourse.bass_utils import run_bass_kernel_spmd

    v = {k: np.asarray(a) for k, a in inputs.items()}
    one = {k: a[0] for k, a in v.items()}
    cst, sel = constants()
    arrays = {
        "xT": np.ascontiguousarray(one["x"].T.reshape(KD, P, T).transpose(1, 0, 2)),
        "memT": np.ascontiguousarray(one["mem"].T.reshape(KD, P, NMEM).transpose(1, 0, 2)),
        "pos": np.ascontiguousarray(np.broadcast_to(one["positions"][None, :], (P, T))),
        "weights": weight_stream(one),
        "columns": columns(one),
        "constants": cst,
        "selectors": sel,
    }
    nc = bacc.Bacc("TRN2", target_bir_lowering=False, num_devices=1)
    args = [nc.dram_tensor("in_" + k, a.shape, mybir.dt.from_np(a.dtype), kind="ExternalInput").ap()
            for k, a in arrays.items()]
    out = nc.dram_tensor("out_x", (KD, P, T), F32, kind="ExternalOutput").ap()
    build(nc, *args, out)
    r = run_bass_kernel_spmd(nc, [{"in_" + k: a for k, a in arrays.items()}], core_ids=[0])
    y = r.results[0]["out_x"]
    return np.ascontiguousarray(y.reshape(D, T).T)[None]
```

```python
import math
from contextlib import ExitStack

import numpy as np

import concourse.bass as bass
from concourse import mybir

F32 = mybir.dt.float32
F32R = mybir.dt.float32r
I32 = mybir.dt.int32
ALU = mybir.AluOpType
ACT = mybir.ActivationFunctionType
AX = mybir.AxisListType

P = 128
D = 1024
KD = D // P
T = 1024
HT = T // 2
FF = 2816
NF = FF // P
NPAIR = NF // 2
NMEM = 256
NG = 24
NT = T // P
MLH = 4
SWH = 8
MXH = 4
EPS = 1e-6
NEG = -1e30
WIN = 192

B_FFN1 = 0
B_MIX1 = B_FFN1 + 6 * NPAIR
N_MIX1 = 18
B_GATE1 = B_MIX1 + N_MIX1
GATES1 = 12
B_MIX2 = B_GATE1 + GATES1
N_MIX2 = 13
B_GATE2 = B_MIX2 + N_MIX2
B_MERGE = B_GATE2 + NG - GATES1
B_FFN2 = B_MERGE + 20
NB = B_FFN2 + 6 * NPAIR

COLS = {}
for _n, _w in (("ffn1", KD), ("mix", KD), ("ffn2", KD), ("mem", KD), ("bgate", NG), ("convq", 8),
               ("convk", 8), ("mlnorm", 4), ("swq", 1), ("swk", 1), ("mxq", 1), ("mxk", 1),
               ("sink", SWH), ("bi", 1), ("bf", 1), ("inv", 1), ("eps", 1)):
    COLS[_n] = (sum(w for _, w in COLS.values()), _w)
NCOL = sum(w for _, w in COLS.values())

C_ID, C_ONE, C_BLK, C_PERM, C_MASK = (P * i for i in range(5))
C_BLK2 = 5 * P
NCONST = C_BLK2 + 2

PI2_A = 6.28125
PI2_B = float(np.float32(np.round((2 * np.pi - PI2_A) * 2.0**21) / 2.0**21))
PI2_C = float(np.float32(2 * np.pi - PI2_A - PI2_B))
ROUND = 12582912.0
PI_IN = 3.1415925


def build(nc, xT, memT, pos, wts, cols_d, const_d, sel_d, out):
    with ExitStack() as top:
        sem_names = []

        def sem(name):
            sem_names.append(name)
            return top.enter_context(nc.semaphore(name))

        def era(side):
            st = ExitStack()

            def sb(name, shape, dt=F32):
                return st.enter_context(nc.sbuf_tensor(name, shape, dt, side=side))
            return st, sb

        gate_scr = nc.dram_tensor("gate_scr", (NG, P, T), F32, kind="Internal").ap()
        x_scr = nc.dram_tensor("x_scr", (P, KD, T), F32, kind="Internal").ap()

        base, sb = era("left")
        raw = [sb(f"raw{i}", [P, 1024]) for i in range(2)]
        whi = [sb(f"whi{i}", [P, 1024], F32R) for i in range(2)]
        wlo = [sb(f"wlo{i}", [P, 1024], F32R) for i in range(2)]
        cst = sb("cst", [P, NCONST])
        cols = sb("cols", [P, NCOL])
        norm_s = sb("norm_s", [P, 2, 4])

        def col(name, i=0, p0=0, p1=P):
            c = COLS[name][0] + i
            return cols[p0:p1, c:c + 1]

        ident = cst[:, C_ID:C_ID + P]
        ones = cst[:, C_ONE:C_ONE + P]
        blk64 = cst[:, C_BLK:C_BLK + P]
        perm = cst[:, C_PERM:C_PERM + P]
        mask = cst[:, C_MASK:C_MASK + P]
        blk2 = cst[:, C_BLK2:C_BLK2 + 2]

        eh, sb = era("left")
        h_hi = sb("h_hi", [P, KD, T], F32R)
        h_lo = sb("h_lo", [P, KD, T], F32R)
        em_, sb = era("left")
        mh_hi = sb("mh_hi", [P, KD, NMEM], F32R)
        mh_lo = sb("mh_lo", [P, KD, NMEM], F32R)

        def ffn_buffers(tag, sb):
            return dict(
                u_hi=sb("u_hi" + tag, [P, 2, T], F32R), u_lo=sb("u_lo" + tag, [P, 2, T], F32R),
                sa=sb("sa" + tag, [P, 2, HT]), uf=sb("uf" + tag, [P, 2, 2, HT]),
                sq=sb("sq" + tag, [P, 4, HT]), hf=sb("hf" + tag, [P, 2, HT]), rs=sb("rs" + tag, [P, 2, HT]))

        e1, sb = era("right")
        x1 = sb("x1", [P, KD, T])
        f1 = ffn_buffers("1", sb)
        memx = sb("memx", [P, KD, NMEM])
        e1.close()

        ey, sb = era("right")
        y_c = sb("y_c", [P, 4, T])
        y_b = sb("y_b", [P, 4, T])
        m1, sb = era("right")
        kv_all = sb("kv_all", [P, 2, 64 + T])
        rope_c = sb("rope_c", [P, T])
        rope_s = sb("rope_s", [P, T])
        ck = sb("ck", [P, MXH, NMEM])
        cv = sb("cv", [P, 2, 4 * P])
        rq = sb("rq", [P, NT, 12])
        p_mx = sb("p_mx", [P, MXH, NMEM])
        pt_mx = sb("pt_mx", [P, 2 * MXH, P])
        p_sw = sb("p_sw", [P, SWH, P])
        pt_sw = sb("pt_sw", [P, SWH, P])
        q_mx = sb("q_mx", [P, 4, P])
        q_sw = sb("q_sw", [P, 4, P])
        q_rot = sb("q_rot", [P, 4, P])
        q_tmp = sb("q_tmp", [P, 4, P])
        kv_st = sb("kv_st", [P, 2, WIN])
        v_win = sb("v_win", [P, 2, P])
        gst1 = [sb(f"gst1_{i}", [P, HT]) for i in range(2)]
        gains = sb("gains", [P, 2])
        rq_st = sb("rq_st", [P, 12])
        m_mx, nb_mx, sum_mx, ri_mx = (sb(n, [P, MXH]) for n in ("m_mx", "nb_mx", "sum_mx", "ri_mx"))
        m_sw, nb_sw, sum_sw, ri_sw, es_in, es = (sb(n, [P, SWH]) for n in ("m_sw", "nb_sw", "sum_sw", "ri_sw", "es_in", "es"))
        negrow = sb("negrow", [1, 2 * P])
        pos_i = pt_mx[:, :, :].rearrange("p a b -> p (a b)").bitcast(I32)
        m1.close()
        em_.close()

        m2, sb = era("right")
        y_a = sb("y_a", [P, 4, T])
        m2b, sb = era("right")
        ml_q = sb("ml_q", [P, 2, T])
        ml_k = sb("ml_k", [P, 2, T])
        ml_v = sb("ml_v", [P, 4, T])
        rows = sb("rows", [68, T])
        cwt = sb("cwt", [P, NT, 8])
        m2d, sb = era("right")
        cpad = [sb(f"cpad{i}", [P, 3 + T]) for i in range(2)]
        cacc = sb("cacc", [P, T])
        cw = sb("cw", [36, T])
        reset = sb("reset", [4, T])
        mst = sb("mst", [4, NT])
        m2d.close()
        m2e, sb = era("right")
        sel = sb("sel", [4, 6 * P])
        ks = sb("ks", [P, MLH, P])
        ktok = sb("ktok", [P, MLH, 64])
        vs = sb("vs", [P, 4, P])
        qd = sb("qd", [P, 2, P])
        rws = sb("rws", [4, 3, P])
        dec = sb("dec", [P, 2])
        cw_st = sb("cw_st", [P, 8])
        ml_e = sb("ml_e", [P, 4, P])
        em_sb = sb("em_sb", [P, 4 * P])
        t_sb = sb("t_sb", [P, 4 * P])
        wvx = sb("wvx", [P, 4, 2 * P])
        num_sb = sb("num_sb", [P, 4 * P])
        c_st = sb("c_st", [P, MLH, 2 * P])
        gst2 = [sb(f"gst2_{i}", [P, HT]) for i in range(2)]
        m2e.close()
        m2b.close()
        eh.close()

        ex, sb = era("left")
        x2 = sb("x2", [P, KD, T])
        eyh, sb = era("left")
        yh = {b: sb(f"yh_{b}", [P, 4, T], F32R) for b in "cba"}
        yl = {b: sb(f"yl_{b}", [P, 4, T], F32R) for b in "cba"}
        m2.close()
        ey.close()
        eg, sb = era("right")
        gt = {g: sb(f"gt_{g}", [P, T]) for g in ("c0", "b0", "a0", "a1", "c1", "b1")}
        mg_hi = sb("mg_hi", [P, 2, T], F32R)
        mg_lo = sb("mg_lo", [P, 2, T], F32R)
        mg = sb("mg", [P, 2, T])
        mtmp = sb("mtmp", [P, HT])
        eg.close()
        eyh.close()
        e2, sb = era("left")
        h2_hi = sb("h2_hi", [P, KD, T], F32R)
        h2_lo = sb("h2_lo", [P, KD, T], F32R)
        f2 = ffn_buffers("2", sb)
        e2.close()
        ex.close()

        bank = [top.enter_context(nc.psum_tensor(f"bank{i}", [P, HT], F32)) for i in range(4)]
        wide = [top.enter_context(nc.psum_tensor(f"wide{i}", [P, 2 * HT], F32)) for i in range(2)]
        bank += [wide[i // 2][:, (i % 2) * HT:(i % 2 + 1) * HT] for i in range(4)]
        bank = [b if i >= 4 else b[:, :] for i, b in enumerate(bank)]

        raw_loaded = [sem(f"raw_loaded{i}") for i in range(2)]
        w_hi_ready = sem("w_hi_ready")
        split_ready = sem("split_ready")
        block_done = sem("block_done")
        const_in, cols_in, mem_in, pos_in, sel_in = (sem(n) for n in ("const_in", "cols_in", "mem_in", "pos_in", "sel_in"))
        x_in = [sem(f"x_in{i}") for i in range(KD // 2)]
        x_saved, x_back, out_done = sem("x_saved"), sem("x_back"), sem("out_done")
        gate_stored = [sem(f"gate_stored{i}") for i in range(2)]
        gt_in = {g: sem(f"gt_in_{g}") for g in gt}
        mem_sq, mem_acc, mem_sum, mem_rms, mem_rstd, mem_h, mem_hi, mem_ready = (
            sem(n) for n in ("mem_sq", "mem_acc", "mem_sum", "mem_rms", "mem_rstd", "mem_h", "mem_hi", "mem_ready"))
        sq_ready, sq_used, acc_ready, sum_ready, rms_ready, rinv_ready, diag_ready, rs_ready, hf_ready, h_hi_ready, h_ready = (
            sem(n) for n in ("sq_ready", "sq_used", "acc_ready", "sum_ready", "rms_ready", "rinv_ready", "diag_ready",
                             "rs_ready", "hf_ready", "h_hi_ready", "h_ready"))
        a_full, a_free, b_full, b_free = sem("a_full"), sem("a_free"), sem("b_full"), sem("b_free")
        u_hi_ready, u_ready, o_full, x_added = sem("u_hi_ready"), sem("u_ready"), sem("o_full"), sem("x_added")

        block = top.enter_context(nc.Block())

        def half(t):
            return slice(t * HT, (t + 1) * HT)

        PAIRS = {"ffn1": 0, "merge": NPAIR, "ffn2": NPAIR + 4}

        BY_FEATURE = [(k, t) for k in range(KD) for t in range(2)]
        BY_HALF = [(k, t) for t in range(2) for k in range(KD)]
        NORM_ORDER = [BY_FEATURE, BY_HALF, BY_HALF]
        norm_bank = [bank[3], bank[4]]

        def out_signal(order, n, pair, o):
            last0 = max(i for i, (k, _) in enumerate(order) if k < KD // 2)
            if o in (last0, 15):
                return block_done, n + (2 if o == 15 else 1)
            return o_full, pair * 14 + (o + 1 - (o > last0))

        def square_slot(i, k, t):
            return 14 * i + [kt for kt in NORM_ORDER[i] if kt[0]].index((k, t))

        def done(j):
            return j + 2

        def prev(j):
            return j + 1

        def lsem(name):
            return sem(name)

        p_full, p_free, psq_ready, stats_done = (sem(n) for n in ("p_full", "p_free", "psq_ready", "stats_done"))
        consts_ready, own = sem("consts_ready"), sem("dve_chain")
        sin_arg, rope_ready = sem("sin_arg"), sem("rope_ready")
        rq_rms, rq_ready = sem("rq_rms"), sem("rq_ready")
        k_sum, k_rms, k_rstd, k_norm, k_swap, k_ready = (sem(n) for n in ("k_sum", "k_rms", "k_rstd", "k_norm", "k_swap", "k_ready"))
        c_sum, c_rms, c_rstd, ck_ready, cv_turned, cv_ready = (sem(n) for n in ("c_sum", "c_rms", "c_rstd", "ck_ready", "cv_turned", "cv_ready"))
        gate_full, gate_done = sem("gate_full"), sem("gate_done")
        (q_mx_ready, q_sw_ready, kv_ready, rq_tile, s1_done, mx_max, mx_bias, rope_t, rope_x, q_rot_ready, mx_exp,
         mx_rinv, mx_p_ready, s2_done, sw_max, sw_bias, sw_exp, sw_rinv, sw_p_ready, neg_done, v_win_ready, mx_turned,
         mx_pt, sw_turned, sw_pt, mx_out, y_c_done, sw_out, y_b_done) = L1 = [lsem(n) for n in (
            "q_mx_ready", "q_sw_ready", "kv_ready", "rq_tile", "s1_done", "mx_max", "mx_bias", "rope_t", "rope_x",
            "q_rot_ready", "mx_exp", "mx_rinv", "mx_p_ready", "s2_done", "sw_max", "sw_bias", "sw_exp", "sw_rinv",
            "sw_p_ready", "neg_done", "v_win_ready", "mx_turned", "mx_pt", "sw_turned", "sw_pt", "mx_out", "y_c_done",
            "sw_out", "y_b_done")]
        sw_small = sem("sw_small")
        ml_small, row_init = sem("ml_small"), sem("row_init")
        y_split, yh_ready, m_full, m_prod, gated = (sem(n) for n in ("y_split", "yh_ready", "m_full", "m_prod", "gated"))
        waited = sem("waited")

        def apart(eng):
            eng.sem_inc(waited, 1)

        STEP = 4

        def gate_at(block0, gate0, i, u, k):
            b, t = divmod(3 * u + k, 2)
            return i * 6 + (block0 + b), (block0 + b) % 2, i * 6 + (gate0 + b), t

        def gate_group(pe, feature_group, n, slot, g, t):
            if t == 0:
                pe.wait_ge(split_ready, n + 1)
            pe.wait_ge(gate_done, g * 2 + (t + 1))
            mm = feature_group(bank[t], slot, h_hi, h_lo, half(t))
            mm.then_inc(block_done if t else gate_full, 1)

        def gate_tanh(act, n, _, g, t, gst):
            if t == 0:
                act.wait_ge(gate_full, g + 1)
            else:
                act.wait_ge(block_done, n + 1)
            act.wait_ge(gate_stored[t], g * 16 + 16)
            apart(act)
            act.activation(gst[t][:, :], bank[t], ACT.Tanh, bias=cols[:, bass.ds(g + COLS["bgate"][0], 1)],
                           scale=0.5).then_inc(gate_done, 1)
            act.wait_ge(gate_done, g * 2 + (t + 3))
            act.dma_start(gate_scr[bass.ds(g, 1), :, half(t)].rearrange("a p n -> p (a n)"), gst[t][:, :]
                          ).then_inc(gate_stored[t], 16)

        sqs = [p_sw[:, :, :].rearrange("p a b -> p (a b)"), pt_sw[:, :, :].rearrange("p a b -> p (a b)")]
        p_mxf = p_mx[:, :, :].rearrange("p a b -> p (a b)")
        pt_mxf = pt_mx[:, :, :].rearrange("p a b -> p (a b)")
        ckf = ck[:, :, :].rearrange("p a b -> p (a b)")
        w0, w1 = wide[0][:, :], wide[1][:, :]
        k_raw = kv_all[:, 0, 64:64 + T]

        def tile_of(ap, j):
            return ap[:, :, bass.ds(j * P, P)]

        def mix1_pe(pe, feature_group, first_blocks):
            def stats(f):
                pe.wait_ge(psq_ready, f + 1)
                rhs, c, w = (ones[:, 0:1], f, 1) if f < 4 else (blk2, 4 + 2 * (f - 4), 2)
                for t in range(NT):
                    mm = pe.matmul(bank[4][:, 12 * t + c:12 * t + c + w], sqs[f % 2][:, t * P:(t + 1) * P], rhs,
                                   start=True, stop=True)
                mm.then_inc(stats_done, 1)

            for f in range(18):
                n = B_MIX1 + f
                if f < 2:
                    if f == 0:
                        first_blocks(1, n, bank, (p_full, p_full), h_hi, h_lo)
                    else:
                        stats(0)
                    continue
                pe.wait_ge(split_ready, n + 1)
                if f < 10:
                    for t in range(2):
                        q = 2 * f + t
                        if q >= 4:
                            pe.wait_ge(p_free, q - 3)
                        mm = feature_group(bank[q % 4], n % 2, h_hi, h_lo, half(t))
                        mm.then_inc(block_done if t else p_full, 1)
                else:
                    q = 10 + f
                    pe.wait_ge(p_free, q - 3)
                    if f == 10:
                        pe.wait_ge(mem_ready, 1)
                    mm = feature_group(bank[q % 4][:, 0:NMEM], n % 2, mh_hi, mh_lo, slice(0, NMEM))
                    mm.then_inc(block_done, 1)
                if 1 <= f <= 8:
                    stats(f - 1)
                if f == 9:
                    pe.wait_ge(psq_ready, 9)
                    for t in range(2):
                        mm = pe.matmul(wide[1][:, half(t)], blk64, sqs[0][:, half(t)], start=True, stop=True)
                    mm.then_inc(k_sum, 1)
                if f == 15:
                    pe.wait_ge(k_norm, 1)
                    for t in range(2):
                        mm = pe.matmul(wide[1][:, half(t)], perm, kv_all[:, 0, 64 + t * HT:64 + (t + 1) * HT], start=True, stop=True)
                    mm.then_inc(k_swap, 1)
                if f == 17:
                    pe.wait_ge(psq_ready, 10)
                    pe.wait_ge(k_ready, 1)
                    for t in range(2):
                        mm = pe.matmul(wide[1][:, half(t)], ones, sqs[1][:, half(t)], start=True, stop=True)
                    mm.then_inc(c_sum, 1)
            pe.wait_ge(p_free, 28)
            pe.wait_ge(rq_rms, 2)
            for h in range(MXH):
                for kk in range(2):
                    mm = pe.transpose(wide[0][:, kk * 4 * P + h * P:kk * 4 * P + (h + 1) * P], p_mx[:, h, kk * P:(kk + 1) * P], ident)
            mm.then_inc(cv_turned, 1)
            pe.wait_ge(ck_ready, 1)
            pe.wait_ge(cv_ready, 1)

            for s in (s1_done, s2_done, mx_turned, sw_turned, mx_out, sw_out):
                pe.sem_inc(s, 1)
            with pe.Fori(0, NT // STEP) as i:
                for u in range(STEP):
                    j = i * STEP + u
                    pe.wait_ge(q_mx_ready, done(j))
                    pe.wait_ge(mx_pt, prev(j))
                    for h in range(MXH):
                        pe.matmul(w0[:, h * NMEM:(h + 1) * NMEM], q_mx[:, h, :], ck[:, h, :], start=True, stop=True)
                    pe.wait_ge(q_sw_ready, done(j))
                    pe.wait_ge(y_b_done, prev(j))
                    pe.matmul(bank[3], perm, q_sw[:, :, :].rearrange("p a b -> p (a b)"), start=True, stop=True)
                    pe.wait_ge(kv_ready, done(j))
                    pe.wait_ge(y_c_done, prev(j))
                    for w in range(2):
                        mm = pe.transpose(bank[2][:, w * P:(w + 1) * P], kv_st[:, 1, 64 * w:64 * w + P], ident)
                    mm.then_inc(s1_done, 1)
                    gate_group(pe, feature_group, *gate_at(B_GATE1, 0, i, u, 0))
                    pe.wait_ge(q_rot_ready, done(j))
                    pe.wait_ge(sw_pt, prev(j))
                    pe.wait_ge(neg_done, prev(j))
                    for g in range(2):
                        pe.matmul(w1[:, g * HT:(g + 1) * HT], negrow[0:1, 0:P],
                                  negrow[0:1, P:2 * P].unsqueeze(1).broadcast_to([1, 4, P]), start=True, stop=False,
                                  skip_group_check=True)
                        for c in range(4):
                            for w in range(2):
                                mm = pe.matmul(w1[64 * w:64 * w + 64, g * HT + c * P:g * HT + (c + 1) * P],
                                               q_rot[64 * g:64 * g + 64, c, 64 * w:64 * w + 64],
                                               kv_st[64 * g:64 * g + 64, 0, 64 * w:64 * w + P], start=False, stop=(c == 3 and w == 1),
                                               skip_group_check=True)
                    mm.then_inc(s2_done, 1)
                    gate_group(pe, feature_group, *gate_at(B_GATE1, 0, i, u, 1))
                    pe.wait_ge(mx_p_ready, done(j))
                    for h in range(MXH):
                        for kk in range(2):
                            mm = pe.transpose(w0[:, (2 * h + kk) * P:(2 * h + kk + 1) * P], p_mx[:, h, kk * P:(kk + 1) * P], ident)
                    mm.then_inc(mx_turned, 1)
                    pe.wait_ge(sw_p_ready, done(j))
                    for h in range(SWH):
                        mm = pe.transpose(w1[:, h * P:(h + 1) * P], p_sw[:, h, :], ident)
                    mm.then_inc(sw_turned, 1)
                    pe.wait_ge(mx_pt, done(j))
                    pe.wait_ge(v_win_ready, done(j))
                    for h in range(MXH):
                        for kk in range(2):
                            mm = pe.matmul(bank[2][:, h * P:(h + 1) * P], cv[:, kk, h * P:(h + 1) * P], pt_mx[:, 2 * h + kk, :],
                                           start=kk == 0, stop=kk == 1)
                    mm.then_inc(mx_out, 1)
                    gate_group(pe, feature_group, *gate_at(B_GATE1, 0, i, u, 2))
                    pe.wait_ge(sw_pt, done(j))
                    b3 = bank[3].rearrange("p (i c) -> p i c", i=4)
                    for g in range(2):
                        for w in range(2):
                            mm = pe.matmul(b3[64 * g:64 * g + 64, :, 64 * w:64 * w + 64], v_win[:, w, 64 * g:64 * g + 64],
                                           pt_sw[:, 4 * g:4 * g + 4, 64 * w:64 * w + 64], start=True, stop=True)
                    mm.then_inc(sw_out, 1)

        def mix1_act(act):
            act.wait_ge(x_saved, 16)
            act.wait_ge(h_ready, 32)
            act.dma_start(pos_i, pos).then_inc(pos_in, 16)
            for f in range(8):
                act.wait_ge(p_free, 2 * f + 2)
                if f >= 2:
                    act.wait_ge(stats_done, f - 1)
                act.activation(sqs[f % 2], (y_c if f < 4 else y_b)[:, f % 4, :], ACT.Square).then_inc(psq_ready, 1)
                if f == 3:
                    for i, table in enumerate((rope_s, rope_c)):
                        act.wait_ge(sin_arg, i + 1)
                        act.activation(table[:, :], table[:, :], ACT.Sin).then_inc(rope_ready, 1)
            act.wait_ge(p_free, 18)
            act.wait_ge(stats_done, 7)
            act.activation(sqs[0], k_raw, ACT.Square).then_inc(psq_ready, 1)
            act.wait_ge(stats_done, 8)
            st = bank[4][:, 0:12 * NT].rearrange("p (t c) -> p t c", c=12)
            act.activation(rq[:, :, 0:4], st[:, :, 0:4], ACT.Sqrt, bias=col("eps"), scale=1.0 / P).then_inc(rq_rms, 1)
            act.activation(rq[:, :, 4:12], st[:, :, 4:12], ACT.Sqrt, bias=col("eps"), scale=1.0 / 64).then_inc(rq_rms, 1)
            act.wait_ge(k_sum, 1)
            act.wait_ge(sin_arg, 2)
            act.activation(pt_mxf, w1, ACT.Sqrt, bias=col("eps"), scale=1.0 / 64).then_inc(k_rms, 1)
            act.wait_ge(p_free, 24)
            act.activation(sqs[1], ckf, ACT.Square).then_inc(psq_ready, 1)
            act.wait_ge(c_sum, 1)
            act.activation(sqs[0], w1, ACT.Sqrt, bias=col("eps"), scale=1.0 / P).then_inc(c_rms, 1)
            act.wait_ge(cv_turned, 1)
            act.activation(cv[:, :, :].rearrange("p a b -> p (a b)"), w0, ACT.Copy).then_inc(cv_ready, 1)
            act.wait_ge(c_rstd, 1)
            act.wait_ge(ck_ready, 1)
            for s in (mx_exp, sw_exp, v_win_ready, mx_pt, sw_pt, y_c_done, y_b_done):
                act.sem_inc(s, 1)
            act.sem_inc(gate_done, 2)
            for t in range(2):
                act.sem_inc(gate_stored[t], 16)
            with act.Fori(0, NT // STEP) as i:
                for u in range(STEP):
                    j = i * STEP + u
                    act.wait_ge(mx_bias, done(j))
                    act.wait_ge(mx_turned, prev(j))
                    for h in range(MXH):
                        ins = act.activation(p_mx[:, h, :], w0[:, h * NMEM:(h + 1) * NMEM], ACT.Exp, bias=nb_mx[:, h:h + 1],
                                             scale=rq_st[:, h:h + 1], accum_out=sum_mx[:, h:h + 1])
                    ins.then_inc(mx_exp, 1)
                    act.wait_ge(sw_out, prev(j))
                    act.activation(v_win[:, :, :].rearrange("p a b -> p (a b)"), bank[2][:, 0:2 * P], ACT.Copy).then_inc(v_win_ready, 1)
                    gate_tanh(act, *gate_at(B_GATE1, 0, i, u, 0), gst1)
                    act.wait_ge(sw_bias, done(j))
                    act.wait_ge(sw_turned, prev(j))
                    act.activation(es[:, :], es_in[:, :], ACT.Exp)
                    for h in range(SWH):
                        c = 4 + 2 * (h % 4) + h // 4
                        ins = act.activation(p_sw[:, h, :], w1[:, h * P:(h + 1) * P], ACT.Exp, bias=nb_sw[:, h:h + 1],
                                             scale=rq_st[:, c:c + 1], accum_out=sum_sw[:, h:h + 1])
                    ins.then_inc(sw_exp, 1)
                    gate_tanh(act, *gate_at(B_GATE1, 0, i, u, 1), gst1)
                    act.wait_ge(mx_turned, done(j))
                    act.wait_ge(mx_out, prev(j))
                    act.activation(pt_mxf, w0, ACT.Copy).then_inc(mx_pt, 1)
                    act.wait_ge(sw_turned, done(j))
                    act.wait_ge(sw_out, prev(j))
                    act.activation(sqs[1], w1, ACT.Copy).then_inc(sw_pt, 1)
                    act.wait_ge(mx_out, done(j))
                    apart(act)
                    act.activation(tile_of(y_c, j), bank[2].rearrange("p (a b) -> p a b", a=4), ACT.Copy).then_inc(y_c_done, 1)
                    gate_tanh(act, *gate_at(B_GATE1, 0, i, u, 2), gst1)
                    act.wait_ge(sw_out, done(j))
                    apart(act)
                    act.activation(tile_of(y_b, j), bank[3].rearrange("p (a b) -> p a b", a=4), ACT.Copy).then_inc(y_b_done, 1)

        def mix1_dve(dve):
            step = [0]

            def chain(ins):
                ins.then_inc(own, 1)
                step[0] += 1
                dve.wait_ge(own, step[0])

            def evac(f, dst, t):
                if f < 10:
                    q, width = 2 * f + t, HT
                    if t == 0:
                        dve.wait_ge(p_full, f + 1)
                    else:
                        dve.wait_ge(block_done, B_MIX1 + f + 1)
                else:
                    q, width = 10 + f, NMEM
                    dve.wait_ge(block_done, B_MIX1 + f + 1)
                dve.tensor_copy(dst, bank[q % 4][:, 0:width]).then_inc(p_free, 1)

            def angles():
                dve.wait_ge(pos_in, 16)
                chain(dve.tensor_copy(rope_c[:, :], pos_i))
                chain(dve.tensor_scalar(p_mxf, rope_c[:, :], col("inv"), None, ALU.mult))
                for table, turn in ((rope_s, 0.0), (rope_c, 0.25)):
                    chain(dve.tensor_scalar(pt_mxf, p_mxf, 1.0 / (2 * math.pi), turn, ALU.mult, ALU.add))
                    chain(dve.tensor_scalar(pt_mxf, pt_mxf, ROUND, ROUND, ALU.add, ALU.subtract))
                    src = p_mxf
                    for part in (PI2_A, PI2_B, PI2_C):
                        chain(dve.scalar_tensor_tensor(table[:, :], pt_mxf, -part, src, ALU.mult, ALU.add))
                        src = table[:, :]
                    chain(dve.tensor_scalar(table[:, :], table[:, :], 2 * math.pi * turn, PI_IN, ALU.add, ALU.min))
                    dve.tensor_scalar(table[:, :], table[:, :], -PI_IN, None, ALU.max).then_inc(sin_arg, 1)
                    dve.wait_ge(sin_arg, 1 if turn == 0.0 else 2)

            dve.wait_ge(x_saved, 16)
            chain(dve.memset(kv_all[:, :, 0:64], 0.0))
            chain(dve.memset(negrow[:, :], 0.0))
            chain(dve.memset(negrow[0:1, 0:64], 1.0))
            chain(dve.memset(negrow[0:1, P:P + 64], NEG))
            chain(dve.tensor_scalar(gains[:, 0:1], col("swq"), 64 ** -0.5, None, ALU.mult))
            chain(dve.scalar_tensor_tensor(gains[:, 1:2], col("mxq"), float(P) ** -0.5, col("mxk"), ALU.mult, ALU.mult))
            for f in range(10):
                for t in range(2):
                    dst = (y_c[:, f % 4, half(t)] if f < 4 else y_b[:, f % 4, half(t)] if f < 8
                           else kv_all[:, f - 8, 64 + t * HT:64 + (t + 1) * HT])
                    evac(f, dst, t)
                if f == 0:
                    angles()
            for f in range(10, 14):
                evac(f, ck[:, f - 10, :], 0)
            dve.wait_ge(k_rms, 1)
            dve.reciprocal(pt_mxf, pt_mxf).then_inc(k_rstd, 1)
            dve.wait_ge(k_rstd, 1)
            dve.scalar_tensor_tensor(k_raw, k_raw, col("swk"), pt_mxf, ALU.mult, ALU.mult).then_inc(k_norm, 1)
            dve.wait_ge(rq_rms, 2)
            dve.reciprocal(rq[:, :, :], rq[:, :, :]).then_inc(rq_ready, 1)
            for f in range(14, 16):
                evac(f, p_mx[:, f - 14, :], 0)
            dve.wait_ge(k_swap, 1)
            dve.wait_ge(rope_ready, 2)
            dve.wait_ge(k_norm, 1)
            chain(dve.tensor_tensor(pt_mxf, w1, rope_s[:, :], ALU.mult))
            chain(dve.tensor_tensor(k_raw, k_raw, rope_c[:, :], ALU.mult))
            dve.tensor_tensor(k_raw, k_raw, pt_mxf, ALU.add).then_inc(k_ready, 1)
            dve.wait_ge(k_ready, 1)
            for f in range(16, 18):
                evac(f, p_mx[:, f - 14, :], 0)
            dve.wait_ge(c_rms, 1)
            dve.reciprocal(sqs[0], sqs[0]).then_inc(c_rstd, 1)
            dve.wait_ge(c_rstd, 1)
            dve.scalar_tensor_tensor(ckf, ckf, gains[:, 1:2], sqs[0], ALU.mult, ALU.mult).then_inc(ck_ready, 1)
            dve.wait_ge(rq_ready, 1)

            for s in (q_mx_ready, q_sw_ready, kv_ready, rq_tile, mx_max, mx_bias, rope_t, rope_x, q_rot_ready, mx_rinv,
                      mx_p_ready, sw_max, sw_bias, sw_rinv, sw_p_ready, neg_done):
                dve.sem_inc(s, 1)
            rqt = rq_st[:, 4:12].rearrange("p (i g) -> p g i", g=2)
            with dve.Fori(0, NT // STEP) as i:
                for u in range(STEP):
                    j = i * STEP + u
                    dve.wait_ge(s1_done, prev(j))
                    dve.tensor_copy(q_mx[:, :, :], tile_of(y_c, j)).then_inc(q_mx_ready, 1)
                    dve.wait_ge(q_rot_ready, prev(j))
                    dve.tensor_scalar(q_sw[:, :, :], tile_of(y_b, j), gains[:, 0:1], None, ALU.mult).then_inc(q_sw_ready, 1)
                    dve.wait_ge(s2_done, prev(j))
                    dve.tensor_copy(kv_st[:, :, :], kv_all[:, :, bass.ds(j * P, WIN)]).then_inc(kv_ready, 1)
                    dve.wait_ge(sw_exp, prev(j))
                    dve.tensor_copy(rq_st[:, :], rq[:, bass.ds(j, 1), :].rearrange("p a b -> p (a b)")).then_inc(rq_tile, 1)
                    dve.wait_ge(s1_done, done(j))
                    dve.tensor_reduce(m_mx[:, :], w0.rearrange("p (h k) -> p h k", h=MXH), AX.X, ALU.max).then_inc(mx_max, 1)
                    dve.wait_ge(mx_max, done(j))
                    dve.wait_ge(rq_tile, done(j))
                    dve.scalar_tensor_tensor(nb_mx[:, :], m_mx[:, :], -1.0, rq_st[:, 0:4], ALU.mult, ALU.mult).then_inc(mx_bias, 1)
                    dve.tensor_tensor(q_tmp[:, :, :], bank[3].rearrange("p (a b) -> p a b", a=4),
                                      rope_s[:, bass.ds(j * P, P)].unsqueeze(1).broadcast_to([P, 4, P]), ALU.mult).then_inc(rope_t, 1)
                    dve.wait_ge(q_sw_ready, done(j))
                    dve.tensor_tensor(q_rot[:, :, :], q_sw[:, :, :],
                                      rope_c[:, bass.ds(j * P, P)].unsqueeze(1).broadcast_to([P, 4, P]), ALU.mult).then_inc(rope_x, 1)
                    dve.wait_ge(rope_t, done(j))
                    dve.wait_ge(rope_x, done(j))
                    dve.tensor_tensor(q_rot[:, :, :], q_rot[:, :, :], q_tmp[:, :, :], ALU.add).then_inc(q_rot_ready, 1)
                    dve.wait_ge(mx_exp, done(j))
                    dve.reciprocal(ri_mx[:, :], sum_mx[:, :]).then_inc(mx_rinv, 1)
                    dve.wait_ge(mx_rinv, done(j))
                    dve.tensor_tensor(p_mx[:, :, :], p_mx[:, :, :], ri_mx[:, :].unsqueeze(2).broadcast_to([P, MXH, NMEM]),
                                      ALU.mult).then_inc(mx_p_ready, 1)
                    dve.wait_ge(s2_done, done(j))
                    dve.memset(negrow[0:1, P:P + 64], 0.0).then_inc(neg_done, 1)
                    dve.tensor_reduce(m_sw[:, :], w1.rearrange("p (h k) -> p h k", h=SWH), AX.X, ALU.max).then_inc(sw_max, 1)
                    dve.wait_ge(sw_max, done(j))
                    dve.tensor_tensor(m_sw[:, :].rearrange("p (g i) -> p g i", g=2), m_sw[:, :].rearrange("p (g i) -> p g i", g=2),
                                      rqt, ALU.mult).then_inc(sw_small, 1)
                    dve.wait_ge(sw_small, j * 4 + 1)
                    sink = cols[:, COLS["sink"][0]:COLS["sink"][0] + SWH]
                    dve.tensor_tensor(m_sw[:, :], m_sw[:, :], sink, ALU.max).then_inc(sw_small, 1)
                    dve.wait_ge(sw_small, j * 4 + 2)
                    dve.tensor_scalar(nb_sw[:, :], m_sw[:, :], -1.0, None, ALU.mult).then_inc(sw_small, 1)
                    dve.tensor_tensor(es_in[:, :], sink, m_sw[:, :], ALU.subtract).then_inc(sw_bias, 1)
                    dve.wait_ge(sw_exp, done(j))
                    dve.tensor_tensor(sum_sw[:, :], sum_sw[:, :], es[:, :], ALU.add).then_inc(sw_small, 1)
                    dve.wait_ge(sw_small, j * 4 + 4)
                    dve.reciprocal(ri_sw[:, :], sum_sw[:, :]).then_inc(sw_rinv, 1)
                    dve.wait_ge(sw_rinv, done(j))
                    dve.tensor_tensor(p_sw[:, :, :], p_sw[:, :, :], ri_sw[:, :].unsqueeze(2).broadcast_to([P, SWH, P]),
                                      ALU.mult).then_inc(sw_p_ready, 1)

        cw_turned, cwt_ready = sem("cw_turned"), sem("cwt_ready")
        o_free, conv_step, ml_silu, q_scaled, zi_ready, zabs, row_ln, row_step, row_arg, row_exp, y_a_gain = (sem(n) for n in (
            "o_free", "conv_step", "ml_silu", "q_scaled", "zi_ready", "zabs", "row_ln", "row_step", "row_arg", "row_exp",
            "y_a_gain"))
        (ml_staged, v_staged, b_rows, b_kqv, qd_ready, e_arg, e_exp, e_masked, sc_ready, em_copied, kv_tok, wv_done,
         numden, c_upd, num_copied, den_abs, num_sq, c_new, dn_ready, d2_ready, ms_done, t_ready, t_ok, t_root,
         t_inv, y_norm, y_a_done) = [lsem(n) for n in (
            "ml_staged", "v_staged", "b_rows", "b_kqv", "qd_ready", "e_arg", "e_exp", "e_masked", "sc_ready", "em_copied",
            "kv_tok", "wv_done", "numden", "c_upd", "num_copied", "den_abs", "num_sq", "c_new", "dn_ready", "d2_ready",
            "ms_done", "t_ready", "t_ok", "t_root", "t_inv", "y_norm", "y_a_done")]

        dabs = wvx[:, 0:2, :].rearrange("p a b -> p (a b)")
        sqn = wvx[:, 2:4, :].rearrange("p a b -> p (a b)")
        zrow, irow, lrow, mrow = cpad[0][0:4, 0:T], cpad[1][0:4, 0:T], cacc[0:4, :], reset[:, :]

        def by_chunk(ap):
            return ap.rearrange("p (c t) -> p c t", t=P)

        def mix2_pe(pe, feature_group):
            pe.wait_ge(gate_done, 2 + 2 * GATES1)
            pe.wait_ge(y_b_done, done(NT - 1))
            for f in range(N_MIX2):
                n = B_MIX2 + f
                pe.wait_ge(split_ready, n + 1)
                for t in range(2):
                    q = 2 * f + t
                    if f >= 11:
                        pe.wait_ge(o_free, 2 * (f - 11) + t + 1)
                    else:
                        pe.wait_ge(p_free, 28 + q - 3 if q >= 4 else 28)
                    mm = feature_group(bank[q % 4], n % 2, h_hi, h_lo, half(t))
                    mm.then_inc(block_done if t else p_full, 1)
                if f == 8:
                    pe.wait_ge(row_exp, 3)
                    for c in range(NT):
                        mm = pe.transpose(bank[4][:, 36 * c:36 * (c + 1)], cw[:, c * P:(c + 1) * P], ident[0:36, 0:36])
                    mm.then_inc(cw_turned, 1)
            pe.wait_ge(o_free, 8)
            pe.wait_ge(sel_in, 16)
            for s in (b_rows, b_kqv, numden, c_upd, ms_done):
                pe.sem_inc(s, 1)
            with pe.Fori(0, NT // STEP) as i:
                for u in range(STEP):
                    j = i * STEP + u
                    pe.wait_ge(ml_staged, done(j))
                    pe.wait_ge(num_copied, prev(j))
                    for h in range(MLH):
                        pe.matmul(bank[2][:, h * P:(h + 1) * P], sel[:, h * P:(h + 1) * P], rws[:, 0, :], start=True, stop=True)
                    pe.wait_ge(em_copied, prev(j))
                    for h in range(MLH):
                        pe.matmul(bank[3][:, h * P:(h + 1) * P], sel[:, h * P:(h + 1) * P], rws[:, 2, :], start=True, stop=True)
                    pe.wait_ge(qd_ready, prev(j))
                    for pr in range(2):
                        mm = pe.matmul(bank[4][:, pr * P:(pr + 1) * P], sel[:, (4 + pr) * P:(5 + pr) * P], rws[:, 1, :], start=True, stop=True)
                    mm.then_inc(b_rows, 1)
                    pe.wait_ge(c_new, prev(j))
                    for h in range(MLH):
                        pe.matmul(bank[5][:, h * P:(h + 1) * P], ks[:, h, :], ml_q[:, h // 2, bass.ds(j * P, P)], start=True, stop=True)
                    pe.wait_ge(t_ready, prev(j))
                    for h in range(MLH):
                        pe.transpose(bank[6][:, h * P:(h + 1) * P], ks[:, h, :], ident)
                    pe.wait_ge(v_staged, done(j))
                    pe.wait_ge(den_abs, prev(j))
                    for h in range(MLH):
                        mm = pe.transpose(bank[7][:, h * P:(h + 1) * P], vs[:, h, :], ident)
                    mm.then_inc(b_kqv, 1)
                    gate_group(pe, feature_group, *gate_at(B_GATE2, GATES1, i, u, 0))
                    pe.wait_ge(sc_ready, done(j))
                    pe.wait_ge(kv_tok, done(j))
                    pe.wait_ge(qd_ready, done(j))
                    pe.matmul(bank[7], ones, ml_e[:, :, :].rearrange("p a b -> p (a b)"), start=True, stop=False, skip_group_check=True)
                    for h in range(MLH):
                        pe.matmul(bank[7][:, h * P:(h + 1) * P], c_st[:, h, P:2 * P], qd[:, h // 2, :],
                                  start=False, stop=h == 3, skip_group_check=True)
                    for h in range(MLH):
                        pe.matmul(bank[2][:, h * P:(h + 1) * P], vs[:, h, :], ml_e[:, h, :], start=True, stop=False)
                        mm = pe.matmul(bank[2][:, h * P:(h + 1) * P], c_st[:, h, 0:P], qd[:, h // 2, :],
                                       start=False, stop=True)
                    mm.then_inc(numden, 1)
                    pe.wait_ge(wv_done, done(j))
                    for h in range(MLH):
                        r = 64 * (h % 2)
                        mm = pe.matmul(bank[5][r:r + 64, (h // 2) * 2 * P:(h // 2 + 1) * 2 * P], ktok[:, h, :],
                                       wvx[:, h, :], start=True, stop=True)
                    mm.then_inc(c_upd, 1)
                    gate_group(pe, feature_group, *gate_at(B_GATE2, GATES1, i, u, 1))
                    pe.wait_ge(num_sq, done(j))
                    pe.matmul(bank[6], ones, sqn, start=True, stop=True).then_inc(ms_done, 1)
                    gate_group(pe, feature_group, *gate_at(B_GATE2, GATES1, i, u, 2))

        def mix2_act(act):
            for t in range(2):
                act.wait_ge(gate_stored[t], 16 * (GATES1 + 1))
            act.wait_ge(y_b_done, done(NT - 1))
            for f in range(4):
                act.wait_ge(conv_step, 4 * (f + 1))
                act.activation((ml_q if f < 2 else ml_k)[:, f % 2, :], cacc[:, :], ACT.Silu).then_inc(ml_silu, 1)
            act.wait_ge(zi_ready, 4)
            act.wait_ge(ml_silu, 4)
            act.activation(lrow, zrow, ACT.Abs).then_inc(zabs, 1)
            act.wait_ge(zabs, 1)
            act.activation(lrow, lrow, ACT.Exp, scale=-1.0).then_inc(zabs, 1)
            act.wait_ge(zabs, 2)
            act.activation(lrow, lrow, ACT.Ln, bias=ones[0:4, 0:1]).then_inc(row_ln, 1)
            act.wait_ge(row_step, 3)
            act.activation(rows[64:68, :], mrow, ACT.Exp, scale=-1.0).then_inc(row_exp, 1)
            act.wait_ge(row_arg, 2)
            act.activation(rows[32:36, :], zrow, ACT.Exp).then_inc(row_exp, 1)
            act.activation(cw[32:36, :], irow, ACT.Exp).then_inc(row_exp, 1)
            act.wait_ge(cw_turned, 1)
            act.dma_start(sel[:, :], sel_d).then_inc(sel_in, 16)
            for f in range(9, 13):
                for t in range(2):
                    if t == 0:
                        act.wait_ge(p_full, 10 + f + 1)
                    else:
                        act.wait_ge(block_done, B_MIX2 + f + 1)
                    act.activation(y_a[:, f - 9, half(t)], bank[(2 * f + t) % 4], ACT.Sigmoid).then_inc(o_free, 1)
            for s in (v_staged, e_exp, em_copied, kv_tok, num_copied, den_abs, num_sq, d2_ready, t_root):
                act.sem_inc(s, 1)
            def root(j):
                act.wait_ge(t_ok, done(j))
                act.activation(t_sb[:, :], t_sb[:, :], ACT.Sqrt).then_inc(t_root, 1)

            with act.Fori(0, NT // STEP) as i:
                for u in range(STEP):
                    j = i * STEP + u
                    act.wait_ge(numden, prev(j))
                    act.wait_ge(wv_done, prev(j))
                    apart(act)
                    act.activation(vs[:, :, :], tile_of(ml_v, j), ACT.Copy).then_inc(v_staged, 1)
                    act.wait_ge(b_rows, done(j))
                    act.wait_ge(t_ready, prev(j))
                    act.activation(em_sb[:, :], bank[3], ACT.Copy).then_inc(em_copied, 1)
                    act.wait_ge(e_arg, done(j))
                    ef = ml_e[:, :, :].rearrange("p a b -> p (a b)")
                    act.activation(ef, ef, ACT.Exp).then_inc(e_exp, 1)
                    act.wait_ge(b_kqv, done(j))
                    for o in range(2):
                        act.activation(ktok[:, o:MLH:2, :], bank[6].rearrange("p (a b) -> p a b", a=4)[:, o:MLH:2, 64 * o:64 * o + 64],
                                       ACT.Copy)
                    act.activation(vs[:, :, :].rearrange("p a b -> p (a b)"), bank[7], ACT.Copy).then_inc(kv_tok, 1)
                    gate_tanh(act, *gate_at(B_GATE2, GATES1, i, u, 0), gst2)
                    if u:
                        root(j - 1)
                        act.wait_ge(y_a_done, prev(j))
                    act.wait_ge(numden, done(j))
                    act.activation(num_sb[:, :], bank[2], ACT.Copy).then_inc(num_copied, 1)
                    act.wait_ge(c_upd, done(j))
                    act.wait_ge(num_copied, done(j))
                    act.activation(sqn, num_sb[:, :], ACT.Square).then_inc(num_sq, 1)
                    act.activation(dabs, bank[7], ACT.Abs).then_inc(den_abs, 1)
                    gate_tanh(act, *gate_at(B_GATE2, GATES1, i, u, 1), gst2)
                    act.wait_ge(dn_ready, done(j))
                    act.activation(em_sb[:, :], em_sb[:, :], ACT.Square, scale=EPS ** 0.5).then_inc(d2_ready, 1)
                    if u == STEP - 1:
                        root(j)
                    gate_tanh(act, *gate_at(B_GATE2, GATES1, i, u, 2), gst2)

        def mix2_dve(dve):
            for t in range(2):
                dve.wait_ge(gate_stored[t], 16 * (GATES1 + 1))
            dve.wait_ge(y_b_done, done(NT - 1))
            inits = [(cpad[0][:, 0:3], 0.0), (cpad[1][:, 0:3], 0.0), (rows[:, :], 0.0), (cw[:, :], 0.0),
                     (reset[:, :], 1.0), (mst[:, :], 0.0)]
            for k, (where, value) in enumerate(inits):
                dve.memset(where, value).then_inc(row_init, 1)
            dve.wait_ge(row_init, len(inits))
            dve.memset(by_chunk(reset[:, :])[:, :, 0:1], 0.0).then_inc(row_init, 1)

            def wait_full(f, t):
                if t == 0:
                    dve.wait_ge(p_full, 10 + f + 1)
                else:
                    dve.wait_ge(block_done, B_MIX2 + f + 1)

            for f in range(4):
                pad = cpad[f % 2]
                for t in range(2):
                    wait_full(f, t)
                    dve.tensor_copy(pad[:, 3 + t * HT:3 + (t + 1) * HT], bank[(2 * f + t) % 4]).then_inc(p_free, 1)
                dve.wait_ge(p_free, 28 + 2 * f + 2)
                if f:
                    dve.wait_ge(ml_silu, f)
                for s, tap in enumerate((3, 2, 1, 0)):
                    w = col("convq" if f < 2 else "convk", 4 * (f % 2) + tap)
                    if s == 0:
                        dve.tensor_scalar(cacc[:, :], pad[:, tap:tap + T], w, None, ALU.mult).then_inc(conv_step, 1)
                    else:
                        dve.wait_ge(conv_step, 4 * f + s)
                        dve.scalar_tensor_tensor(cacc[:, :], pad[:, tap:tap + T], w, cacc[:, :], ALU.mult, ALU.add
                                                 ).then_inc(conv_step, 1)
            dve.wait_ge(ml_silu, 2)
            dve.tensor_scalar(ml_q[:, :, :], ml_q[:, :, :], 64 ** -0.5, None, ALU.mult).then_inc(q_scaled, 1)
            for t in range(2):
                wait_full(4, t)
                b = bank[(8 + t) % 4]
                dve.wait_ge(conv_step, 16)
                dve.tensor_scalar(zrow[:, half(t)], b[32:36, :], col("bf", 0, 32, 36), None, ALU.add).then_inc(zi_ready, 1)
                dve.tensor_scalar(irow[:, half(t)], b[0:4, :], col("bi", 0, 0, 4), None, ALU.add).then_inc(zi_ready, 1)
                dve.wait_ge(zi_ready, 2 * t + 2)
                dve.sem_inc(p_free, 1)
            dve.wait_ge(row_ln, 1)
            dve.scalar_tensor_tensor(zrow, zrow, 0.0, lrow, ALU.min, ALU.subtract).then_inc(row_step, 1)
            dve.wait_ge(row_step, 1)
            dve.wait_ge(row_init, len(inits) + 1)
            dve.tensor_tensor_scan(lrow, reset[:, :], zrow, 0.0, ALU.mult, ALU.add).then_inc(row_step, 1)
            dve.wait_ge(row_step, 2)
            dve.tensor_tensor_scan(mrow, zrow, irow, 0.0, ALU.add, ALU.max).then_inc(row_step, 1)
            dve.wait_ge(row_step, 3)
            dve.tensor_tensor(rows[0:4, :], lrow, mrow, ALU.subtract).then_inc(row_step, 1)
            dve.tensor_tensor(cw[0:4, :], irow, lrow, ALU.subtract).then_inc(row_step, 1)
            dve.tensor_copy(mst[:, 1:NT].unsqueeze(2), by_chunk(mrow)[:, 0:NT - 1, P - 1:P]).then_inc(row_step, 1)
            dve.wait_ge(row_step, 6)
            r_c, c_c = by_chunk(rows[0:4, :]), by_chunk(cw[0:4, :])
            dve.tensor_tensor(by_chunk(zrow), r_c, mst[:, :].unsqueeze(2).broadcast_to([4, NT, P]), ALU.add).then_inc(row_arg, 1)
            dve.tensor_tensor(by_chunk(irow), c_c, r_c[:, :, P - 1:P].broadcast_to([4, NT, P]), ALU.add).then_inc(row_arg, 1)
            for f in range(5, 9):
                for t in range(2):
                    wait_full(f, t)
                    dve.tensor_copy(ml_v[:, f - 5, half(t)], bank[(2 * f + t) % 4]).then_inc(p_free, 1)
            for i in range(4):
                dve.wait_ge(o_free, 2 * i + 2)
                dve.tensor_scalar(y_a[:, i, :], y_a[:, i, :], col("mlnorm", i), None, ALU.mult).then_inc(y_a_gain, 1)
            dve.wait_ge(y_a_gain, 4)
            dve.wait_ge(row_exp, 3)
            dve.wait_ge(q_scaled, 1)
            dve.wait_ge(cw_turned, 1)
            turned = bank[4][:, 0:36 * NT].rearrange("p (c r) -> p c r", r=36)
            for k in range(2):
                dve.tensor_copy(cwt[:, :, 4 * k:4 * k + 4], turned[:, :, 32 * k:32 * k + 4]).then_inc(cwt_ready, 1)
            dve.wait_ge(cwt_ready, 2)
            dve.memset(c_st[:, :, :], 0.0).then_inc(row_init, 1)
            dve.memset(ks[:, :, :], 0.0).then_inc(row_init, 1)
            dve.wait_ge(row_init, len(inits) + 3)
            for s in (ml_staged, qd_ready, e_arg, e_masked, sc_ready, wv_done, c_new, dn_ready, t_ready, t_ok, t_inv,
                      y_norm, y_a_done):
                dve.sem_inc(s, 1)
            def finish(j):
                dve.wait_ge(t_root, done(j))
                dve.reciprocal(t_sb[:, :], t_sb[:, :]).then_inc(t_inv, 1)
                dve.wait_ge(t_inv, done(j))
                dve.tensor_tensor(num_sb[:, :], num_sb[:, :], t_sb[:, :], ALU.mult).then_inc(y_norm, 1)
                dve.wait_ge(y_norm, done(j))
                dve.tensor_tensor(tile_of(y_a, j), tile_of(y_a, j), by_chunk(num_sb[:, :]), ALU.mult).then_inc(y_a_done, 1)

            with dve.Fori(0, NT // STEP) as i:
                for u in range(STEP):
                    j = i * STEP + u
                    tok = bass.ds(j * P, P)
                    dve.wait_ge(c_upd, prev(j))
                    for k in range(3):
                        dve.tensor_copy(rws[:, k, :], rows[32 * k:32 * k + 4, tok])
                    for o in range(2):
                        r = 64 * o
                        ins = dve.tensor_copy(ks[r:r + 64, o:MLH:2, :], ml_k[r:r + 64, :, tok])
                    ins.then_inc(ml_staged, 1)
                    dve.tensor_copy(cw_st[:, :], cwt[:, bass.ds(j, 1), :].rearrange("p a b -> p (a b)")).then_inc(ml_small, 1)
                    dve.wait_ge(b_rows, done(j))
                    dve.tensor_copy(dec[:, :].unsqueeze(2), by_chunk(bank[4][:, 0:2 * P])[:, :, P - 1:P]).then_inc(ml_small, 1)
                    dve.tensor_tensor(qd[:, :, :], tile_of(ml_q, j), by_chunk(bank[4][:, 0:2 * P]), ALU.mult).then_inc(qd_ready, 1)
                    dve.wait_ge(ml_small, j * 2 + 2)
                    for h in range(MLH):
                        ins = dve.tensor_scalar(ml_e[:, h, :], bank[2][:, h * P:(h + 1) * P], cw_st[:, h:h + 1], 0.0, ALU.add, ALU.min)
                    ins.then_inc(e_arg, 1)
                    dve.wait_ge(e_exp, done(j))
                    dve.tensor_tensor(ml_e[:, :, :], ml_e[:, :, :], mask.unsqueeze(1).broadcast_to([P, MLH, P]), ALU.mult
                                      ).then_inc(e_masked, 1)
                    dve.wait_ge(e_masked, done(j))
                    dve.wait_ge(b_kqv, done(j))
                    dve.tensor_tensor(ml_e[:, :, :], ml_e[:, :, :], by_chunk(bank[5]), ALU.mult).then_inc(sc_ready, 1)
                    dve.wait_ge(kv_tok, done(j))
                    dve.tensor_tensor(wvx[:, :, 0:P], vs[:, :, :], cw_st[:, 4:8].unsqueeze(2).broadcast_to([P, MLH, P]), ALU.mult)
                    dve.tensor_copy(wvx[:, :, P:2 * P], cw_st[:, 4:8].unsqueeze(2).broadcast_to([P, MLH, P])).then_inc(wv_done, 1)
                    if u:
                        finish(j - 1)
                    dve.wait_ge(c_upd, done(j))
                    for h in range(MLH):
                        r, pr = 64 * (h % 2), h // 2
                        ins = dve.scalar_tensor_tensor(c_st[r:r + 64, h, :], c_st[r:r + 64, h, :], dec[r:r + 64, pr:pr + 1],
                                                       bank[5][r:r + 64, pr * 2 * P:(pr + 1) * 2 * P], ALU.mult, ALU.add)
                    ins.then_inc(c_new, 1)
                    dve.wait_ge(den_abs, done(j))
                    dve.tensor_tensor(em_sb[:, :], em_sb[:, :], dabs, ALU.max).then_inc(dn_ready, 1)
                    dve.wait_ge(ms_done, done(j))
                    dve.wait_ge(d2_ready, done(j))
                    dve.scalar_tensor_tensor(t_sb[:, :], bank[6], 1.0 / P, em_sb[:, :], ALU.mult, ALU.add).then_inc(t_ready, 1)
                    dve.wait_ge(t_ready, done(j))
                    dve.tensor_scalar(t_sb[:, :], t_sb[:, :], 2.0 ** -116, 2.0 ** 117, ALU.max, ALU.min).then_inc(t_ok, 1)
                    if u == STEP - 1:
                        finish(j)

        ys = {"c": y_c, "b": y_b, "a": y_a}
        MERGE = ((("c", 0), ("b", 0)), (("a", 0), ("a", 1)), (("c", 1), ("b", 1)))

        def merge_block(p, b):
            return B_MERGE + b if p == 0 else B_MERGE + 3 + 5 * (p - 1) + (b if b < 2 else 4)

        def merge_out(p):
            return B_MERGE + (5 * (p + 1) if p < 3 else 18)

        def merge_pe(pe, passes, project_out, project_last):
            def products(p, b):
                n = merge_block(p, b)
                pe.wait_ge(split_ready, n + 1)
                for i, (branch, _) in enumerate(MERGE[b]):
                    for t in range(2):
                        g = 2 * i + t
                        q = 3 * p + b
                        if q:
                            pe.wait_ge(gated, 4 * q + g - 3)
                        for k in range(4):
                            if p == 0 and t == 0:
                                pe.wait_ge(y_split, 4 * "cba".index(branch) + k + 1)
                            mm = passes(bank[g], n % 2, (4 * i + k) * P, yh[branch][:, k, half(t)], yl[branch][:, k, half(t)],
                                        k == 0, k == 3)
                        mm.then_inc(block_done if g == 3 else m_full, 1)

            pe.wait_ge(gate_done, 2 * NG + 2)
            pe.wait_ge(t_ready, done(NT - 1))
            for p in range(4):
                products(p, 0)
                products(p, 1)
                if p:
                    project_out(PAIRS["merge"] + p - 1, merge_out(p - 1), merge_out(p - 1) % 2, mg_hi, mg_lo)
                products(p, 2)
            project_last(PAIRS["merge"] + 3, merge_out(3), merge_out(3) % 2, mg_hi, mg_lo, 2)

        def merge_act(act):
            act.wait_ge(block_done, B_MERGE)
            for t in range(2):
                act.wait_ge(gate_stored[t], 16 * (NG + 1))
            for b in "cba":
                if b == "a":
                    act.wait_ge(y_a_done, done(NT - 1))
                for k in range(4):
                    act.activation(yh[b][:, k, :], ys[b][:, k, :], ACT.Copy).then_inc(yh_ready, 1)
            act.wait_ge(y_split, 12)
            for p in range(4):
                for m in range(2):
                    for t in range(2):
                        act.wait_ge(gated, 12 * p + (5 + t if m == 0 else 11 + t))
                        if p and m == 0 and t == 0:
                            act.wait_ge(block_done, merge_out(p - 1) + 2)
                        act.activation(mg_hi[:, m, half(t)], mg[:, m, half(t)], ACT.Copy).then_inc(u_hi_ready, 1)

        def merge_dve(dve, add_out, split_u):
            dve.wait_ge(block_done, B_MERGE)
            for t in range(2):
                dve.wait_ge(gate_stored[t], 16 * (NG + 1))
            dve.wait_ge(y_a_done, done(NT - 1))
            for b in "cba":
                for k in range(4):
                    dve.wait_ge(yh_ready, 4 * "cba".index(b) + k + 1)
                    dve.tensor_tensor(yl[b][:, k, :], ys[b][:, k, :], yh[b][:, k, :], ALU.subtract).then_inc(y_split, 1)
            dve.wait_ge(y_split, 12)

            def gate(p, b):
                n = merge_block(p, b)
                for i, (branch, m) in enumerate(MERGE[b]):
                    g = gt[branch + str(m)]
                    for t in range(2):
                        if 2 * i + t == 3:
                            dve.wait_ge(block_done, n + 1)
                        else:
                            dve.wait_ge(m_full, 9 * p + 3 * b + 2 * i + t + 1)
                        if t == 0:
                            dve.wait_ge(gt_in[branch + str(m)], 16 * (p + 1))
                        first = (branch, m) in (("c", 0), ("a", 1))
                        dst = mg[:, m, half(t)] if first else mtmp[:, :]
                        count = 12 * p + 4 * b + 2 * i + t + 1
                        if count > 1:
                            dve.wait_ge(gated, count - 1)
                        ins = dve.scalar_tensor_tensor(dst, g[:, half(t)], 1.0, bank[2 * i + t], ALU.add, ALU.mult)
                        if first:
                            ins.then_inc(gated, 1)
                        else:
                            ins.then_inc(m_prod, 1)
                            m_count[0] += 1
                            dve.wait_ge(m_prod, m_count[0])
                            dve.tensor_tensor(mg[:, m, half(t)], mg[:, m, half(t)], mtmp[:, :], ALU.add).then_inc(gated, 1)

            m_count = [0]
            for p in range(4):
                gate(p, 0)
                gate(p, 1)
                if p:
                    add_out(PAIRS["merge"] + p - 1, merge_out(p - 1), x2)
                else:
                    dve.wait_ge(x_back, 16)
                split_u(PAIRS["merge"] + p, 0, mg, mg_hi, mg_lo)
                gate(p, 2)
                split_u(PAIRS["merge"] + p, 1, mg, mg_hi, mg_lo)

        @block.sync
        def _(sp):
            def load(n, slot):
                sp.wait_ge(split_ready, n - 1)
                sp.dma_start(raw[slot][:, :], wts[bass.ds(n, 1)].rearrange("a p n -> p (a n)")
                             ).then_inc(raw_loaded[slot], 16)

            def load_gate(g, m, uses):
                if uses:
                    sp.wait_ge(gated, uses)
                elif g == "c0":
                    sp.wait_ge(y_split, 12)
                    for i in range(2):
                        sp.wait_ge(gate_stored[i], 16 * (NG + 1))
                sp.dma_start(gt[g][:, :], gate_scr[{"a": 0, "b": 8, "c": 16}[g[0]] + m]).then_inc(gt_in[g], 16)

            for i, part in enumerate(x_in):
                sp.dma_start(x1[:, 2 * i:2 * i + 2, :], xT[:, 2 * i:2 * i + 2, :]).then_inc(part, 16)
            sp.dma_start(cst[:, :], const_d).then_inc(const_in, 16)
            for i in range(2):
                sp.dma_start(raw[i][:, :], wts[i]).then_inc(raw_loaded[i], 16)
            sp.dma_start(memx[:, :, :], memT).then_inc(mem_in, 16)
            with sp.Fori(1, B_MIX1 // 2 + 1) as i:
                load(i * 2, 0)
                load(i * 2 + 1, 1)
            sp.wait_ge(x_added, 16 * (NPAIR + 1))
            sp.dma_start(x_scr, x1[:, :, :]).then_inc(x_saved, 16)
            with sp.Fori(B_MIX1 // 2 + 1, B_MERGE // 2) as i:
                load(i * 2, 0)
                load(i * 2 + 1, 1)
            for n in range(2 * (B_MERGE // 2), B_MERGE):
                load(n, n % 2)
            for k in range(20):
                for p in range(1, 4):
                    if k == 5 * p - 2:
                        load_gate("c0", 2 * p, 12 * (p - 1) + 2)
                        load_gate("b0", 2 * p, 12 * (p - 1) + 4)
                    if k == 5 * p - 1:
                        load_gate("a0", 2 * p, 12 * (p - 1) + 6)
                        load_gate("a1", 2 * p + 1, 12 * (p - 1) + 8)
                    if k == 5 * p + 1:
                        load_gate("c1", 2 * p + 1, 12 * (p - 1) + 10)
                        load_gate("b1", 2 * p + 1, 12 * (p - 1) + 12)
                load(B_MERGE + k, (B_MERGE + k) % 2)
                if k == 1:
                    sp.wait_ge(block_done, B_MERGE)
                    sp.wait_ge(x_saved, 16)
                    sp.dma_start(x2[:, :, :], x_scr).then_inc(x_back, 16)
                    for g in ("c0", "b0", "a0", "a1", "c1", "b1"):
                        load_gate(g, int(g[1]), 0)
            for n in range(B_FFN2, B_FFN2 + B_FFN2 % 2):
                load(n, n % 2)
            with sp.Fori((B_FFN2 + 1) // 2, NB // 2) as i:
                load(i * 2, 0)
                load(i * 2 + 1, 1)
            for n in range(NB - NB % 2, NB):
                load(n, n % 2)
            for k in range(KD):
                sp.wait_ge(x_added, 16 * (PAIRS["ffn2"] + NPAIR) + 2 * k + 2)
                sp.dma_start(out[k], x2[:, k, :]).then_inc(out_done, 16)
            sp.wait_ge(out_done, 16 * KD)

        @block.gpsimd
        def _(pool):
            def split(n, turn, slot):
                if not (isinstance(n, int) and n < 2):
                    pool.wait_ge(block_done, n - 1)
                pool.wait_ge(raw_loaded[slot], turn * 16 + 16)
                apart(pool)
                pool.tensor_scalar(whi[slot][:, :], raw[slot][:, :], 1.0, 0.0, ALU.mult, ALU.add).then_inc(w_hi_ready, 1)
                pool.wait_ge(w_hi_ready, n + 1)
                pool.tensor_tensor(wlo[slot][:, :], raw[slot][:, :], whi[slot][:, :],
                                   ALU.subtract).then_inc(split_ready, 1)

            pool.dma_start(cols[:, :], cols_d).then_inc(cols_in, 16)
            pool.wait_ge(cols_in, 16)
            split(0, 0, 0)
            split(1, 0, 1)
            with pool.Fori(1, NB // 2) as i:
                split(i * 2, i, 0)
                split(i * 2 + 1, i, 1)
            for n in range(NB - NB % 2, NB):
                split(n, n // 2, n % 2)

        @block.tensor
        def _(pe):
            def passes(dst, slot, wcol, r_hi, r_lo, first, last):
                w_h, w_l = whi[slot][:, wcol:wcol + P], wlo[slot][:, wcol:wcol + P]
                pe.matmul(dst, w_h, r_hi, start=first, stop=False)
                pe.matmul(dst, w_h, r_lo, start=False, stop=False)
                return pe.matmul(dst, w_l, r_hi, start=False, stop=last)

            def feature_group(dst, slot, hi, lo, cols_of, k_wait=None):
                for k in range(KD):
                    if k_wait is not None:
                        pe.wait_ge(h_ready, k_wait + k + 1)
                    mm = passes(dst, slot, k * P, hi[:, k, cols_of], lo[:, k, cols_of], k == 0, k == KD - 1)
                return mm

            def norm_sum(i, t):
                f = (f1, f1, f2)[i]
                pe.wait_ge(acc_ready, 2 * i + t + 1)
                for c in range(4):
                    mm = pe.matmul(norm_bank[t][:, c:c + 1], f["rs"][:, t, c * P:(c + 1) * P], ones[:, 0:1], start=True, stop=True)
                mm.then_inc(sum_ready, 1)

            def norm_spread(i, t):
                f = (f1, f1, f2)[i]
                pe.wait_ge(diag_ready, 2 * i + t + 1)
                pe.matmul(norm_bank[t], ones, f["uf"][:, 0, t, :], start=True, stop=True).then_inc(rs_ready, 1)

            def ffn_tile(r, tile, n, slot_a, hi, lo):
                for which, full, free in ((0, a_full, a_free), (1, b_full, b_free)):
                    slot = (slot_a + which) % 2
                    pe.wait_ge(split_ready, n + which + 1)
                    for t in range(2):
                        pe.wait_ge(free, 44 * r + tile * 2 + t - 1)
                        mm = feature_group(bank[2 * which + t], slot, hi, lo, half(t))
                        mm.then_inc(block_done if t else full, 1)

            def first_blocks(i, n, banks, full, hi, lo):
                for t in range(2):
                    if t:
                        if i:
                            norm_sum(i, 1)
                        norm_spread(i, 1)
                    for w in range(2):
                        if t == 0:
                            pe.wait_ge(split_ready, n + w + 1)
                        mm = feature_group(banks[2 * w + t], (n + w) % 2, hi, lo, half(t), 16 * i + 8 * t if w == 0 else None)
                        mm.then_inc(block_done if t else full[w], 1)

            def project_out(pair, n, slot0, hi, lo, order=BY_FEATURE, between={}):
                pe.wait_ge(u_ready, pair * 4 + 4)
                seen = -1
                for o, (k, t) in enumerate(order):
                    b, m = divmod(k, 4)
                    slot = (slot0 + b) % 2
                    if b > seen:
                        pe.wait_ge(split_ready, n + b + 1)
                        seen = b
                    pe.wait_ge(x_added, pair * 16 + (o + 13))
                    for c in range(2):
                        mm = passes(bank[4 + o % 4], slot, (2 * m + c) * P, hi[:, c, half(t)], lo[:, c, half(t)], c == 0, c == 1)
                    mm.then_inc(out_signal(order, n, pair, o)[0], 1)
                    if o in between:
                        between[o]()

            def project_last(pair, n, slot0, hi, lo, i):
                project_out(pair, n, slot0, hi, lo, BY_HALF, {9: lambda: norm_sum(i, 0), 11: lambda: norm_spread(i, 0)})

            def ffn(r, f, hi, lo, b0, pairs, i):
                s0 = b0 % 2
                if r:
                    pe.wait_ge(b_free, 44)
                first_blocks(i, b0, bank, (a_full, b_full), hi, lo)
                if r == 0:
                    pe.wait_ge(mem_acc, 1)
                    pe.matmul(bank[4][:, 0:NMEM], ones, f["rs"][:, 0, 0:NMEM], start=True, stop=True).then_inc(mem_sum, 1)
                ffn_tile(r, 1, b0 + 2, s0, hi, lo)
                with pe.Fori(1, NPAIR) as c:
                    n = c * 6 + (b0 - 2)
                    ffn_tile(r, c * 2, n, s0, hi, lo)
                    project_out(c + (pairs - 1), n + 2, s0, f["u_hi"], f["u_lo"])
                    ffn_tile(r, c * 2 + 1, n + 4, s0, hi, lo)
                if r == 0:
                    project_last(pairs + NPAIR - 1, b0 + 6 * NPAIR - 2, s0, f["u_hi"], f["u_lo"], 1)
                else:
                    project_out(pairs + NPAIR - 1, b0 + 6 * NPAIR - 2, s0, f["u_hi"], f["u_lo"])

            pe.wait_ge(const_in, 16)
            for t in range(2):
                norm_sum(0, t)
            norm_spread(0, 0)
            ffn(0, f1, h_hi, h_lo, B_FFN1, PAIRS["ffn1"], 0)
            mix1_pe(pe, feature_group, first_blocks)
            mix2_pe(pe, feature_group)
            merge_pe(pe, passes, project_out, project_last)
            ffn(1, f2, h2_hi, h2_lo, B_FFN2, PAIRS["ffn2"], 2)

        @block.scalar
        def _(act):
            def norm(i, x, f, hi):
                order = NORM_ORDER[i]

                def squares(first, end):
                    for o in range(first, end):
                        k, t = order[o]
                        if i == 0 and t == 0:
                            act.wait_ge(x_in[k // 2], 16)
                        if i:
                            act.wait_ge(x_added, 16 * (PAIRS["ffn1"] + NPAIR if i == 1 else PAIRS["ffn2"]) + 1 + o)
                        if k == 0:
                            dst = f["rs"][:, t, :]
                        else:
                            m = square_slot(i, k, t)
                            dst = f["sq"][:, m % 4, :]
                            if m >= 4:
                                act.wait_ge(sq_used, m - 3)
                        act.activation(dst, x[:, k, half(t)], ACT.Square).then_inc(sq_ready, 1)

                def root(t):
                    act.wait_ge(sum_ready, 2 * i + t + 1)
                    act.activation(norm_s[:, t, :], norm_bank[t][:, 0:4], ACT.Sqrt, bias=col("eps"), scale=1.0 / D).then_inc(rms_ready, 1)

                def round_h(t):
                    for k in range(KD):
                        act.wait_ge(hf_ready, 16 * i + 8 * t + k + 1)
                        act.activation(hi[:, k, half(t)], f["hf"][:, k % 2, :], ACT.Copy).then_inc(h_hi_ready, 1)

                if i == 0:
                    squares(0, 16)
                    root(0)
                    root(1)
                    round_h(0)
                else:
                    squares(0, 10)
                    root(0)
                    squares(10, 13)
                    round_h(0)
                    squares(13, 16)
                    root(1)
                round_h(1)

            def ffn(r, f, b0, pairs):
                def silu(tile, n, t):
                    if t == 0:
                        act.wait_ge(a_full, tile + (22 * r + 1))
                    else:
                        act.wait_ge(block_done, n + 1)
                    if not (isinstance(tile, int) and tile == 0):
                        act.wait_ge(b_free, tile * 2 + (44 * r + t - 1))
                    act.activation(f["sa"][:, t, :], bank[t], ACT.Silu).then_inc(a_free, 1)

                def round_u(tile, which, t):
                    act.wait_ge(b_free, tile * 2 + (44 * r + t + 1))
                    act.activation(f["u_hi"][:, which, half(t)], f["uf"][:, which, t, :], ACT.Copy).then_inc(u_hi_ready, 1)

                for tile in range(2):
                    for t in range(2):
                        silu(tile, b0 + 2 * tile, t)
                    if r == 0 and tile == 0:
                        act.wait_ge(mem_sum, 1)
                        act.activation(f["rs"][:, 1, 0:NMEM], bank[4][:, 0:NMEM], ACT.Sqrt, bias=col("eps"), scale=1.0 / D
                                       ).then_inc(mem_rms, 1)
                    for t in range(2):
                        round_u(tile, tile, t)
                if r == 0:
                    act.wait_ge(mem_h, KD)
                    act.activation(mh_hi[:, :, :].rearrange("p a b -> p (a b)"), mxv, ACT.Copy).then_inc(mem_hi, 1)
                with act.Fori(1, NPAIR) as c:
                    n = c * 6 + (b0 - 2)
                    for t in range(2):
                        silu(c * 2, n, t)
                    act.wait_ge(block_done, n + 4)
                    for t in range(2):
                        round_u(c * 2, 0, t)
                    for t in range(2):
                        silu(c * 2 + 1, n + 4, t)
                    for t in range(2):
                        round_u(c * 2 + 1, 1, t)

            act.wait_ge(cols_in, 16)
            norm(0, x1, f1, h_hi)
            mxv = memx[:, :, :].rearrange("p a b -> p (a b)")
            act.wait_ge(mem_in, 16)
            act.activation(f1["sq"][:, :, :].rearrange("p a b -> p (a b)"), mxv, ACT.Square).then_inc(mem_sq, 1)
            ffn(0, f1, B_FFN1, PAIRS["ffn1"])
            norm(1, x1, f1, h_hi)
            mix1_act(act)
            mix2_act(act)
            merge_act(act)
            norm(2, x2, f2, h2_hi)
            ffn(1, f2, B_FFN2, PAIRS["ffn2"])

        @block.vector
        def _(dve):
            def norm(i, x, f, hi, lo, gain, outs=None):
                order = NORM_ORDER[i]

                def add_square(o):
                    k, t = order[o]
                    if k:
                        m = square_slot(i, k, t)
                        dve.wait_ge(sq_ready, 16 * i + o + 1)
                        if k > 1:
                            dve.wait_ge(sq_used, square_slot(i, k - 1, t) + 1)
                        acc = f["rs"][:, t, :]
                        ins = dve.tensor_tensor(acc, acc, f["sq"][:, m % 4, :], ALU.add)
                        ins.then_inc(sq_used, 1)
                        if k == KD - 1:
                            dve.wait_ge(sq_used, m + 1)
                            dve.sem_inc(acc_ready, 1)

                def diagonal(t):
                    dve.wait_ge(rms_ready, 2 * i + t + 1)
                    dve.reciprocal(norm_s[:, t, :], norm_s[:, t, :]).then_inc(rinv_ready, 1)
                    dve.wait_ge(rinv_ready, 2 * i + t + 1)
                    dve.tensor_tensor(f["uf"][:, 0, t, :].rearrange("p (c n) -> p c n", c=4), ident.unsqueeze(1).broadcast_to([P, 4, P]),
                                      norm_s[:, t, :].unsqueeze(2).broadcast_to([P, 4, P]), ALU.mult).then_inc(diag_ready, 1)

                def scale(t, k):
                    n = 16 * i + 8 * t + k
                    if k == 0:
                        dve.wait_ge(rs_ready, 2 * i + t + 1)
                    if n % 16 >= 2:
                        dve.wait_ge(h_ready, n - 1)
                    dve.scalar_tensor_tensor(f["hf"][:, k % 2, :], x[:, k, half(t)], col(gain, k), norm_bank[t],
                                             ALU.mult, ALU.mult).then_inc(hf_ready, 1)

                def split_h(t, k):
                    n = 16 * i + 8 * t + k
                    dve.wait_ge(h_hi_ready, n + 1)
                    dve.tensor_tensor(lo[:, k, half(t)], f["hf"][:, k % 2, :], hi[:, k, half(t)], ALU.subtract).then_inc(h_ready, 1)

                if i == 0:
                    for o in range(16):
                        add_square(o)
                    for t in range(2):
                        diagonal(t)
                    for part in x_in:
                        dve.wait_ge(part, 16)
                    dve.sem_inc(x_added, 16)
                else:
                    for o in range(8):
                        outs(o, o + 1)
                        if o:
                            add_square(o - 1)
                    add_square(7)
                    outs(8, 10)
                    diagonal(0)
                    outs(10, 12)
                for k in range(KD + 1):
                    if k < KD:
                        scale(0, k)
                    if k:
                        split_h(0, k - 1)
                    if i and k < 4:
                        outs(12 + k, 13 + k)
                if i:
                    for o in range(8, 16):
                        add_square(o)
                    diagonal(1)
                for k in range(KD + 1):
                    if k < KD:
                        scale(1, k)
                    if k:
                        split_h(1, k - 1)

            def add_out(pair, n, x, first=0, end=16, order=BY_FEATURE):
                for o in range(first, end):
                    k, t = order[o]
                    dve.wait_ge(*out_signal(order, n, pair, o))
                    dve.wait_ge(x_added, pair * 16 + (o + 1))
                    xs = x[:, k, half(t)]
                    dve.scalar_tensor_tensor(xs, bank[4 + o % 4], 0.5, xs, ALU.mult, ALU.add).then_inc(x_added, 1)

            def split_u(pair, which, src, f_hi, f_lo):
                for t in range(2):
                    dve.wait_ge(u_hi_ready, pair * 4 + (2 * which + t + 1))
                    dve.tensor_tensor(f_lo[:, which, half(t)], src[:, which, t, :] if len(src.shape) == 4 else src[:, which, half(t)],
                                      f_hi[:, which, half(t)], ALU.subtract).then_inc(u_ready, 1)

            def ffn(r, x, f, b0, pairs):
                def product(tile, which, n):
                    for t in range(2):
                        if t == 0:
                            dve.wait_ge(b_full, tile + (22 * r + 1))
                        else:
                            dve.wait_ge(block_done, n + 2)
                        dve.wait_ge(a_free, tile * 2 + (44 * r + t + 1))
                        dve.tensor_tensor(f["uf"][:, which, t, :], f["sa"][:, t, :], bank[2 + t], ALU.mult).then_inc(b_free, 1)

                rstd = f["rs"][:, 1, 0:NMEM]
                if r == 0:
                    dve.wait_ge(mem_sq, 1)
                    dve.tensor_reduce(f["rs"][:, 0, 0:NMEM], f["sq"][:, :, :].rearrange("p a b -> p (a b)").rearrange("p (k n) -> p n k", k=KD),
                                      AX.X, ALU.add).then_inc(mem_acc, 1)
                for tile in range(2):
                    product(tile, tile, b0 + 2 * tile)
                    if r == 0 and tile == 0:
                        dve.wait_ge(mem_rms, 1)
                        dve.reciprocal(rstd, rstd).then_inc(mem_rstd, 1)
                        dve.wait_ge(mem_rstd, 1)
                        for k in range(KD):
                            dve.scalar_tensor_tensor(memx[:, k, :], memx[:, k, :], col("mem", k), rstd, ALU.mult, ALU.mult
                                                     ).then_inc(mem_h, 1)
                    split_u(pairs, tile, f["uf"], f["u_hi"], f["u_lo"])
                if r == 0:
                    dve.wait_ge(mem_hi, 1)
                    dve.tensor_tensor(mh_lo[:, :, :], memx[:, :, :], mh_hi[:, :, :], ALU.subtract).then_inc(mem_ready, 1)
                with dve.Fori(1, NPAIR) as c:
                    n = c * 6 + (b0 - 2)
                    product(c * 2, 0, n)
                    add_out(c + (pairs - 1), n + 2, x)
                    split_u(c + pairs, 0, f["uf"], f["u_hi"], f["u_lo"])
                    product(c * 2 + 1, 1, n + 4)
                    split_u(c + pairs, 1, f["uf"], f["u_hi"], f["u_lo"])

            dve.wait_ge(cols_in, 16)
            bgate = cols[:, COLS["bgate"][0]:COLS["bgate"][0] + NG]
            dve.tensor_scalar(bgate, bgate, 0.5, None, ALU.mult).then_inc(consts_ready, 1)
            norm(0, x1, f1, h_hi, h_lo, "ffn1")
            ffn(0, x1, f1, B_FFN1, PAIRS["ffn1"])

            def last_outs(pair, n, x):
                return lambda first, end: add_out(pair, n, x, first, end, BY_HALF)

            norm(1, x1, f1, h_hi, h_lo, "mix", last_outs(PAIRS["ffn1"] + NPAIR - 1, B_MIX1 - 2, x1))
            mix1_dve(dve)
            mix2_dve(dve)
            merge_dve(dve, add_out, split_u)
            norm(2, x2, f2, h2_hi, h2_lo, "ffn2", last_outs(PAIRS["merge"] + 3, merge_out(3), x2))
            ffn(1, x2, f2, B_FFN2, PAIRS["ffn2"])
            add_out(PAIRS["ffn2"] + NPAIR - 1, NB - 2, x2)


def constants():
    c = np.zeros((P, NCONST), np.float32)
    i = np.arange(P)
    c[:, C_ID:C_ID + P] = np.eye(P)
    c[:, C_ONE:C_ONE + P] = 1.0
    c[:, C_BLK:C_BLK + P] = (i[:, None] // 64 == i[None, :] // 64)
    for o in (0, 64):
        for d in range(8):
            c[o + d + 8, C_PERM + o + d] = -1.0
            c[o + d, C_PERM + o + d + 8] = 1.0
    c[:, C_MASK:C_MASK + P] = (i[:, None] <= i[None, :])
    c[:, C_BLK2:C_BLK2 + 2] = (i[:, None] // 64 == np.arange(2)[None, :])
    s = np.zeros((MLH, 6 * P), np.float32)
    for h in range(MLH):
        s[h, h * P:(h + 1) * P] = 1.0
        s[h, (8 + h) * 64:(9 + h) * 64] = 1.0
    return c, s


def weight_stream(w):
    def feature(m, j=None):
        m = m if j is None else m[:, j * P:(j + 1) * P]
        return m.reshape(KD, P, P).transpose(1, 0, 2).reshape(P, 1024)

    def outs(m, pair):
        v = m[2 * pair * P:(2 * pair + 2) * P].reshape(2, P, 2, 4, P)
        return [v[:, :, b].transpose(1, 2, 0, 3).reshape(P, 1024) for b in range(2)]

    def ffn(w_in, w_out):
        blocks = []
        for c in range(NPAIR):
            ab = [feature(w_in, o + 2 * c + i) for i in range(2) for o in (0, NF)]
            blocks += ab[:2] + (outs(w_out, c - 1) if c else []) + ab[2:]
        return blocks + outs(w_out, NPAIR - 1)

    at = np.cumsum((0, 256, 256, 512, 4, 4, 512, 512, 128, 128, 512, 3072))
    mq, mk, mv, mi, mf, mo, sq, sk, sv, cq, gates = (w["w_in"][:, a:b] for a, b in zip(at[:-1], at[1:]))
    order = [h for i in range(4) for h in (i, i + 4)]
    sq = sq.reshape(D, SWH, 64)[:, order].reshape(D, 512)
    br_sw = w["w_br_sw"].reshape(SWH, 64, D)[order].reshape(512, D)
    pre = np.zeros((D, P), np.float32)
    pre[:, 0:4], pre[:, 32:36] = mi, mf
    gate = [feature(gates, g) for g in range(NG)]
    blocks = ffn(w["ffn1_w_in"], w["ffn1_w_out"])
    blocks += [feature(cq, i) for i in range(4)] + [feature(sq, i) for i in range(4)] + [feature(sk), feature(sv)]
    blocks += [feature(w["mx_w_kv"], i) for i in range(8)]
    blocks += gate[:GATES1]
    blocks += [feature(mq, i) for i in range(2)] + [feature(mk, i) for i in range(2)] + [feature(pre)]
    blocks += [feature(mv, i) for i in range(4)] + [feature(mo, i) for i in range(4)]
    blocks += gate[GATES1:]
    branch = {"a": w["w_br_ml"], "b": br_sw, "c": w["w_br_mx"]}

    def half_block(b, m):
        return branch[b][:, m * P:(m + 1) * P].reshape(4, P, P).transpose(1, 0, 2).reshape(P, 512)

    for p in range(4):
        m0, m1 = 2 * p, 2 * p + 1
        b = [np.concatenate([half_block(*x), half_block(*y)], axis=1) for x, y in (
            (("c", m0), ("b", m0)), (("a", m0), ("a", m1)), (("c", m1), ("b", m1)))]
        blocks += b[:2] + (outs(w["w_out"], p - 1) if p else []) + b[2:]
    blocks += outs(w["w_out"], 3)
    blocks += ffn(w["ffn2_w_in"], w["ffn2_w_out"])
    assert len(blocks) == NB
    return np.stack(blocks)


def columns(v):
    c = np.zeros((P, NCOL), np.float32)

    def put(name, x):
        c[:, COLS[name][0]:COLS[name][0] + COLS[name][1]] = x

    for name, key in (("ffn1", "ffn1_norm"), ("mix", "mix_norm"), ("ffn2", "ffn2_norm"), ("mem", "mem_norm"),
                      ("bgate", "b_gate"), ("mlnorm", "ml_out_norm"), ("mxq", "mx_q_norm"), ("mxk", "mx_k_norm")):
        put(name, v[key].reshape(-1, P).T)
    for name, key in (("convq", "ml_conv_q"), ("convk", "ml_conv_k")):
        put(name, v[key].reshape(4, 2, P).transpose(2, 1, 0).reshape(P, 8))
    for name, key in (("swq", "sw_q_norm"), ("swk", "sw_k_norm")):
        put(name, np.concatenate([v[key], v[key]])[:, None])
    put("sink", np.broadcast_to(v["sw_sinks"][None, :], (P, SWH)))
    c[0:4, COLS["bi"][0]] = v["ml_b_i"]
    c[32:36, COLS["bf"][0]] = v["ml_b_f"]
    half = 8
    inv = np.float32(500000.0) ** (-np.arange(half, dtype=np.float32) * np.float32(2.0 / 16))
    for o in (0, 8, 64, 72):
        c[o:o + 8, COLS["inv"][0]] = inv
    c[:, COLS["eps"][0]] = EPS
    return c


def kernel(**inputs):
    import concourse.bacc as bacc
    from concourse.bass_utils import run_bass_kernel_spmd

    v = {k: np.asarray(a) for k, a in inputs.items()}
    one = {k: a[0] for k, a in v.items()}
    cst, sel = constants()
    arrays = {
        "xT": np.ascontiguousarray(one["x"].T.reshape(KD, P, T).transpose(1, 0, 2)),
        "memT": np.ascontiguousarray(one["mem"].T.reshape(KD, P, NMEM).transpose(1, 0, 2)),
        "pos": np.ascontiguousarray(np.broadcast_to(one["positions"][None, :], (P, T))),
        "weights": weight_stream(one),
        "columns": columns(one),
        "constants": cst,
        "selectors": sel,
    }
    nc = bacc.Bacc("TRN2", target_bir_lowering=False, num_devices=1)
    args = [nc.dram_tensor("in_" + k, a.shape, mybir.dt.from_np(a.dtype), kind="ExternalInput").ap()
            for k, a in arrays.items()]
    out = nc.dram_tensor("out_x", (KD, P, T), F32, kind="ExternalOutput").ap()
    build(nc, *args, out)
    r = run_bass_kernel_spmd(nc, [{"in_" + k: a for k, a in arrays.items()}], core_ids=[0])
    y = r.results[0]["out_x"]
    return np.ascontiguousarray(y.reshape(D, T).T)[None]
```

```python
import math
from contextlib import ExitStack

import numpy as np

import concourse.bass as bass
from concourse import mybir

F32 = mybir.dt.float32
F32R = mybir.dt.float32r
I32 = mybir.dt.int32
ALU = mybir.AluOpType
ACT = mybir.ActivationFunctionType
AX = mybir.AxisListType

P = 128
D = 1024
KD = D // P
T = 1024
HT = T // 2
FF = 2816
NF = FF // P
NPAIR = NF // 2
NMEM = 256
NG = 24
NT = T // P
MLH = 4
SWH = 8
MXH = 4
EPS = 1e-6
NEG = -1e30
M_LEAST = -41.0
WIN = 192

B_FFN1 = 0
B_MIX1 = B_FFN1 + 6 * NPAIR
N_MIX1 = 18
B_GATE1 = B_MIX1 + N_MIX1
GATES1 = 12
B_MIX2 = B_GATE1 + GATES1
N_MIX2 = 13
B_GATE2 = B_MIX2 + N_MIX2
B_MERGE = B_GATE2 + NG - GATES1
B_FFN2 = B_MERGE + 20
NB = B_FFN2 + 6 * NPAIR

COLS = {}
for _n, _w in (("ffn1", KD), ("mix", KD), ("ffn2", KD), ("mem", KD), ("bgate", NG), ("convq", 8),
               ("convk", 8), ("mlnorm", 4), ("swq", 1), ("swk", 1), ("mxq", 1), ("mxk", 1),
               ("sink", SWH), ("bi", 1), ("bf", 1), ("inv", 1), ("eps", 1)):
    COLS[_n] = (sum(w for _, w in COLS.values()), _w)
NCOL = sum(w for _, w in COLS.values())

C_ID, C_ONE, C_BLK, C_PERM, C_MASK = (P * i for i in range(5))
C_BLK2 = 5 * P
NCONST = C_BLK2 + 2

PI2_A = 6.28125
PI2_B = float(np.float32(np.round((2 * np.pi - PI2_A) * 2.0**21) / 2.0**21))
PI2_C = float(np.float32(2 * np.pi - PI2_A - PI2_B))
ROUND = 12582912.0
PI_IN = 3.1415925


def build(nc, xT, memT, pos, wts, cols_d, const_d, sel_d, out):
    with ExitStack() as top:
        def sem(name):
            return top.enter_context(nc.semaphore(name))

        def era(side):
            st = ExitStack()

            def sb(name, shape, dt=F32):
                return st.enter_context(nc.sbuf_tensor(name, shape, dt, side=side))
            return st, sb

        gate_scr = nc.dram_tensor("gate_scr", (NG, P, T), F32, kind="Internal").ap()
        x_scr = nc.dram_tensor("x_scr", (P, KD, T), F32, kind="Internal").ap()

        base, sb = era("left")
        raw = [sb(f"raw{i}", [P, 1024]) for i in range(2)]
        whi = [sb(f"whi{i}", [P, 1024], F32R) for i in range(2)]
        wlo = [sb(f"wlo{i}", [P, 1024], F32R) for i in range(2)]
        cst = sb("cst", [P, NCONST])
        cols = sb("cols", [P, NCOL])
        norm_s = sb("norm_s", [P, 2, 4])
        warm = sb("warm", [1, 3])

        def col(name, i=0, p0=0, p1=P):
            c = COLS[name][0] + i
            return cols[p0:p1, c:c + 1]

        ident = cst[:, C_ID:C_ID + P]
        ones = cst[:, C_ONE:C_ONE + P]
        blk64 = cst[:, C_BLK:C_BLK + P]
        perm = cst[:, C_PERM:C_PERM + P]
        mask = cst[:, C_MASK:C_MASK + P]
        blk2 = cst[:, C_BLK2:C_BLK2 + 2]

        eh, sb = era("left")
        h_hi = sb("h_hi", [P, KD, T], F32R)
        h_lo = sb("h_lo", [P, KD, T], F32R)
        em_, sb = era("left")
        mh_hi = sb("mh_hi", [P, KD, NMEM], F32R)
        mh_lo = sb("mh_lo", [P, KD, NMEM], F32R)

        def ffn_buffers(tag, sb):
            return dict(
                u_hi=sb("u_hi" + tag, [P, 2, T], F32R), u_lo=sb("u_lo" + tag, [P, 2, T], F32R),
                sa=sb("sa" + tag, [P, 2, HT]), uf=sb("uf" + tag, [P, 2, 2, HT]),
                sq=sb("sq" + tag, [P, 4, HT]), hf=sb("hf" + tag, [P, 2, HT]), rs=sb("rs" + tag, [P, 2, HT]))

        e1, sb = era("right")
        x1 = sb("x1", [P, KD, T])
        f1 = ffn_buffers("1", sb)
        memx = sb("memx", [P, KD, NMEM])
        e1.close()

        ey, sb = era("right")
        y_c = sb("y_c", [P, 4, T])
        y_b = sb("y_b", [P, 4, T])
        m1, sb = era("right")
        kv_all = sb("kv_all", [P, 2, 64 + T])
        rope_c = sb("rope_c", [P, T])
        rope_s = sb("rope_s", [P, T])
        ck = sb("ck", [P, MXH, NMEM])
        cv = sb("cv", [P, 2, 4 * P])
        rq = sb("rq", [P, NT, 12])
        p_mx = sb("p_mx", [P, MXH, NMEM])
        pt_mx = sb("pt_mx", [P, 2 * MXH, P])
        p_sw = sb("p_sw", [P, SWH, P])
        pt_sw = sb("pt_sw", [P, SWH, P])
        q_mx = sb("q_mx", [P, 4, P])
        q_sw = sb("q_sw", [P, 4, P])
        q_rot = sb("q_rot", [P, 4, P])
        q_tmp = sb("q_tmp", [P, 4, P])
        kv_st = sb("kv_st", [P, 2, WIN])
        v_win = sb("v_win", [P, 2, P])
        gst1 = [sb(f"gst1_{i}", [P, HT]) for i in range(2)]
        gains = sb("gains", [P, 2])
        rq_st = sb("rq_st", [P, 12])
        m_mx, nb_mx, sum_mx, ri_mx = (sb(n, [P, MXH]) for n in ("m_mx", "nb_mx", "sum_mx", "ri_mx"))
        m_sw, nb_sw, sum_sw, ri_sw, es_in, es = (sb(n, [P, SWH]) for n in ("m_sw", "nb_sw", "sum_sw", "ri_sw", "es_in", "es"))
        negrow = sb("negrow", [1, 2 * P])
        pos_i = pt_mx[:, :, :].rearrange("p a b -> p (a b)").bitcast(I32)
        m1.close()
        em_.close()

        m2, sb = era("right")
        y_a = sb("y_a", [P, 4, T])
        m2b, sb = era("right")
        ml_q = sb("ml_q", [P, 2, T])
        ml_k = sb("ml_k", [P, 2, T])
        ml_v = sb("ml_v", [P, 4, T])
        rows = sb("rows", [68, T])
        cwt = sb("cwt", [P, NT, 8])
        m2d, sb = era("right")
        cpad = [sb(f"cpad{i}", [P, 3 + T]) for i in range(2)]
        cacc = sb("cacc", [P, T])
        cw = sb("cw", [36, T])
        reset = sb("reset", [4, T])
        mst = sb("mst", [4, NT])
        m2d.close()
        m2e, sb = era("right")
        sel = sb("sel", [4, 6 * P])
        ks = sb("ks", [P, MLH, P])
        ktok = sb("ktok", [P, MLH, 64])
        vs = sb("vs", [P, 4, P])
        qd = sb("qd", [P, 2, P])
        rws = sb("rws", [4, 3, P])
        dec = sb("dec", [P, 2])
        cw_st = sb("cw_st", [P, 8])
        ml_e = sb("ml_e", [P, 4, P])
        em_sb = sb("em_sb", [P, 4 * P])
        t_sb = sb("t_sb", [P, 4 * P])
        wvx = sb("wvx", [P, 4, 2 * P])
        num_sb = sb("num_sb", [P, 4 * P])
        c_st = sb("c_st", [P, MLH, 2 * P])
        gst2 = [sb(f"gst2_{i}", [P, HT]) for i in range(2)]
        m2e.close()
        m2b.close()
        eh.close()

        ex, sb = era("left")
        x2 = sb("x2", [P, KD, T])
        eyh, sb = era("left")
        yh, yl = {}, {}
        for b in "cba":
            yh[b], yl[b] = (sb(f"y{x}_{b}", [P, 4, T], F32R) for x in "hl")
        m2.close()
        ey.close()
        eg, sb = era("right")
        gt = {g: sb(f"gt_{g}", [P, T]) for g in ("c0", "b0", "a0", "a1", "c1", "b1")}
        mg_hi = sb("mg_hi", [P, 2, T], F32R)
        mg_lo = sb("mg_lo", [P, 2, T], F32R)
        mg = sb("mg", [P, 2, T])
        mtmp = sb("mtmp", [P, HT])
        eg.close()
        eyh.close()
        e2, sb = era("left")
        h2_hi = sb("h2_hi", [P, KD, T], F32R)
        h2_lo = sb("h2_lo", [P, KD, T], F32R)
        f2 = ffn_buffers("2", sb)
        e2.close()
        ex.close()

        bank = [top.enter_context(nc.psum_tensor(f"bank{i}", [P, HT], F32)) for i in range(4)]
        wide = [top.enter_context(nc.psum_tensor(f"wide{i}", [P, 2 * HT], F32)) for i in range(2)]
        bank += [wide[i // 2][:, (i % 2) * HT:(i % 2 + 1) * HT] for i in range(4)]
        bank = [b if i >= 4 else b[:, :] for i, b in enumerate(bank)]

        raw_loaded = [sem(f"raw_loaded{i}") for i in range(2)]
        w_hi_ready = sem("w_hi_ready")
        split_ready = sem("split_ready")
        block_done = sem("block_done")
        const_in = sem("const_in")
        cols_in = sem("cols_in")
        mem_in = sem("mem_in")
        pos_in = sem("pos_in")
        sel_in = sem("sel_in")
        x_saved = sem("x_saved")
        x_back = sem("x_back")
        out_done = sem("out_done")
        x_in = [sem(f"x_in{i}") for i in range(KD // 2)]
        gate_stored = [sem(f"gate_stored{i}") for i in range(2)]
        gt_in = {g: sem(f"gt_in_{g}") for g in gt}
        mem_sq = sem("mem_sq")
        mem_acc = sem("mem_acc")
        mem_sum = sem("mem_sum")
        mem_rms = sem("mem_rms")
        mem_rstd = sem("mem_rstd")
        mem_h = sem("mem_h")
        mem_hi = sem("mem_hi")
        mem_ready = sem("mem_ready")
        sq_ready = sem("sq_ready")
        sq_used = sem("sq_used")
        sum_ready = sem("sum_ready")
        rms_ready = sem("rms_ready")
        rinv_ready = sem("rinv_ready")
        diag_ready = sem("diag_ready")
        rs_ready = sem("rs_ready")
        hf_ready = sem("hf_ready")
        h_hi_ready = sem("h_hi_ready")
        h_ready = sem("h_ready")
        h_ready_pool = sem("h_ready_pool")
        a_full = sem("a_full")
        a_free = sem("a_free")
        b_full = sem("b_full")
        b_free = sem("b_free")
        u_hi_ready = sem("u_hi_ready")
        u_ready = sem("u_ready")
        o_full = sem("o_full")
        x_added = sem("x_added")

        block = top.enter_context(nc.Block())

        def half(t):
            return slice(t * HT, (t + 1) * HT)

        PAIRS = {"ffn1": 0, "merge": NPAIR, "ffn2": NPAIR + 4}

        BY_FEATURE = [(k, t) for k in range(KD) for t in range(2)]
        BY_HALF = [(k, t) for t in range(2) for k in range(KD)]
        NORM_ORDER = [BY_FEATURE, BY_HALF, BY_HALF]
        norm_bank = [bank[3], bank[4]]

        def out_signal(order, n, pair, o):
            last0 = max(i for i, (k, _) in enumerate(order) if k < KD // 2)
            if o in (last0, 15):
                return block_done, n + (2 if o == 15 else 1)
            return o_full, pair * 14 + (o + 1 - (o > last0))

        def add_square(eng, i, o):
            k, t = NORM_ORDER[i][o]
            if k:
                m = square_slot(i, k, t)
                f = (f1, f1, f2)[i]
                eng.wait_ge(sq_ready, 16 * i + o + 1)
                if k > 1 or t:
                    eng.wait_ge(sq_used, m if i else max(m - 1, 1))
                acc = f["rs"][:, t, :]
                eng.tensor_tensor(acc, acc, f["sq"][:, m % 4, :], ALU.add).then_inc(sq_used, 1)

        def h_signal(i, t, k):
            if t and k % 2:
                return h_ready_pool, 4 * i + k // 2 + 1
            return h_ready, 12 * i + (8 + k // 2 if t else k) + 1

        def hf_slot(f, k):
            return f["uf"][:, 1, k // 2 % 2, :] if k % 2 else f["hf"][:, k // 2 % 2, :]

        def split_h(eng, i, t, k, hi, lo):
            eng.wait_ge(h_hi_ready, 16 * i + 8 * t + k + 1)
            eng.tensor_tensor(lo[:, k, half(t)], hf_slot((f1, f1, f2)[i], k), hi[:, k, half(t)], ALU.subtract
                              ).then_inc(h_signal(i, t, k)[0], 1)

        def square_slot(i, k, t):
            return 14 * i + [kt for kt in NORM_ORDER[i] if kt[0]].index((k, t))

        def done(j):
            return j + 2

        def prev(j):
            return j + 1

        p_full = sem("p_full")
        p_free = sem("p_free")
        psq_ready = sem("psq_ready")
        stats_done = sem("stats_done")
        rq_rms = sem("rq_rms")
        rq_ready = sem("rq_ready")
        consts_ready = sem("consts_ready")
        sin_arg = sem("sin_arg")
        rope_ready = sem("rope_ready")
        k_sum = sem("k_sum")
        k_rms = sem("k_rms")
        k_rstd = sem("k_rstd")
        k_norm = sem("k_norm")
        k_swap = sem("k_swap")
        k_ready = sem("k_ready")
        c_sum = sem("c_sum")
        c_rms = sem("c_rms")
        c_rstd = sem("c_rstd")
        ck_ready = sem("ck_ready")
        cv_turned = sem("cv_turned")
        cv_ready = sem("cv_ready")
        gate_full = sem("gate_full")
        gate_done = sem("gate_done")
        q_mx_ready = sem("q_mx_ready")
        q_sw_ready = sem("q_sw_ready")
        kv_ready = sem("kv_ready")
        rq_tile = sem("rq_tile")
        s1_done = sem("s1_done")
        mx_max = sem("mx_max")
        mx_bias = sem("mx_bias")
        rope_t = sem("rope_t")
        rope_x = sem("rope_x")
        q_rot_ready = sem("q_rot_ready")
        mx_exp = sem("mx_exp")
        mx_rinv = sem("mx_rinv")
        mx_p_ready = sem("mx_p_ready")
        s2_done = sem("s2_done")
        sw_max = sem("sw_max")
        sw_bias = sem("sw_bias")
        sw_exp = sem("sw_exp")
        sw_rinv = sem("sw_rinv")
        sw_p_ready = sem("sw_p_ready")
        sw_small = sem("sw_small")
        neg_done = sem("neg_done")
        v_win_ready = sem("v_win_ready")
        mx_turned = sem("mx_turned")
        mx_pt = sem("mx_pt")
        sw_turned = sem("sw_turned")
        sw_pt = sem("sw_pt")
        mx_out = sem("mx_out")
        y_c_done = sem("y_c_done")
        sw_out = sem("sw_out")
        y_b_done = sem("y_b_done")
        yh_ready = sem("yh_ready")
        y_split = sem("y_split")
        m_full = sem("m_full")
        m_prod = sem("m_prod")
        gated = sem("gated")
        waited = sem("waited")
        own = sem("own")

        def apart(eng):
            eng.sem_inc(waited, 1)

        STEP = 4

        def gate_at(block0, gate0, i, u, k):
            b, t = divmod(3 * u + k, 2)
            return i * 6 + (block0 + b), (block0 + b) % 2, i * 6 + (gate0 + b), t

        def gate_group(pe, feature_group, n, slot, g, t, before={}):
            if t == 0:
                pe.wait_ge(split_ready, n + 1)
            pe.wait_ge(gate_done, g * 2 + (t + 1))
            mm = feature_group(bank[t], slot, h_hi, h_lo, half(t), None, before)
            mm.then_inc(block_done if t else gate_full, 1)

        def gate_tanh(act, n, _, g, t, gst):
            if t == 0:
                act.wait_ge(gate_full, g + 1)
            else:
                act.wait_ge(block_done, n + 1)
            act.wait_ge(gate_stored[t], g * 16 + 16)
            apart(act)
            act.activation(gst[t][:, :], bank[t], ACT.Tanh, bias=cols[:, bass.ds(g + COLS["bgate"][0], 1)],
                           scale=0.5).then_inc(gate_done, 1)
            act.wait_ge(gate_done, g * 2 + (t + 3))
            act.dma_start(gate_scr[bass.ds(g, 1), :, half(t)].rearrange("a p n -> p (a n)"), gst[t][:, :]
                          ).then_inc(gate_stored[t], 16)

        sqs = [p_sw[:, :, :].rearrange("p a b -> p (a b)"), pt_sw[:, :, :].rearrange("p a b -> p (a b)")]
        p_mxf = p_mx[:, :, :].rearrange("p a b -> p (a b)")
        pt_mxf = pt_mx[:, :, :].rearrange("p a b -> p (a b)")
        ckf = ck[:, :, :].rearrange("p a b -> p (a b)")
        w0, w1 = wide[0][:, :], wide[1][:, :]
        k_raw = kv_all[:, 0, 64:64 + T]

        def tile_of(ap, j):
            return ap[:, :, bass.ds(j * P, P)]

        def mix1_bank(f, t):
            return 2 * f + t if f < 4 else f + 4 if f < 12 else 2 * f - 8 + t

        def mix1_full(f, t):
            if t == 0 and (f < 4 or f >= 12):
                return p_full, (f if f < 4 else f - 8) + 1
            return block_done, B_MIX1 + f + 1

        def mix1_pe(pe, feature_group, first_blocks):
            def stats(s):
                pe.wait_ge(psq_ready, s + 1)
                rhs, c, w = (ones[:, 0:1], s, 1) if s < 4 else (blk2, 4 + 2 * (s - 6), 2)
                for t in range(NT):
                    mm = pe.matmul(bank[4][:, 12 * t + c:12 * t + c + w], sqs[s % 2][:, t * P:(t + 1) * P], rhs,
                                   start=True, stop=True)
                mm.then_inc(stats_done, 1)

            def both_halves(stationary, src, done_sem):
                for t in range(2):
                    mm = pe.matmul(w1[:, half(t)], stationary, src[:, half(t)], start=True, stop=True)
                mm.then_inc(done_sem, 1)

            for f in range(N_MIX1):
                n = B_MIX1 + f
                if f == 0:
                    first_blocks(1, n, bank, (p_full, p_full), h_hi, h_lo)
                elif 4 <= f < 12:
                    pe.wait_ge(split_ready, n + 1)
                    pe.wait_ge(p_free, mix1_bank(f, 0) - 3)
                    if f == 4:
                        pe.wait_ge(mem_ready, 1)
                    mm = feature_group(bank[mix1_bank(f, 0) % 4][:, 0:NMEM], n % 2, mh_hi, mh_lo, slice(0, NMEM))
                    mm.then_inc(block_done, 1)
                elif f > 1:
                    pe.wait_ge(split_ready, n + 1)
                    for t in range(2):
                        if f == 17 and t == 1:
                            stats(9)
                        pe.wait_ge(p_free, max(mix1_bank(f, t) - 3, 1))
                        mm = feature_group(bank[mix1_bank(f, t) % 4], n % 2, h_hi, h_lo, half(t))
                        mm.then_inc(block_done if t else p_full, 1)
                if 1 <= f <= 4:
                    stats(f - 1)
                if f == 9:
                    pe.wait_ge(psq_ready, 5)
                    both_halves(ones, sqs[0], c_sum)
                if f == 12:
                    pe.wait_ge(p_free, 16)
                    pe.wait_ge(c_rms, 1)
                    for h in range(MXH):
                        for kk in range(2):
                            mm = pe.transpose(w1[:, kk * 4 * P + h * P:kk * 4 * P + (h + 1) * P], p_mx[:, h, kk * P:(kk + 1) * P], ident)
                    mm.then_inc(cv_turned, 1)
                if f == 13:
                    pe.wait_ge(psq_ready, 6)
                    pe.wait_ge(cv_ready, 1)
                    both_halves(blk64, sqs[1], k_sum)
                if 14 <= f <= 16:
                    stats(f - 8)
                if f == 15:
                    pe.wait_ge(k_norm, 1)
                    both_halves(perm, k_raw, k_swap)
            pe.wait_ge(p_free, 28)
            pe.wait_ge(rq_rms, 2)
            pe.wait_ge(ck_ready, 1)
            pe.wait_ge(cv_ready, 1)
            pe.wait_ge(k_ready, 1)

            for s in (s1_done, s2_done, mx_turned, sw_turned, mx_out, sw_out):
                pe.sem_inc(s, 1)
            with pe.Fori(0, NT // STEP) as i:
                for u in range(STEP):
                    j = i * STEP + u
                    pe.wait_ge(q_mx_ready, done(j))
                    pe.wait_ge(mx_pt, prev(j))
                    for h in range(MXH):
                        pe.matmul(w0[:, h * NMEM:(h + 1) * NMEM], q_mx[:, h, :], ck[:, h, :], start=True, stop=True)
                    pe.wait_ge(q_sw_ready, done(j))
                    pe.wait_ge(y_b_done, prev(j))
                    pe.matmul(bank[3], perm, q_sw[:, :, :].rearrange("p a b -> p (a b)"), start=True, stop=True)
                    pe.wait_ge(kv_ready, done(j))
                    pe.wait_ge(y_c_done, prev(j))
                    for w in range(2):
                        mm = pe.transpose(bank[2][:, w * P:(w + 1) * P], kv_st[:, 1, 64 * w:64 * w + P], ident)
                    mm.then_inc(s1_done, 1)
                    gate_group(pe, feature_group, *gate_at(B_GATE1, 0, i, u, 0))
                    pe.wait_ge(q_rot_ready, done(j))
                    pe.wait_ge(sw_pt, prev(j))
                    if u == 0:
                        pe.wait_ge(neg_done, i + 1)
                    else:
                        apart(pe)
                    for g in range(2):
                        if u == 0:
                            pe.matmul(w1[:, g * HT:(g + 1) * HT], negrow[0:1, 0:P],
                                      negrow[0:1, P:2 * P].unsqueeze(1).broadcast_to([1, 4, P]), start=True, stop=False,
                                      skip_group_check=True)
                        for c in range(4):
                            for w in range(2):
                                mm = pe.matmul(w1[64 * w:64 * w + 64, g * HT + c * P:g * HT + (c + 1) * P],
                                               q_rot[64 * g:64 * g + 64, c, 64 * w:64 * w + 64],
                                               kv_st[64 * g:64 * g + 64, 0, 64 * w:64 * w + P], start=u != 0, stop=u != 0 or (c == 3 and w == 1),
                                               skip_group_check=True)
                    mm.then_inc(s2_done, 1)
                    gate_group(pe, feature_group, *gate_at(B_GATE1, 0, i, u, 1))
                    pe.wait_ge(mx_p_ready, done(j))
                    for h in range(MXH):
                        for kk in range(2):
                            mm = pe.transpose(w0[:, (2 * h + kk) * P:(2 * h + kk + 1) * P], p_mx[:, h, kk * P:(kk + 1) * P], ident)
                    mm.then_inc(mx_turned, 1)
                    gate_group(pe, feature_group, *gate_at(B_GATE1, 0, i, u, 2))
                    pe.wait_ge(sw_p_ready, done(j))
                    for h in range(SWH):
                        mm = pe.transpose(w1[:, h * P:(h + 1) * P], p_sw[:, h, :], ident)
                    mm.then_inc(sw_turned, 1)
                    pe.wait_ge(mx_pt, done(j))
                    pe.wait_ge(v_win_ready, done(j))
                    for h in range(MXH):
                        for kk in range(2):
                            mm = pe.matmul(bank[2][:, h * P:(h + 1) * P], cv[:, kk, h * P:(h + 1) * P], pt_mx[:, 2 * h + kk, :],
                                           start=kk == 0, stop=kk == 1)
                    mm.then_inc(mx_out, 1)
                    pe.wait_ge(sw_pt, done(j))
                    b3 = bank[3].rearrange("p (i c) -> p i c", i=4)
                    for g in range(2):
                        for w in range(2):
                            mm = pe.matmul(b3[64 * g:64 * g + 64, :, 64 * w:64 * w + 64], v_win[:, w, 64 * g:64 * g + 64],
                                           pt_sw[:, 4 * g:4 * g + 4, 64 * w:64 * w + 64], start=True, stop=True)
                    mm.then_inc(sw_out, 1)

        def mix1_act(act):
            act.wait_ge(x_saved, 16)
            act.wait_ge(*h_signal(1, 1, KD - 2))
            act.wait_ge(*h_signal(1, 1, KD - 1))
            act.dma_start(pos_i, pos).then_inc(pos_in, 16)
            def square(s, src, copied, used):
                act.wait_ge(p_free, copied)
                if used:
                    act.wait_ge(*used)
                act.activation(sqs[s % 2], src, ACT.Square).then_inc(psq_ready, 1)

            for s in range(4):
                square(s, y_c[:, s, :], 2 * s + 2, (stats_done, s - 1) if s > 1 else None)
            for i, table in enumerate((rope_s, rope_c)):
                act.wait_ge(sin_arg, i + 1)
                act.activation(table[:, :], table[:, :], ACT.Sin).then_inc(rope_ready, 1)
            square(4, ckf, 12, (stats_done, 3))
            act.wait_ge(c_sum, 1)
            act.activation(pt_mxf, w1, ACT.Sqrt, bias=col("eps"), scale=1.0 / P).then_inc(c_rms, 1)
            square(5, k_raw, 18, (stats_done, 4))
            act.wait_ge(cv_turned, 1)
            act.activation(cv[:, :, :].rearrange("p a b -> p (a b)"), w1, ACT.Copy).then_inc(cv_ready, 1)
            act.wait_ge(k_sum, 1)
            act.wait_ge(ck_ready, 1)
            act.activation(pt_mxf, w1, ACT.Sqrt, bias=col("eps"), scale=1.0 / 64).then_inc(k_rms, 1)
            for s, used in ((6, (c_sum, 1)), (7, (k_sum, 1)), (8, (stats_done, 5)), (9, (stats_done, 6))):
                square(s, y_b[:, s - 6, :], 2 * (s - 6) + 20, used)
            act.wait_ge(stats_done, 8)
            st = bank[4][:, 0:12 * NT].rearrange("p (t c) -> p t c", c=12)
            act.activation(rq[:, :, 0:4], st[:, :, 0:4], ACT.Sqrt, bias=col("eps"), scale=1.0 / P).then_inc(rq_rms, 1)
            act.activation(rq[:, :, 4:12], st[:, :, 4:12], ACT.Sqrt, bias=col("eps"), scale=1.0 / 64).then_inc(rq_rms, 1)
            act.wait_ge(k_ready, 1)
            for s in (mx_exp, sw_exp, v_win_ready, mx_pt, sw_pt, y_c_done, y_b_done):
                act.sem_inc(s, 1)
            act.sem_inc(gate_done, 2)
            for t in range(2):
                act.sem_inc(gate_stored[t], 16)
            with act.Fori(0, NT // STEP) as i:
                for u in range(STEP):
                    j = i * STEP + u
                    act.wait_ge(mx_bias, done(j))
                    act.wait_ge(mx_turned, prev(j))
                    for h in range(MXH):
                        ins = act.activation(p_mx[:, h, :], w0[:, h * NMEM:(h + 1) * NMEM], ACT.Exp, bias=nb_mx[:, h:h + 1],
                                             scale=rq_st[:, h:h + 1], accum_out=sum_mx[:, h:h + 1])
                    ins.then_inc(mx_exp, 1)
                    act.wait_ge(sw_out, prev(j))
                    act.activation(v_win[:, :, :].rearrange("p a b -> p (a b)"), bank[2][:, 0:2 * P], ACT.Copy).then_inc(v_win_ready, 1)
                    gate_tanh(act, *gate_at(B_GATE1, 0, i, u, 0), gst1)
                    act.wait_ge(sw_bias, done(j))
                    act.wait_ge(sw_turned, prev(j))
                    act.activation(es[:, :], es_in[:, :], ACT.Exp)
                    for h in range(SWH):
                        c = 4 + 2 * (h % 4) + h // 4
                        ins = act.activation(p_sw[:, h, :], w1[:, h * P:(h + 1) * P], ACT.Exp, bias=nb_sw[:, h:h + 1],
                                             scale=rq_st[:, c:c + 1], accum_out=sum_sw[:, h:h + 1])
                    ins.then_inc(sw_exp, 1)
                    gate_tanh(act, *gate_at(B_GATE1, 0, i, u, 1), gst1)
                    act.wait_ge(mx_turned, done(j))
                    act.wait_ge(mx_out, prev(j))
                    act.activation(pt_mxf, w0, ACT.Copy).then_inc(mx_pt, 1)
                    gate_tanh(act, *gate_at(B_GATE1, 0, i, u, 2), gst1)
                    act.wait_ge(sw_turned, done(j))
                    act.wait_ge(sw_out, prev(j))
                    act.activation(sqs[1], w1, ACT.Copy).then_inc(sw_pt, 1)
                    act.wait_ge(mx_out, done(j))
                    apart(act)
                    act.activation(tile_of(y_c, j), bank[2].rearrange("p (a b) -> p a b", a=4), ACT.Copy).then_inc(y_c_done, 1)
                    act.wait_ge(sw_out, done(j))
                    apart(act)
                    act.activation(tile_of(y_b, j), bank[3].rearrange("p (a b) -> p a b", a=4), ACT.Copy).then_inc(y_b_done, 1)

        def mix1_dve(dve):
            step = [0]

            def chain(ins):
                ins.then_inc(own, 1)
                step[0] += 1
                dve.wait_ge(own, step[0])

            def evac(f):
                halves = range(1 if 4 <= f < 12 else 2)
                for t in halves:
                    dst = (y_c[:, f, half(t)] if f < 4 else ck[:, f - 4, :] if f < 8 else p_mx[:, f - 8, :] if f < 12
                           else y_b[:, f - 13, half(t)] if 13 <= f < 17
                           else kv_all[:, f // 17, 64 + t * HT:64 + (t + 1) * HT])
                    dve.wait_ge(*mix1_full(f, t))
                    src = bank[mix1_bank(f, t) % 4]
                    dve.tensor_copy(dst, src if len(halves) == 2 else src[:, 0:NMEM]).then_inc(p_free, 1)

            def angles(table, turn, count):
                chain(dve.tensor_scalar(pt_mxf, p_mxf, 1.0 / (2 * math.pi), turn, ALU.mult, ALU.add))
                chain(dve.tensor_scalar(pt_mxf, pt_mxf, ROUND, ROUND, ALU.add, ALU.subtract))
                src = p_mxf
                for part in (PI2_A, PI2_B, PI2_C):
                    chain(dve.scalar_tensor_tensor(table[:, :], pt_mxf, -part, src, ALU.mult, ALU.add))
                    src = table[:, :]
                chain(dve.tensor_scalar(table[:, :], table[:, :], 2 * math.pi * turn, PI_IN, ALU.add, ALU.min))
                dve.tensor_scalar(table[:, :], table[:, :], -PI_IN, None, ALU.max).then_inc(sin_arg, 1)
                dve.wait_ge(sin_arg, count)

            dve.wait_ge(x_saved, 16)
            dve.wait_ge(*h_signal(1, 1, KD - 1))
            chain(dve.memset(kv_all[:, :, 0:64], 0.0))
            chain(dve.memset(negrow[:, :], 0.0))
            chain(dve.memset(negrow[0:1, 0:64], 1.0))
            chain(dve.memset(negrow[0:1, P:P + 64], NEG))
            chain(dve.tensor_scalar(gains[:, 0:1], col("swq"), 64 ** -0.5, None, ALU.mult))
            chain(dve.scalar_tensor_tensor(gains[:, 1:2], col("mxq"), float(P) ** -0.5, col("mxk"), ALU.mult, ALU.mult))
            evac(0)
            evac(1)
            dve.wait_ge(pos_in, 16)
            chain(dve.tensor_copy(rope_c[:, :], pos_i))
            chain(dve.tensor_scalar(p_mxf, rope_c[:, :], col("inv"), None, ALU.mult))
            angles(rope_s, 0.0, 1)
            evac(2)
            angles(rope_c, 0.25, 2)
            for f in range(3, 12):
                evac(f)
            dve.wait_ge(c_rms, 1)
            dve.reciprocal(pt_mxf, pt_mxf).then_inc(c_rstd, 1)
            dve.wait_ge(c_rstd, 1)
            dve.scalar_tensor_tensor(ckf, ckf, gains[:, 1:2], pt_mxf, ALU.mult, ALU.mult).then_inc(ck_ready, 1)
            evac(12)
            evac(13)
            dve.wait_ge(k_rms, 1)
            dve.reciprocal(pt_mxf, pt_mxf).then_inc(k_rstd, 1)
            dve.wait_ge(k_rstd, 1)
            dve.scalar_tensor_tensor(k_raw, k_raw, col("swk"), pt_mxf, ALU.mult, ALU.mult).then_inc(k_norm, 1)
            evac(14)
            evac(15)
            dve.wait_ge(k_swap, 1)
            dve.wait_ge(rope_ready, 2)
            dve.wait_ge(k_norm, 1)
            chain(dve.tensor_tensor(pt_mxf, w1, rope_s[:, :], ALU.mult))
            chain(dve.tensor_tensor(k_raw, k_raw, rope_c[:, :], ALU.mult))
            dve.tensor_tensor(k_raw, k_raw, pt_mxf, ALU.add).then_inc(k_ready, 1)
            dve.wait_ge(k_ready, 1)
            evac(16)
            dve.wait_ge(rq_rms, 2)
            dve.reciprocal(rq[:, :, :], rq[:, :, :]).then_inc(rq_ready, 1)
            evac(17)
            dve.wait_ge(rq_ready, 1)

            for s in (q_mx_ready, q_sw_ready, kv_ready, rq_tile, mx_max, mx_bias, rope_t, rope_x, q_rot_ready, mx_rinv,
                      mx_p_ready, sw_max, sw_bias, sw_rinv, sw_p_ready, neg_done):
                dve.sem_inc(s, 1)
            rqt = rq_st[:, 4:12].rearrange("p (i g) -> p g i", g=2)
            with dve.Fori(0, NT // STEP) as i:
                for u in range(STEP):
                    j = i * STEP + u
                    dve.wait_ge(s1_done, prev(j))
                    dve.tensor_copy(q_mx[:, :, :], tile_of(y_c, j)).then_inc(q_mx_ready, 1)
                    dve.wait_ge(q_rot_ready, prev(j))
                    dve.tensor_scalar(q_sw[:, :, :], tile_of(y_b, j), gains[:, 0:1], None, ALU.mult).then_inc(q_sw_ready, 1)
                    dve.wait_ge(s2_done, prev(j))
                    dve.tensor_copy(kv_st[:, :, :], kv_all[:, :, bass.ds(j * P, WIN)]).then_inc(kv_ready, 1)
                    dve.wait_ge(sw_exp, prev(j))
                    dve.tensor_copy(rq_st[:, :], rq[:, bass.ds(j, 1), :].rearrange("p a b -> p (a b)")).then_inc(rq_tile, 1)
                    dve.wait_ge(s1_done, done(j))
                    dve.tensor_reduce(m_mx[:, :], w0.rearrange("p (h k) -> p h k", h=MXH), AX.X, ALU.max).then_inc(mx_max, 1)
                    dve.wait_ge(mx_max, done(j))
                    dve.wait_ge(rq_tile, done(j))
                    dve.scalar_tensor_tensor(nb_mx[:, :], m_mx[:, :], -1.0, rq_st[:, 0:4], ALU.mult, ALU.mult).then_inc(mx_bias, 1)
                    dve.tensor_tensor(q_tmp[:, :, :], bank[3].rearrange("p (a b) -> p a b", a=4),
                                      rope_s[:, bass.ds(j * P, P)].unsqueeze(1).broadcast_to([P, 4, P]), ALU.mult).then_inc(rope_t, 1)
                    dve.wait_ge(q_sw_ready, done(j))
                    dve.tensor_tensor(q_rot[:, :, :], q_sw[:, :, :],
                                      rope_c[:, bass.ds(j * P, P)].unsqueeze(1).broadcast_to([P, 4, P]), ALU.mult).then_inc(rope_x, 1)
                    dve.wait_ge(rope_t, done(j))
                    dve.wait_ge(rope_x, done(j))
                    dve.tensor_tensor(q_rot[:, :, :], q_rot[:, :, :], q_tmp[:, :, :], ALU.add).then_inc(q_rot_ready, 1)
                    dve.wait_ge(mx_exp, done(j))
                    dve.reciprocal(ri_mx[:, :], sum_mx[:, :]).then_inc(mx_rinv, 1)
                    dve.wait_ge(mx_rinv, done(j))
                    dve.tensor_tensor(p_mx[:, :, :], p_mx[:, :, :], ri_mx[:, :].unsqueeze(2).broadcast_to([P, MXH, NMEM]),
                                      ALU.mult).then_inc(mx_p_ready, 1)
                    dve.wait_ge(s2_done, done(j))
                    if u == 0:
                        dve.memset(negrow[0:1, P:P + 64], 0.0).then_inc(neg_done, 1)
                    dve.tensor_reduce(m_sw[:, :], w1.rearrange("p (h k) -> p h k", h=SWH), AX.X, ALU.max).then_inc(sw_max, 1)
                    dve.wait_ge(sw_max, done(j))
                    dve.tensor_tensor(m_sw[:, :].rearrange("p (g i) -> p g i", g=2), m_sw[:, :].rearrange("p (g i) -> p g i", g=2),
                                      rqt, ALU.mult).then_inc(sw_small, 1)
                    dve.wait_ge(sw_small, j * 4 + 1)
                    sink = cols[:, COLS["sink"][0]:COLS["sink"][0] + SWH]
                    dve.tensor_tensor(m_sw[:, :], m_sw[:, :], sink, ALU.max).then_inc(sw_small, 1)
                    dve.wait_ge(sw_small, j * 4 + 2)
                    dve.tensor_scalar(nb_sw[:, :], m_sw[:, :], -1.0, None, ALU.mult).then_inc(sw_small, 1)
                    dve.tensor_tensor(es_in[:, :], sink, m_sw[:, :], ALU.subtract).then_inc(sw_bias, 1)
                    dve.wait_ge(sw_exp, done(j))
                    dve.tensor_tensor(sum_sw[:, :], sum_sw[:, :], es[:, :], ALU.add).then_inc(sw_small, 1)
                    dve.wait_ge(sw_small, j * 4 + 4)
                    dve.reciprocal(ri_sw[:, :], sum_sw[:, :]).then_inc(sw_rinv, 1)
                    dve.wait_ge(sw_rinv, done(j))
                    dve.tensor_tensor(p_sw[:, :, :], p_sw[:, :, :], ri_sw[:, :].unsqueeze(2).broadcast_to([P, SWH, P]),
                                      ALU.mult).then_inc(sw_p_ready, 1)

        o_free = sem("o_free")
        conv_step = sem("conv_step")
        ml_silu = sem("ml_silu")
        q_scaled = sem("q_scaled")
        zi_ready = sem("zi_ready")
        zabs = sem("zabs")
        row_ln = sem("row_ln")
        row_step = sem("row_step")
        row_arg = sem("row_arg")
        row_exp = sem("row_exp")
        row_init = sem("row_init")
        cw_turned = sem("cw_turned")
        cwt_ready = sem("cwt_ready")
        y_a_gain = sem("y_a_gain")
        ml_small = sem("ml_small")
        ml_staged = sem("ml_staged")
        v_staged = sem("v_staged")
        b_rows = sem("b_rows")
        b_kqv = sem("b_kqv")
        qd_ready = sem("qd_ready")
        e_arg = sem("e_arg")
        e_exp = sem("e_exp")
        e_masked = sem("e_masked")
        sc_ready = sem("sc_ready")
        em_copied = sem("em_copied")
        kv_tok = sem("kv_tok")
        wv_done = sem("wv_done")
        numden = sem("numden")
        c_upd = sem("c_upd")
        num_copied = sem("num_copied")
        num_sq = sem("num_sq")
        den_abs = sem("den_abs")
        ms_done = sem("ms_done")
        c_new = sem("c_new")
        dn_ready = sem("dn_ready")
        d2_ready = sem("d2_ready")
        t_ready = sem("t_ready")
        t_ok = sem("t_ok")
        t_root = sem("t_root")
        t_inv = sem("t_inv")
        y_norm = sem("y_norm")
        y_a_done = sem("y_a_done")

        dabs = wvx[:, 0:2, :].rearrange("p a b -> p (a b)")
        sqn = wvx[:, 2:4, :].rearrange("p a b -> p (a b)")
        zrow, irow, lrow, mrow = cpad[0][0:4, 0:T], cpad[1][0:4, 0:T], cacc[0:4, :], reset[:, :]

        def by_chunk(ap):
            return ap.rearrange("p (c t) -> p c t", t=P)

        def mix2_pe(pe, feature_group):
            pe.wait_ge(gate_done, 2 + 2 * GATES1)
            pe.wait_ge(y_b_done, done(NT - 1))
            for f in range(N_MIX2):
                n = B_MIX2 + f
                pe.wait_ge(split_ready, n + 1)
                for t in range(2):
                    q = 2 * f + t
                    if f >= 11:
                        pe.wait_ge(o_free, 2 * (f - 11) + t + 1)
                    else:
                        pe.wait_ge(p_free, 28 + q - 3 if q >= 4 else 28)
                    mm = feature_group(bank[q % 4], n % 2, h_hi, h_lo, half(t))
                    mm.then_inc(block_done if t else p_full, 1)
                if f == 8:
                    pe.wait_ge(row_exp, 3)
                    for c in range(NT):
                        mm = pe.transpose(bank[4][:, 36 * c:36 * (c + 1)], cw[:, c * P:(c + 1) * P], ident[0:36, 0:36])
                    mm.then_inc(cw_turned, 1)
            pe.wait_ge(o_free, 8)
            pe.wait_ge(sel_in, 16)
            for s in (b_rows, b_kqv, numden, c_upd, ms_done):
                pe.sem_inc(s, 1)
            with pe.Fori(0, NT // STEP) as i:
                for u in range(STEP):
                    j = i * STEP + u
                    pe.wait_ge(ml_staged, done(j))
                    pe.wait_ge(num_copied, prev(j))
                    for h in range(MLH):
                        pe.matmul(bank[2][:, h * P:(h + 1) * P], sel[:, h * P:(h + 1) * P], rws[:, 0, :], start=True, stop=True)
                    pe.wait_ge(em_copied, prev(j))
                    for h in range(MLH):
                        pe.matmul(bank[3][:, h * P:(h + 1) * P], sel[:, h * P:(h + 1) * P], rws[:, 2, :], start=True, stop=True)
                    pe.wait_ge(qd_ready, prev(j))
                    for pr in range(2):
                        mm = pe.matmul(bank[4][:, pr * P:(pr + 1) * P], sel[:, (4 + pr) * P:(5 + pr) * P], rws[:, 1, :], start=True, stop=True)
                    mm.then_inc(b_rows, 1)
                    pe.wait_ge(c_new, prev(j))
                    for h in range(MLH):
                        pe.matmul(bank[5][:, h * P:(h + 1) * P], ks[:, h, :], ml_q[:, h // 2, bass.ds(j * P, P)], start=True, stop=True)
                    pe.wait_ge(t_ready, prev(j))
                    for h in range(MLH):
                        pe.transpose(bank[6][:, h * P:(h + 1) * P], ks[:, h, :], ident)
                    pe.wait_ge(v_staged, done(j))
                    pe.wait_ge(den_abs, prev(j))
                    for h in range(MLH):
                        mm = pe.transpose(bank[7][:, h * P:(h + 1) * P], vs[:, h, :], ident)
                    mm.then_inc(b_kqv, 1)
                    gate_group(pe, feature_group, *gate_at(B_GATE2, GATES1, i, u, 0))
                    pe.wait_ge(sc_ready, done(j))
                    pe.wait_ge(kv_tok, done(j))
                    pe.wait_ge(qd_ready, done(j))
                    pe.matmul(bank[7], ones, ml_e[:, :, :].rearrange("p a b -> p (a b)"), start=True, stop=False, skip_group_check=True)
                    for h in range(MLH):
                        pe.matmul(bank[7][:, h * P:(h + 1) * P], c_st[:, h, P:2 * P], qd[:, h // 2, :],
                                  start=False, stop=h == 3, skip_group_check=True)
                    for h in range(MLH):
                        pe.matmul(bank[2][:, h * P:(h + 1) * P], vs[:, h, :], ml_e[:, h, :], start=True, stop=False)
                        mm = pe.matmul(bank[2][:, h * P:(h + 1) * P], c_st[:, h, 0:P], qd[:, h // 2, :],
                                       start=False, stop=True)
                    mm.then_inc(numden, 1)
                    pe.wait_ge(wv_done, done(j))
                    for h in range(MLH):
                        r = 64 * (h % 2)
                        mm = pe.matmul(bank[5][r:r + 64, (h // 2) * 2 * P:(h // 2 + 1) * 2 * P], ktok[:, h, :],
                                       wvx[:, h, :], start=True, stop=True)
                    mm.then_inc(c_upd, 1)


                    def mean_square():
                        pe.wait_ge(num_sq, done(j))
                        pe.matmul(bank[6], ones, sqn, start=True, stop=True).then_inc(ms_done, 1)

                    gate_group(pe, feature_group, *gate_at(B_GATE2, GATES1, i, u, 1), {4: mean_square})
                    gate_group(pe, feature_group, *gate_at(B_GATE2, GATES1, i, u, 2))

        def mix2_act(act):
            for t in range(2):
                act.wait_ge(gate_stored[t], 16 * (GATES1 + 1))
            act.wait_ge(y_b_done, done(NT - 1))
            for f in range(4):
                act.wait_ge(conv_step, 4 * (f + 1))
                act.activation((ml_q if f < 2 else ml_k)[:, f % 2, :], cacc[:, :], ACT.Silu).then_inc(ml_silu, 1)
            act.wait_ge(zi_ready, 4)
            act.wait_ge(ml_silu, 4)
            act.activation(lrow, zrow, ACT.Abs).then_inc(zabs, 1)
            act.wait_ge(zabs, 1)
            act.activation(lrow, lrow, ACT.Exp, scale=-1.0).then_inc(zabs, 1)
            act.wait_ge(zabs, 2)
            act.activation(lrow, lrow, ACT.Ln, bias=ones[0:4, 0:1]).then_inc(row_ln, 1)
            act.wait_ge(row_step, 4)
            act.activation(rows[64:68, :], rows[64:68, :], ACT.Exp, scale=-1.0).then_inc(row_exp, 1)
            act.wait_ge(row_arg, 2)
            act.activation(rows[32:36, :], zrow, ACT.Exp).then_inc(row_exp, 1)
            act.activation(cw[32:36, :], irow, ACT.Exp).then_inc(row_exp, 1)
            act.wait_ge(cw_turned, 1)
            act.dma_start(sel[:, :], sel_d).then_inc(sel_in, 16)
            for f in range(9, 13):
                for t in range(2):
                    if t == 0:
                        act.wait_ge(p_full, 10 + f + 1)
                    else:
                        act.wait_ge(block_done, B_MIX2 + f + 1)
                    act.activation(y_a[:, f - 9, half(t)], bank[(2 * f + t) % 4], ACT.Sigmoid).then_inc(o_free, 1)
            for s in (v_staged, e_exp, em_copied, kv_tok, num_copied, den_abs, num_sq, d2_ready, t_root):
                act.sem_inc(s, 1)
            def root(j):
                act.wait_ge(t_ok, done(j))
                act.activation(t_sb[:, :], t_sb[:, :], ACT.Sqrt).then_inc(t_root, 1)

            with act.Fori(0, NT // STEP) as i:
                for u in range(STEP):
                    j = i * STEP + u
                    act.wait_ge(numden, prev(j))
                    act.wait_ge(wv_done, prev(j))
                    apart(act)
                    act.activation(vs[:, :, :], tile_of(ml_v, j), ACT.Copy).then_inc(v_staged, 1)
                    act.wait_ge(b_rows, done(j))
                    act.wait_ge(t_ready, prev(j))
                    act.activation(em_sb[:, :], bank[3], ACT.Copy).then_inc(em_copied, 1)
                    act.wait_ge(e_arg, done(j))
                    ef = ml_e[:, :, :].rearrange("p a b -> p (a b)")
                    act.activation(ef, ef, ACT.Exp).then_inc(e_exp, 1)
                    act.wait_ge(b_kqv, done(j))
                    for o in range(2):
                        act.activation(ktok[:, o:MLH:2, :], bank[6].rearrange("p (a b) -> p a b", a=4)[:, o:MLH:2, 64 * o:64 * o + 64],
                                       ACT.Copy)
                    act.activation(vs[:, :, :].rearrange("p a b -> p (a b)"), bank[7], ACT.Copy).then_inc(kv_tok, 1)
                    gate_tanh(act, *gate_at(B_GATE2, GATES1, i, u, 0), gst2)
                    act.wait_ge(y_a_done, prev(j))
                    act.wait_ge(numden, done(j))
                    act.activation(num_sb[:, :], bank[2], ACT.Copy).then_inc(num_copied, 1)
                    act.wait_ge(c_upd, done(j))
                    act.wait_ge(num_copied, done(j))
                    act.activation(sqn, num_sb[:, :], ACT.Square).then_inc(num_sq, 1)
                    act.activation(dabs, bank[7], ACT.Abs).then_inc(den_abs, 1)
                    act.wait_ge(dn_ready, done(j))
                    act.activation(em_sb[:, :], em_sb[:, :], ACT.Square, scale=EPS ** 0.5).then_inc(d2_ready, 1)
                    root(j)
                    gate_tanh(act, *gate_at(B_GATE2, GATES1, i, u, 1), gst2)
                    gate_tanh(act, *gate_at(B_GATE2, GATES1, i, u, 2), gst2)

        def mix2_dve(dve):
            for t in range(2):
                dve.wait_ge(gate_stored[t], 16 * (GATES1 + 1))
            dve.wait_ge(y_b_done, done(NT - 1))
            inits = [(cpad[0][:, 0:3], 0.0), (cpad[1][:, 0:3], 0.0), (rows[:, :], 0.0), (cw[:, :], 0.0),
                     (reset[:, :], 1.0), (mst[:, :], 0.0)]
            for k, (where, value) in enumerate(inits):
                dve.memset(where, value).then_inc(row_init, 1)
            dve.wait_ge(row_init, len(inits))
            dve.memset(by_chunk(reset[:, :])[:, :, 0:1], 0.0).then_inc(row_init, 1)

            def wait_full(f, t):
                if t == 0:
                    dve.wait_ge(p_full, 10 + f + 1)
                else:
                    dve.wait_ge(block_done, B_MIX2 + f + 1)

            for f in range(4):
                pad = cpad[f % 2]
                for t in range(2):
                    wait_full(f, t)
                    dve.tensor_copy(pad[:, 3 + t * HT:3 + (t + 1) * HT], bank[(2 * f + t) % 4]).then_inc(p_free, 1)
                dve.wait_ge(p_free, 28 + 2 * f + 2)
                if f:
                    dve.wait_ge(ml_silu, f)
                for s, tap in enumerate((3, 2, 1, 0)):
                    w = col("convq" if f < 2 else "convk", 4 * (f % 2) + tap)
                    if s == 0:
                        dve.tensor_scalar(cacc[:, :], pad[:, tap:tap + T], w, None, ALU.mult).then_inc(conv_step, 1)
                    else:
                        dve.wait_ge(conv_step, 4 * f + s)
                        dve.scalar_tensor_tensor(cacc[:, :], pad[:, tap:tap + T], w, cacc[:, :], ALU.mult, ALU.add
                                                 ).then_inc(conv_step, 1)
            dve.wait_ge(ml_silu, 2)
            dve.tensor_scalar(ml_q[:, :, :], ml_q[:, :, :], 64 ** -0.5, None, ALU.mult).then_inc(q_scaled, 1)
            for t in range(2):
                wait_full(4, t)
                b = bank[(8 + t) % 4]
                dve.wait_ge(conv_step, 16)
                dve.tensor_scalar(zrow[:, half(t)], b[32:36, :], col("bf", 0, 32, 36), None, ALU.add).then_inc(zi_ready, 1)
                dve.tensor_scalar(irow[:, half(t)], b[0:4, :], col("bi", 0, 0, 4), None, ALU.add).then_inc(zi_ready, 1)
                dve.wait_ge(zi_ready, 2 * t + 2)
                dve.sem_inc(p_free, 1)
            dve.wait_ge(row_ln, 1)
            dve.scalar_tensor_tensor(zrow, zrow, 0.0, lrow, ALU.min, ALU.subtract).then_inc(row_step, 1)
            dve.wait_ge(row_step, 1)
            dve.wait_ge(row_init, len(inits) + 1)
            dve.tensor_tensor_scan(lrow, reset[:, :], zrow, 0.0, ALU.mult, ALU.add).then_inc(row_step, 1)
            dve.wait_ge(row_step, 2)
            dve.tensor_tensor_scan(mrow, zrow, irow, 0.0, ALU.add, ALU.max).then_inc(row_step, 1)
            dve.wait_ge(row_step, 3)
            dve.tensor_scalar(rows[64:68, :], mrow, M_LEAST, None, ALU.max).then_inc(row_step, 1)
            dve.tensor_tensor(rows[0:4, :], lrow, mrow, ALU.subtract).then_inc(row_step, 1)
            dve.tensor_tensor(cw[0:4, :], irow, lrow, ALU.subtract).then_inc(row_step, 1)
            dve.tensor_copy(mst[:, 1:NT].unsqueeze(2), by_chunk(mrow)[:, 0:NT - 1, P - 1:P]).then_inc(row_step, 1)
            dve.wait_ge(row_step, 7)
            r_c, c_c = by_chunk(rows[0:4, :]), by_chunk(cw[0:4, :])
            dve.tensor_tensor(by_chunk(zrow), r_c, mst[:, :].unsqueeze(2).broadcast_to([4, NT, P]), ALU.add).then_inc(row_arg, 1)
            dve.tensor_tensor(by_chunk(irow), c_c, r_c[:, :, P - 1:P].broadcast_to([4, NT, P]), ALU.add).then_inc(row_arg, 1)
            for f in range(5, 9):
                for t in range(2):
                    wait_full(f, t)
                    dve.tensor_copy(ml_v[:, f - 5, half(t)], bank[(2 * f + t) % 4]).then_inc(p_free, 1)
            dve.wait_ge(row_exp, 3)
            dve.wait_ge(q_scaled, 1)
            dve.wait_ge(cw_turned, 1)
            turned = bank[4][:, 0:36 * NT].rearrange("p (c r) -> p c r", r=36)
            for k in range(2):
                dve.tensor_copy(cwt[:, :, 4 * k:4 * k + 4], turned[:, :, 32 * k:32 * k + 4]).then_inc(cwt_ready, 1)
            dve.wait_ge(cwt_ready, 2)
            dve.memset(c_st[:, :, :], 0.0).then_inc(row_init, 1)
            dve.memset(ks[:, :, :], 0.0).then_inc(row_init, 1)
            for i in range(4):
                dve.wait_ge(o_free, 2 * i + 2)
                dve.tensor_scalar(y_a[:, i, :], y_a[:, i, :], col("mlnorm", i), None, ALU.mult).then_inc(y_a_gain, 1)
            dve.wait_ge(y_a_gain, 4)
            dve.wait_ge(row_init, len(inits) + 3)
            for s in (ml_staged, qd_ready, e_arg, e_masked, sc_ready, wv_done, c_new, dn_ready, t_ready, t_ok, t_inv,
                      y_norm, y_a_done):
                dve.sem_inc(s, 1)
            def invert(j, part):
                dve.wait_ge(t_root, done(j))
                t = t_sb[:, 2 * P * part:2 * P * (part + 1)]
                dve.reciprocal(t, t).then_inc(t_inv, 1)

            def finish(j):
                dve.wait_ge(t_inv, j * 2 + 3)
                dve.tensor_tensor(num_sb[:, :], num_sb[:, :], t_sb[:, :], ALU.mult).then_inc(y_norm, 1)
                dve.wait_ge(y_norm, done(j))
                dve.tensor_tensor(tile_of(y_a, j), tile_of(y_a, j), by_chunk(num_sb[:, :]), ALU.mult).then_inc(y_a_done, 1)

            with dve.Fori(0, NT // STEP) as i:
                for u in range(STEP):
                    j = i * STEP + u
                    tok = bass.ds(j * P, P)
                    dve.wait_ge(c_upd, prev(j))
                    for k in range(3):
                        dve.tensor_copy(rws[:, k, :], rows[32 * k:32 * k + 4, tok])
                    for o in range(2):
                        r = 64 * o
                        ins = dve.tensor_copy(ks[r:r + 64, o:MLH:2, :], ml_k[r:r + 64, :, tok])
                    ins.then_inc(ml_staged, 1)
                    dve.tensor_copy(cw_st[:, :], cwt[:, bass.ds(j, 1), :].rearrange("p a b -> p (a b)")).then_inc(ml_small, 1)
                    if u:
                        invert(j - 1, 0)
                    dve.wait_ge(b_rows, done(j))
                    dve.tensor_copy(dec[:, :].unsqueeze(2), by_chunk(bank[4][:, 0:2 * P])[:, :, P - 1:P]).then_inc(ml_small, 1)
                    dve.tensor_tensor(qd[:, :, :], tile_of(ml_q, j), by_chunk(bank[4][:, 0:2 * P]), ALU.mult).then_inc(qd_ready, 1)
                    dve.wait_ge(ml_small, j * 2 + 2)
                    for h in range(MLH):
                        ins = dve.tensor_scalar(ml_e[:, h, :], bank[2][:, h * P:(h + 1) * P], cw_st[:, h:h + 1], 0.0, ALU.add, ALU.min)
                    ins.then_inc(e_arg, 1)
                    if u:
                        invert(j - 1, 1)
                    dve.wait_ge(e_exp, done(j))
                    dve.tensor_tensor(ml_e[:, :, :], ml_e[:, :, :], mask.unsqueeze(1).broadcast_to([P, MLH, P]), ALU.mult
                                      ).then_inc(e_masked, 1)
                    dve.wait_ge(e_masked, done(j))
                    dve.wait_ge(b_kqv, done(j))
                    dve.tensor_tensor(ml_e[:, :, :], ml_e[:, :, :], by_chunk(bank[5]), ALU.mult).then_inc(sc_ready, 1)
                    dve.wait_ge(kv_tok, done(j))
                    dve.tensor_tensor(wvx[:, :, 0:P], vs[:, :, :], cw_st[:, 4:8].unsqueeze(2).broadcast_to([P, MLH, P]), ALU.mult)
                    dve.tensor_copy(wvx[:, :, P:2 * P], cw_st[:, 4:8].unsqueeze(2).broadcast_to([P, MLH, P])).then_inc(wv_done, 1)
                    if u:
                        finish(j - 1)
                    dve.wait_ge(c_upd, done(j))
                    for h in range(MLH):
                        r, pr = 64 * (h % 2), h // 2
                        ins = dve.scalar_tensor_tensor(c_st[r:r + 64, h, :], c_st[r:r + 64, h, :], dec[r:r + 64, pr:pr + 1],
                                                       bank[5][r:r + 64, pr * 2 * P:(pr + 1) * 2 * P], ALU.mult, ALU.add)
                    ins.then_inc(c_new, 1)
                    dve.wait_ge(den_abs, done(j))
                    dve.tensor_tensor(em_sb[:, :], em_sb[:, :], dabs, ALU.max).then_inc(dn_ready, 1)
                    dve.wait_ge(ms_done, done(j))
                    dve.wait_ge(d2_ready, done(j))
                    dve.scalar_tensor_tensor(t_sb[:, :], bank[6], 1.0 / P, em_sb[:, :], ALU.mult, ALU.add).then_inc(t_ready, 1)
                    dve.wait_ge(t_ready, done(j))
                    dve.tensor_scalar(t_sb[:, :], t_sb[:, :], 2.0 ** -116, 2.0 ** 117, ALU.max, ALU.min).then_inc(t_ok, 1)
                    if u == STEP - 1:
                        for part in range(2):
                            invert(j, part)
                        finish(j)

        ys = {"c": y_c, "b": y_b, "a": y_a}
        MERGE = ((("c", 0), ("b", 0)), (("a", 0), ("a", 1)), (("c", 1), ("b", 1)))

        def merge_block(p, b):
            return B_MERGE + b if p == 0 else B_MERGE + 3 + 5 * (p - 1) + (b if b < 2 else 4)

        def merge_out(p):
            return B_MERGE + (5 * (p + 1) if p < 3 else 18)

        def merge_pe(pe, passes, project_out, project_last):
            def products(p, b):
                n = merge_block(p, b)
                pe.wait_ge(split_ready, n + 1)
                for i, (branch, _) in enumerate(MERGE[b]):
                    for t in range(2):
                        g = 2 * i + t
                        q = 3 * p + b
                        if q:
                            pe.wait_ge(gated, 4 * q + g - 3)
                        for k in range(4):
                            if p == 0 and t == 0:
                                pe.wait_ge(y_split, 4 * "cba".index(branch) + k + 1)
                            mm = passes(bank[g], n % 2, (4 * i + k) * P, yh[branch][:, k, half(t)], yl[branch][:, k, half(t)],
                                        k == 0, k == 3)
                        mm.then_inc(block_done if g == 3 else m_full, 1)

            pe.wait_ge(gate_done, 2 * NG + 2)
            pe.wait_ge(t_ready, done(NT - 1))
            for p in range(4):
                products(p, 0)
                products(p, 1)
                if p:
                    project_out(PAIRS["merge"] + p - 1, merge_out(p - 1), merge_out(p - 1) % 2, mg_hi, mg_lo)
                products(p, 2)
            project_last(PAIRS["merge"] + 3, merge_out(3), merge_out(3) % 2, mg_hi, mg_lo, 2)

        def merge_act(act):
            act.wait_ge(block_done, B_MERGE)
            for b in "cba":
                if b == "b":
                    for t in range(2):
                        act.wait_ge(gate_stored[t], 16 * (NG + 1))
                    act.wait_ge(y_a_done, done(NT - 1))
                for k in range(4):
                    act.activation(yh[b][:, k, :], ys[b][:, k, :], ACT.Copy).then_inc(yh_ready, 1)
            act.wait_ge(y_split, 12)
            for p in range(4):
                for m in range(2):
                    for t in range(2):
                        act.wait_ge(gated, 12 * p + (5 + t if m == 0 else 11 + t))
                        if p and m == 0 and t == 0:
                            act.wait_ge(block_done, merge_out(p - 1) + 2)
                        act.activation(mg_hi[:, m, half(t)], mg[:, m, half(t)], ACT.Copy).then_inc(u_hi_ready, 1)

        def merge_dve(dve, add_out, split_u):
            dve.wait_ge(block_done, B_MERGE)
            dve.wait_ge(y_a_done, done(NT - 1))
            for b in "cba":
                if b == "b":
                    for t in range(2):
                        dve.wait_ge(gate_stored[t], 16 * (NG + 1))
                for k in range(4):
                    dve.wait_ge(yh_ready, 4 * "cba".index(b) + k + 1)
                    dve.tensor_tensor(yl[b][:, k, :], ys[b][:, k, :], yh[b][:, k, :], ALU.subtract).then_inc(y_split, 1)
            dve.wait_ge(y_split, 12)

            def gate(p, b, split=False):
                n = merge_block(p, b)
                for i, (branch, m) in enumerate(MERGE[b]):
                    g = gt[branch + str(m)]
                    for t in range(2):
                        if 2 * i + t == 3:
                            dve.wait_ge(block_done, n + 1)
                        else:
                            dve.wait_ge(m_full, 9 * p + 3 * b + 2 * i + t + 1)
                        if t == 0:
                            dve.wait_ge(gt_in[branch + str(m)], 16 * (p + 1))
                        first = (branch, m) in (("c", 0), ("a", 1))
                        dst = mg[:, m, half(t)] if first else mtmp[:, :]
                        count = 12 * p + 4 * b + 2 * i + t + 1
                        if count > 1:
                            dve.wait_ge(gated, count - 1)
                        ins = dve.scalar_tensor_tensor(dst, g[:, half(t)], 1.0, bank[2 * i + t], ALU.add, ALU.mult)
                        if first:
                            ins.then_inc(gated, 1)
                        else:
                            ins.then_inc(m_prod, 1)
                            m_count[0] += 1
                            dve.wait_ge(m_prod, m_count[0])
                            dve.tensor_tensor(mg[:, m, half(t)], mg[:, m, half(t)], mtmp[:, :], ALU.add).then_inc(gated, 1)
                            if split and i == 1:
                                split_u(PAIRS["merge"] + p, 1, mg, mg_hi, mg_lo, (t,))

            m_count = [0]
            for p in range(4):
                gate(p, 0)
                gate(p, 1)
                if p:
                    add_out(PAIRS["merge"] + p - 1, merge_out(p - 1), x2)
                else:
                    dve.wait_ge(x_back, 16 * 4)
                split_u(PAIRS["merge"] + p, 0, mg, mg_hi, mg_lo)
                gate(p, 2, split=True)

        @block.sync
        def _(sp):
            def load(n, slot):
                sp.wait_ge(split_ready, n - 1)
                sp.dma_start(raw[slot][:, :], wts[bass.ds(n, 1)].rearrange("a p n -> p (a n)")
                             ).then_inc(raw_loaded[slot], 16)

            def load_gate(g, m, uses):
                if uses:
                    sp.wait_ge(gated, uses)
                elif g in ("c0", "c1"):
                    sp.wait_ge(y_split, 4 if g == "c0" else 8)
                sp.dma_start(gt[g][:, :], gate_scr[{"a": 0, "b": 8, "c": 16}[g[0]] + m]).then_inc(gt_in[g], 16)

            for i, part in enumerate(x_in):
                sp.dma_start(x1[:, 2 * i:2 * i + 2, :], xT[:, 2 * i:2 * i + 2, :]).then_inc(part, 16)
            sp.dma_start(cst[:, :], const_d).then_inc(const_in, 16)
            for i in range(2):
                sp.dma_start(raw[i][:, :], wts[i]).then_inc(raw_loaded[i], 16)
            sp.dma_start(memx[:, :, :], memT).then_inc(mem_in, 16)
            with sp.Fori(1, B_MIX1 // 2 + 1) as i:
                load(i * 2, 0)
                load(i * 2 + 1, 1)
            sp.wait_ge(x_added, 16 * (NPAIR + 1))
            sp.dma_start(x_scr, x1[:, :, :]).then_inc(x_saved, 16)
            with sp.Fori(B_MIX1 // 2 + 1, B_MERGE // 2) as i:
                load(i * 2, 0)
                load(i * 2 + 1, 1)
            for n in range(2 * (B_MERGE // 2), B_MERGE):
                load(n, n % 2)
            for k in range(20):
                for p in range(1, 4):
                    if k == 5 * p - 2:
                        load_gate("c0", 2 * p, 12 * (p - 1) + 2)
                        load_gate("b0", 2 * p, 12 * (p - 1) + 4)
                    if k == 5 * p - 1:
                        load_gate("a0", 2 * p, 12 * (p - 1) + 6)
                        load_gate("a1", 2 * p + 1, 12 * (p - 1) + 8)
                    if k == 5 * p + 1:
                        load_gate("c1", 2 * p + 1, 12 * (p - 1) + 10)
                        load_gate("b1", 2 * p + 1, 12 * (p - 1) + 12)
                load(B_MERGE + k, (B_MERGE + k) % 2)
                if k == 1:
                    sp.wait_ge(block_done, B_MERGE)
                    sp.wait_ge(x_saved, 16)
                    for i in range(2):
                        sp.wait_ge(gate_stored[i], 16 * (NG + 1))
                    for g in ("c0", "b0", "a0", "a1"):
                        load_gate(g, int(g[1]), 0)
                if k == 2:
                    for g in ("c1", "b1"):
                        load_gate(g, int(g[1]), 0)
                    for i in range(4):
                        sp.dma_start(x2[:, 2 * i:2 * i + 2, :], x_scr[:, 2 * i:2 * i + 2, :]).then_inc(x_back, 16)
            for n in range(B_FFN2, B_FFN2 + B_FFN2 % 2):
                load(n, n % 2)
            with sp.Fori((B_FFN2 + 1) // 2, NB // 2) as i:
                load(i * 2, 0)
                load(i * 2 + 1, 1)
            for n in range(NB - NB % 2, NB):
                load(n, n % 2)
            for k in range(KD):
                sp.wait_ge(x_added, 16 * (PAIRS["ffn2"] + NPAIR) + 2 * k + 2)
                sp.dma_start(out[k], x2[:, k, :]).then_inc(out_done, 16)
            sp.wait_ge(out_done, 16 * KD)

        @block.gpsimd
        def _(pool):
            def split(n, turn, slot):
                if not (isinstance(n, int) and n < 2):
                    pool.wait_ge(block_done, n - 1)
                pool.wait_ge(raw_loaded[slot], turn * 16 + 16)
                apart(pool)
                pool.tensor_scalar(whi[slot][:, :], raw[slot][:, :], 1.0, 0.0, ALU.mult, ALU.add).then_inc(w_hi_ready, 1)
                pool.wait_ge(w_hi_ready, n + 1)
                pool.tensor_tensor(wlo[slot][:, :], raw[slot][:, :], whi[slot][:, :],
                                   ALU.subtract).then_inc(split_ready, 1)

            pool.dma_start(cols[:, :], cols_d).then_inc(cols_in, 16)
            pool.wait_ge(cols_in, 16)
            split(0, 0, 0)
            split(1, 0, 1)

            def splits(first, end):
                if first % 2:
                    split(first, first // 2, 1)
                with pool.Fori((first + 1) // 2, end // 2) as i:
                    split(i * 2, i, 0)
                    split(i * 2 + 1, i, 1)
                if end % 2:
                    split(end - 1, end // 2, 0)

            def split_odd(i):
                hi, lo = (h_hi, h_lo) if i < 2 else (h2_hi, h2_lo)
                for k in range(1, KD, 2):
                    split_h(pool, i, 1, k, hi, lo)

            def norm_splits(i, n):
                split(n, n // 2, n % 2)
                for o in range(9, 14):
                    add_square(pool, i, o)
                split(n + 1, (n + 1) // 2, (n + 1) % 2)
                for o in range(14, 16):
                    add_square(pool, i, o)
                split_odd(i)

            split_odd(0)
            splits(2, B_MIX1)
            norm_splits(1, B_MIX1)
            splits(B_MIX1 + 2, B_FFN2)
            norm_splits(2, B_FFN2)
            splits(B_FFN2 + 2, NB)

        @block.tensor
        def _(pe):
            def passes(dst, slot, wcol, r_hi, r_lo, first, last):
                w_h, w_l = whi[slot][:, wcol:wcol + P], wlo[slot][:, wcol:wcol + P]
                pe.matmul(dst, w_h, r_hi, start=first, stop=False)
                pe.matmul(dst, w_h, r_lo, start=False, stop=False)
                return pe.matmul(dst, w_l, r_hi, start=False, stop=last)

            def feature_group(dst, slot, hi, lo, cols_of, norm_half=None, before={}):
                for k in range(KD):
                    if k in before:
                        before[k]()
                    if norm_half:
                        pe.wait_ge(*h_signal(*norm_half, k))
                    mm = passes(dst, slot, k * P, hi[:, k, cols_of], lo[:, k, cols_of], k == 0, k == KD - 1)
                return mm

            def norm_sum(i, t):
                f = (f1, f1, f2)[i]
                pe.wait_ge(sq_used, square_slot(i, KD - 1, t) + 1)
                for c in range(4):
                    mm = pe.matmul(norm_bank[t][:, c:c + 1], f["rs"][:, t, c * P:(c + 1) * P], ones[:, 0:1], start=True, stop=True)
                mm.then_inc(sum_ready, 1)

            def norm_spread(i, t):
                f = (f1, f1, f2)[i]
                pe.wait_ge(diag_ready, 2 * i + t + 1)
                pe.matmul(norm_bank[t], ones, f["uf"][:, 0, t, :], start=True, stop=True).then_inc(rs_ready, 1)

            def ffn_tile(r, tile, n, slot_a, hi, lo):
                for which, full, free in ((0, a_full, a_free), (1, b_full, b_free)):
                    slot = (slot_a + which) % 2
                    pe.wait_ge(split_ready, n + which + 1)
                    for t in range(2):
                        pe.wait_ge(free, 44 * r + tile * 2 + t - 1)
                        mm = feature_group(bank[2 * which + t], slot, hi, lo, half(t))
                        mm.then_inc(block_done if t else full, 1)

            def first_blocks(i, n, banks, full, hi, lo):
                for t in range(2):
                    for w in range(2):
                        before = {}
                        if t == 0:
                            pe.wait_ge(split_ready, n + w + 1)
                            if w:
                                before = {4: lambda: norm_spread(i, 1)}
                            elif i:
                                before = {7: lambda: norm_sum(i, 1)}
                        mm = feature_group(banks[2 * w + t], (n + w) % 2, hi, lo, half(t), (i, t) if w == 0 else None, before)
                        mm.then_inc(block_done if t else full[w], 1)

            def project_out(pair, n, slot0, hi, lo, order=BY_FEATURE, between={}):
                pe.wait_ge(u_ready, pair * 4 + 3)
                seen = -1
                for o, (k, t) in enumerate(order):
                    if t and not order[o - 1][1] and k == 0:
                        pe.wait_ge(u_ready, pair * 4 + 4)
                    b, m = divmod(k, 4)
                    slot = (slot0 + b) % 2
                    if b > seen:
                        pe.wait_ge(split_ready, n + b + 1)
                        seen = b
                    pe.wait_ge(x_added, pair * 16 + (o + 13))
                    for c in range(2):
                        mm = passes(bank[4 + o % 4], slot, (2 * m + c) * P, hi[:, c, half(t)], lo[:, c, half(t)], c == 0, c == 1)
                    mm.then_inc(out_signal(order, n, pair, o)[0], 1)
                    if o in between:
                        between[o]()

            def project_last(pair, n, slot0, hi, lo, i):
                project_out(pair, n, slot0, hi, lo, BY_HALF, {9: lambda: norm_sum(i, 0), 11: lambda: norm_spread(i, 0)})

            def ffn(r, f, hi, lo, b0, pairs, i):
                s0 = b0 % 2
                if r:
                    pe.wait_ge(b_free, 44)
                first_blocks(i, b0, bank, (a_full, b_full), hi, lo)
                if r == 0:
                    pe.wait_ge(mem_acc, 1)
                    pe.matmul(bank[4][:, 0:NMEM], ones, f["rs"][:, 0, 0:NMEM], start=True, stop=True).then_inc(mem_sum, 1)
                ffn_tile(r, 1, b0 + 2, s0, hi, lo)
                with pe.Fori(1, NPAIR) as c:
                    n = c * 6 + (b0 - 2)
                    ffn_tile(r, c * 2, n, s0, hi, lo)
                    project_out(c + (pairs - 1), n + 2, s0, f["u_hi"], f["u_lo"])
                    ffn_tile(r, c * 2 + 1, n + 4, s0, hi, lo)
                if r == 0:
                    project_last(pairs + NPAIR - 1, b0 + 6 * NPAIR - 2, s0, f["u_hi"], f["u_lo"], 1)
                else:
                    project_out(pairs + NPAIR - 1, b0 + 6 * NPAIR - 2, s0, f["u_hi"], f["u_lo"])

            pe.wait_ge(const_in, 16)
            for t in range(2):
                norm_sum(0, t)
            norm_spread(0, 0)
            ffn(0, f1, h_hi, h_lo, B_FFN1, PAIRS["ffn1"], 0)
            mix1_pe(pe, feature_group, first_blocks)
            mix2_pe(pe, feature_group)
            merge_pe(pe, passes, project_out, project_last)
            ffn(1, f2, h2_hi, h2_lo, B_FFN2, PAIRS["ffn2"], 2)

        @block.scalar
        def _(act):
            def norm(i, x, f, hi):
                order = NORM_ORDER[i]

                def squares(first, end):
                    for o in range(first, end):
                        k, t = order[o]
                        if i == 0 and t == 0:
                            act.wait_ge(x_in[k // 2], 16)
                        if i:
                            act.wait_ge(x_added, 16 * (PAIRS["ffn1"] + NPAIR if i == 1 else PAIRS["ffn2"]) + 1 + o)
                        if k == 0:
                            dst = f["rs"][:, t, :]
                        else:
                            m = square_slot(i, k, t)
                            dst = f["sq"][:, m % 4, :]
                            if m >= 4:
                                act.wait_ge(sq_used, m - 3)
                        act.activation(dst, x[:, k, half(t)], ACT.Square).then_inc(sq_ready, 1)

                def root(t):
                    act.wait_ge(sum_ready, 2 * i + t + 1)
                    act.activation(norm_s[:, t, :], norm_bank[t][:, 0:4], ACT.Sqrt, bias=col("eps"), scale=1.0 / D).then_inc(rms_ready, 1)

                def round_h(t, first=0, end=KD):
                    for k in range(first, end):
                        act.wait_ge(hf_ready, 16 * i + 8 * t + k + 1)
                        act.activation(hi[:, k, half(t)], hf_slot(f, k), ACT.Copy).then_inc(h_hi_ready, 1)

                act.activation(warm[:, i:i + 1], cols[0:1, COLS["eps"][0]:COLS["eps"][0] + 1], ACT.Sqrt)
                if i == 0:
                    squares(0, 16)
                    root(0)
                    root(1)
                    round_h(0)
                else:
                    squares(0, 10)
                    root(0)
                    squares(10, 12)
                    for k in range(4):
                        round_h(0, k, k + 1)
                        squares(12 + k, 13 + k)
                    round_h(0, 4)
                    root(1)
                round_h(1)

            def ffn(r, f, b0, pairs):
                def silu(tile, n, t):
                    if t == 0:
                        act.wait_ge(a_full, tile + (22 * r + 1))
                    else:
                        act.wait_ge(block_done, n + 1)
                    if not (isinstance(tile, int) and tile == 0):
                        act.wait_ge(b_free, tile * 2 + (44 * r + t - 1))
                    act.activation(f["sa"][:, t, :], bank[t], ACT.Silu).then_inc(a_free, 1)

                def round_u(tile, which, t):
                    act.wait_ge(b_free, tile * 2 + (44 * r + t + 1))
                    act.activation(f["u_hi"][:, which, half(t)], f["uf"][:, which, t, :], ACT.Copy).then_inc(u_hi_ready, 1)

                for tile in range(2):
                    for t in range(2):
                        silu(tile, b0 + 2 * tile, t)
                    if r == 0 and tile == 0:
                        act.wait_ge(mem_sum, 1)
                        act.activation(f["rs"][:, 1, 0:NMEM], bank[4][:, 0:NMEM], ACT.Sqrt, bias=col("eps"), scale=1.0 / D
                                       ).then_inc(mem_rms, 1)
                    for t in range(2):
                        round_u(tile, tile, t)
                if r == 0:
                    act.wait_ge(mem_h, KD)
                    act.activation(mh_hi[:, :, :].rearrange("p a b -> p (a b)"), mxv, ACT.Copy).then_inc(mem_hi, 1)
                with act.Fori(1, NPAIR) as c:
                    n = c * 6 + (b0 - 2)
                    for t in range(2):
                        silu(c * 2, n, t)
                    act.wait_ge(block_done, n + 4)
                    for t in range(2):
                        round_u(c * 2, 0, t)
                    for t in range(2):
                        silu(c * 2 + 1, n + 4, t)
                    for t in range(2):
                        round_u(c * 2 + 1, 1, t)

            act.wait_ge(cols_in, 16)
            norm(0, x1, f1, h_hi)
            mxv = memx[:, :, :].rearrange("p a b -> p (a b)")
            act.wait_ge(mem_in, 16)
            act.activation(f1["sq"][:, :, :].rearrange("p a b -> p (a b)"), mxv, ACT.Square).then_inc(mem_sq, 1)
            ffn(0, f1, B_FFN1, PAIRS["ffn1"])
            norm(1, x1, f1, h_hi)
            mix1_act(act)
            mix2_act(act)
            merge_act(act)
            norm(2, x2, f2, h2_hi)
            ffn(1, f2, B_FFN2, PAIRS["ffn2"])

        @block.vector
        def _(dve):
            def norm(i, x, f, hi, lo, gain, outs=None):
                order = NORM_ORDER[i]

                def diagonal(t):
                    dve.wait_ge(rms_ready, 2 * i + t + 1)
                    dve.reciprocal(norm_s[:, t, :], norm_s[:, t, :]).then_inc(rinv_ready, 1)
                    dve.wait_ge(rinv_ready, 2 * i + t + 1)
                    dve.tensor_tensor(f["uf"][:, 0, t, :].rearrange("p (c n) -> p c n", c=4), ident.unsqueeze(1).broadcast_to([P, 4, P]),
                                      norm_s[:, t, :].unsqueeze(2).broadcast_to([P, 4, P]), ALU.mult).then_inc(diag_ready, 1)

                def scale(t, k):
                    if k == 0:
                        dve.wait_ge(rs_ready, 2 * i + t + 1)
                    if t or k >= 4:
                        dve.wait_ge(*(h_signal(i, t, k - 4) if k >= 4 else h_signal(i, 0, k + 4)))
                    dve.scalar_tensor_tensor(hf_slot(f, k), x[:, k, half(t)], col(gain, k), norm_bank[t],
                                             ALU.mult, ALU.mult).then_inc(hf_ready, 1)

                if i == 0:
                    for o in range(16):
                        add_square(dve, 0, o)
                    for t in range(2):
                        diagonal(t)
                    for part in x_in:
                        dve.wait_ge(part, 16)
                    dve.sem_inc(x_added, 16)
                else:
                    for o in range(8):
                        outs(o, o + 1)
                        if o:
                            add_square(dve, i, o - 1)
                    add_square(dve, i, 7)
                    outs(8, 10)
                    diagonal(0)
                    outs(10, 12)
                for k in range(KD + 1):
                    if k < KD:
                        scale(0, k)
                    if k:
                        split_h(dve, i, 0, k - 1, hi, lo)
                    if i and k < 4:
                        outs(12 + k, 13 + k)
                if i:
                    diagonal(1)
                for k in range(0, KD, 2):
                    scale(1, k)
                    scale(1, k + 1)
                    split_h(dve, i, 1, k, hi, lo)

            def add_out(pair, n, x, first=0, end=16, order=BY_FEATURE):
                for o in range(first, end):
                    k, t = order[o]
                    dve.wait_ge(*out_signal(order, n, pair, o))
                    dve.wait_ge(x_added, pair * 16 + (o + 1))
                    xs = x[:, k, half(t)]
                    dve.scalar_tensor_tensor(xs, bank[4 + o % 4], 0.5, xs, ALU.mult, ALU.add).then_inc(x_added, 1)

            def split_u(pair, which, src, f_hi, f_lo, halves=range(2)):
                for t in halves:
                    dve.wait_ge(u_hi_ready, pair * 4 + (2 * which + t + 1))
                    dve.tensor_tensor(f_lo[:, which, half(t)], src[:, which, t, :] if len(src.shape) == 4 else src[:, which, half(t)],
                                      f_hi[:, which, half(t)], ALU.subtract).then_inc(u_ready, 1)

            def ffn(r, x, f, b0, pairs):
                def product(tile, which, n, halves=range(2)):
                    for t in halves:
                        if t == 0:
                            dve.wait_ge(b_full, tile + (22 * r + 1))
                        else:
                            dve.wait_ge(block_done, n + 2)
                        dve.wait_ge(a_free, tile * 2 + (44 * r + t + 1))
                        dve.tensor_tensor(f["uf"][:, which, t, :], f["sa"][:, t, :], bank[2 + t], ALU.mult).then_inc(b_free, 1)

                rstd = f["rs"][:, 1, 0:NMEM]
                if r == 0:
                    dve.wait_ge(mem_sq, 1)
                    dve.tensor_reduce(f["rs"][:, 0, 0:NMEM], f["sq"][:, :, :].rearrange("p a b -> p (a b)").rearrange("p (k n) -> p n k", k=KD),
                                      AX.X, ALU.add).then_inc(mem_acc, 1)
                for tile in range(2):
                    product(tile, tile, b0 + 2 * tile)
                    if r == 0 and tile == 0:
                        dve.wait_ge(mem_rms, 1)
                        dve.reciprocal(rstd, rstd).then_inc(mem_rstd, 1)
                        dve.wait_ge(mem_rstd, 1)
                        for k in range(KD):
                            dve.scalar_tensor_tensor(memx[:, k, :], memx[:, k, :], col("mem", k), rstd, ALU.mult, ALU.mult
                                                     ).then_inc(mem_h, 1)
                    split_u(pairs, tile, f["uf"], f["u_hi"], f["u_lo"])
                if r == 0:
                    dve.wait_ge(mem_hi, 1)
                    dve.tensor_tensor(mh_lo[:, :, :], memx[:, :, :], mh_hi[:, :, :], ALU.subtract).then_inc(mem_ready, 1)
                with dve.Fori(1, NPAIR) as c:
                    n = c * 6 + (b0 - 2)
                    product(c * 2, 0, n)
                    add_out(c + (pairs - 1), n + 2, x)
                    split_u(c + pairs, 0, f["uf"], f["u_hi"], f["u_lo"])
                    for t in range(2):
                        product(c * 2 + 1, 1, n + 4, (t,))
                        split_u(c + pairs, 1, f["uf"], f["u_hi"], f["u_lo"], (t,))

            dve.wait_ge(cols_in, 16)
            bgate = cols[:, COLS["bgate"][0]:COLS["bgate"][0] + NG]
            dve.tensor_scalar(bgate, bgate, 0.5, None, ALU.mult).then_inc(consts_ready, 1)
            norm(0, x1, f1, h_hi, h_lo, "ffn1")
            ffn(0, x1, f1, B_FFN1, PAIRS["ffn1"])

            def last_outs(pair, n, x):
                return lambda first, end: add_out(pair, n, x, first, end, BY_HALF)

            norm(1, x1, f1, h_hi, h_lo, "mix", last_outs(PAIRS["ffn1"] + NPAIR - 1, B_MIX1 - 2, x1))
            mix1_dve(dve)
            mix2_dve(dve)
            merge_dve(dve, add_out, split_u)
            norm(2, x2, f2, h2_hi, h2_lo, "ffn2", last_outs(PAIRS["merge"] + 3, merge_out(3), x2))
            ffn(1, x2, f2, B_FFN2, PAIRS["ffn2"])
            add_out(PAIRS["ffn2"] + NPAIR - 1, NB - 2, x2)


def constants():
    c = np.zeros((P, NCONST), np.float32)
    i = np.arange(P)
    c[:, C_ID:C_ID + P] = np.eye(P)
    c[:, C_ONE:C_ONE + P] = 1.0
    c[:, C_BLK:C_BLK + P] = (i[:, None] // 64 == i[None, :] // 64)
    for o in (0, 64):
        for d in range(8):
            c[o + d + 8, C_PERM + o + d] = -1.0
            c[o + d, C_PERM + o + d + 8] = 1.0
    c[:, C_MASK:C_MASK + P] = (i[:, None] <= i[None, :])
    c[:, C_BLK2:C_BLK2 + 2] = (i[:, None] // 64 == np.arange(2)[None, :])
    s = np.zeros((MLH, 6 * P), np.float32)
    for h in range(MLH):
        s[h, h * P:(h + 1) * P] = 1.0
        s[h, (8 + h) * 64:(9 + h) * 64] = 1.0
    return c, s


def weight_stream(w):
    def feature(m, j=None):
        m = m if j is None else m[:, j * P:(j + 1) * P]
        return m.reshape(KD, P, P).transpose(1, 0, 2).reshape(P, 1024)

    def outs(m, pair):
        v = m[2 * pair * P:(2 * pair + 2) * P].reshape(2, P, 2, 4, P)
        return [v[:, :, b].transpose(1, 2, 0, 3).reshape(P, 1024) for b in range(2)]

    def ffn(w_in, w_out):
        blocks = []
        for c in range(NPAIR):
            ab = [feature(w_in, o + 2 * c + i) for i in range(2) for o in (0, NF)]
            blocks += ab[:2] + (outs(w_out, c - 1) if c else []) + ab[2:]
        return blocks + outs(w_out, NPAIR - 1)

    at = np.cumsum((0, 256, 256, 512, 4, 4, 512, 512, 128, 128, 512, 3072))
    mq, mk, mv, mi, mf, mo, sq, sk, sv, cq, gates = (w["w_in"][:, a:b] for a, b in zip(at[:-1], at[1:]))
    order = [h for i in range(4) for h in (i, i + 4)]
    sq = sq.reshape(D, SWH, 64)[:, order].reshape(D, 512)
    br_sw = w["w_br_sw"].reshape(SWH, 64, D)[order].reshape(512, D)
    pre = np.zeros((D, P), np.float32)
    pre[:, 0:4], pre[:, 32:36] = mi, mf
    gate = [feature(gates, g) for g in range(NG)]
    blocks = ffn(w["ffn1_w_in"], w["ffn1_w_out"])
    blocks += [feature(cq, i) for i in range(4)] + [feature(w["mx_w_kv"], i) for i in range(8)]
    blocks += [feature(sk)] + [feature(sq, i) for i in range(4)] + [feature(sv)]
    blocks += gate[:GATES1]
    blocks += [feature(mq, i) for i in range(2)] + [feature(mk, i) for i in range(2)] + [feature(pre)]
    blocks += [feature(mv, i) for i in range(4)] + [feature(mo, i) for i in range(4)]
    blocks += gate[GATES1:]
    branch = {"a": w["w_br_ml"], "b": br_sw, "c": w["w_br_mx"]}

    def half_block(b, m):
        return branch[b][:, m * P:(m + 1) * P].reshape(4, P, P).transpose(1, 0, 2).reshape(P, 512)

    for p in range(4):
        m0, m1 = 2 * p, 2 * p + 1
        b = [np.concatenate([half_block(*x), half_block(*y)], axis=1) for x, y in (
            (("c", m0), ("b", m0)), (("a", m0), ("a", m1)), (("c", m1), ("b", m1)))]
        blocks += b[:2] + (outs(w["w_out"], p - 1) if p else []) + b[2:]
    blocks += outs(w["w_out"], 3)
    blocks += ffn(w["ffn2_w_in"], w["ffn2_w_out"])
    assert len(blocks) == NB
    return np.stack(blocks)


def columns(v):
    c = np.zeros((P, NCOL), np.float32)

    def put(name, x):
        c[:, COLS[name][0]:COLS[name][0] + COLS[name][1]] = x

    for name, key in (("ffn1", "ffn1_norm"), ("mix", "mix_norm"), ("ffn2", "ffn2_norm"), ("mem", "mem_norm"),
                      ("bgate", "b_gate"), ("mlnorm", "ml_out_norm"), ("mxq", "mx_q_norm"), ("mxk", "mx_k_norm")):
        put(name, v[key].reshape(-1, P).T)
    for name, key in (("convq", "ml_conv_q"), ("convk", "ml_conv_k")):
        put(name, v[key].reshape(4, 2, P).transpose(2, 1, 0).reshape(P, 8))
    for name, key in (("swq", "sw_q_norm"), ("swk", "sw_k_norm")):
        put(name, np.concatenate([v[key], v[key]])[:, None])
    put("sink", np.broadcast_to(v["sw_sinks"][None, :], (P, SWH)))
    c[0:4, COLS["bi"][0]] = v["ml_b_i"]
    c[32:36, COLS["bf"][0]] = v["ml_b_f"]
    half = 8
    inv = np.float32(500000.0) ** (-np.arange(half, dtype=np.float32) * np.float32(2.0 / 16))
    for o in (0, 8, 64, 72):
        c[o:o + 8, COLS["inv"][0]] = inv
    c[:, COLS["eps"][0]] = EPS
    return c


def kernel(**inputs):
    import concourse.bacc as bacc
    from concourse.bass_utils import run_bass_kernel_spmd

    v = {k: np.asarray(a) for k, a in inputs.items()}
    one = {k: a[0] for k, a in v.items()}
    cst, sel = constants()
    arrays = {
        "xT": np.ascontiguousarray(one["x"].T.reshape(KD, P, T).transpose(1, 0, 2)),
        "memT": np.ascontiguousarray(one["mem"].T.reshape(KD, P, NMEM).transpose(1, 0, 2)),
        "pos": np.ascontiguousarray(np.broadcast_to(one["positions"][None, :], (P, T))),
        "weights": weight_stream(one),
        "columns": columns(one),
        "constants": cst,
        "selectors": sel,
    }
    nc = bacc.Bacc("TRN2", target_bir_lowering=False, num_devices=1)
    args = [nc.dram_tensor("in_" + k, a.shape, mybir.dt.from_np(a.dtype), kind="ExternalInput").ap()
            for k, a in arrays.items()]
    out = nc.dram_tensor("out_x", (KD, P, T), F32, kind="ExternalOutput").ap()
    build(nc, *args, out)
    r = run_bass_kernel_spmd(nc, [{"in_" + k: a for k, a in arrays.items()}], core_ids=[0])
    y = r.results[0]["out_x"]
    return np.ascontiguousarray(y.reshape(D, T).T)[None]
```
